# Optimizing a Trainium2 kernel written in Bass

```python
import math
import jax, jax.numpy as jnp
from jax import lax
import numpy as np

D_MODEL = 1024
BATCH = 1
SEQ = 256
DEPTH = 1

HEAD_DIM = 64
SWA_Q_HEADS = 8
SWA_KV_HEADS = 2
SWA_GROUP = SWA_Q_HEADS // SWA_KV_HEADS
WINDOW = 128
DIFF_HEADS = 4
DIFF_V_DIM = 2 * HEAD_DIM
SWA_WIDTH = SWA_Q_HEADS * HEAD_DIM
DIFF_WIDTH = DIFF_HEADS * DIFF_V_DIM
MIX_WIDTH = SWA_WIDTH + DIFF_WIDTH
QA_COLS = SWA_Q_HEADS * HEAD_DIM
KA_COLS = SWA_KV_HEADS * HEAD_DIM
VA_COLS = SWA_KV_HEADS * HEAD_DIM
QB_COLS = DIFF_HEADS * 2 * HEAD_DIM
KB_COLS = DIFF_HEADS * 2 * HEAD_DIM
VB_COLS = DIFF_HEADS * DIFF_V_DIM
IN_COLS = QA_COLS + KA_COLS + VA_COLS + QB_COLS + KB_COLS + VB_COLS
IN_SPLITS = (QA_COLS, QA_COLS + KA_COLS, QA_COLS + KA_COLS + VA_COLS,
             QA_COLS + KA_COLS + VA_COLS + QB_COLS,
             QA_COLS + KA_COLS + VA_COLS + QB_COLS + KB_COLS)
Q_BLOCK = 128
D_FF = 4 * D_MODEL
CONV_WIDTH = 3
EPS = 1e-6


def rms_norm(x, g):
    xf = x.astype(jnp.float32)
    xf = xf * lax.rsqrt(jnp.mean(xf * xf, axis=-1, keepdims=True) + EPS)
    return (xf * g.astype(jnp.float32)).astype(x.dtype)

def alibi_slopes(n):
    def pow2(m):
        start = 2.0 ** (-8.0 / m)
        return [start ** (i + 1) for i in range(m)]
    if math.log2(n).is_integer():
        s = pow2(n)
    else:
        c = 2 ** int(math.floor(math.log2(n)))
        s = pow2(c) + pow2(2 * c)[0::2][: n - c]
    return np.array(sorted(s, reverse=True), dtype=np.float32)

def swa_sink_attention(q, k, v, sinks, slopes):
    B, S = q.shape[0], q.shape[1]
    nb = S // WINDOW
    qb = q.reshape(B, nb, WINDOW, SWA_KV_HEADS, SWA_GROUP, HEAD_DIM)
    kb = k.reshape(B, nb, WINDOW, SWA_KV_HEADS, HEAD_DIM)
    vb = v.reshape(B, nb, WINDOW, SWA_KV_HEADS, HEAD_DIM)
    pad = ((0, 0), (1, 0), (0, 0), (0, 0), (0, 0))
    kk = jnp.concatenate([jnp.pad(kb, pad)[:, :-1], kb], axis=2)
    vv = jnp.concatenate([jnp.pad(vb, pad)[:, :-1], vb], axis=2)
    scores = jnp.einsum("bnqhgd,bnkhd->bnhgqk", qb, kk).astype(jnp.float32)
    scores = scores * (HEAD_DIM ** -0.5)
    qpos = jnp.arange(WINDOW)[:, None] + WINDOW
    kpos = jnp.arange(2 * WINDOW)[None, :]
    dist = qpos - kpos
    valid = (dist >= 0) & (dist < WINDOW)
    abs_k = jnp.arange(nb)[:, None, None] * WINDOW + kpos[None] - WINDOW
    valid = valid[None] & (abs_k >= 0)
    sl = slopes.reshape(SWA_KV_HEADS, SWA_GROUP)[:, :, None, None]
    scores = scores - sl * dist.astype(jnp.float32)[None, None]
    scores = jnp.where(valid[None, :, None, None], scores, -jnp.inf)
    sink = jnp.broadcast_to(
        sinks.astype(jnp.float32).reshape(1, 1, SWA_KV_HEADS, SWA_GROUP, 1, 1),
        scores.shape[:-1] + (1,))
    p = jax.nn.softmax(jnp.concatenate([scores, sink], axis=-1), axis=-1)[..., :-1]
    out = jnp.einsum("bnhgqk,bnkhd->bnqhgd", p.astype(v.dtype), vv)
    return out.reshape(B, S, SWA_Q_HEADS * HEAD_DIM)

def diff_attention(q, k, v, lam, slopes, subln_g, lambda_init):
    B, S = q.shape[0], q.shape[1]
    nb = S // Q_BLOCK
    qb = q.reshape(B, nb, Q_BLOCK, DIFF_HEADS, 2, HEAD_DIM).transpose(1, 0, 2, 3, 4, 5)
    kpos = jnp.arange(S)

    def block(args):
        q_blk, i = args
        s = jnp.einsum("bqhmd,bkhmd->bhmqk", q_blk, k).astype(jnp.float32)
        s = s * (HEAD_DIM ** -0.5)
        dist = (i * Q_BLOCK + jnp.arange(Q_BLOCK))[:, None] - kpos[None, :]
        s = s - slopes[None, :, None, None, None] * dist.astype(jnp.float32)
        s = jnp.where(dist >= 0, s, -jnp.inf)
        p = jax.nn.softmax(s, axis=-1)
        p_diff = p[:, :, 0] - lam * p[:, :, 1]
        return jnp.einsum("bhqk,bkhe->bqhe", p_diff.astype(v.dtype), v)

    out = lax.map(block, (qb, jnp.arange(nb)))
    out = out.transpose(1, 0, 2, 3, 4).reshape(B, S, DIFF_HEADS, DIFF_V_DIM)
    out = rms_norm(out, subln_g) * (1.0 - lambda_init)
    return out.reshape(B, S, DIFF_HEADS * DIFF_V_DIM)

def conv_ffn(h, w_up, conv_w, conv_b, w_down):
    u = jnp.einsum("bsd,df->bsf", h, w_up)
    up = jnp.pad(u, ((0, 0), (CONV_WIDTH - 1, 0), (0, 0)))
    S = u.shape[1]
    c = (conv_w[0] * up[:, 0:S] + conv_w[1] * up[:, 1:S + 1]
         + conv_w[2] * up[:, 2:S + 2] + conv_b)
    g, val = jnp.split(c, 2, axis=-1)
    return jnp.einsum("bsf,fd->bsd", jax.nn.gelu(g, approximate=True) * val, w_down)

def first_inputs(seed: int = 0) -> dict:
    key = jax.random.key(seed)
    ks = jax.random.split(key, 18)
    f32 = jnp.float32

    def nrm(k, shape, scale):
        return jax.random.normal(k, shape, f32) * scale

    def gain(k, shape):
        return 1.0 + 0.05 * jax.random.normal(k, shape, f32)

    return {
        "x": nrm(ks[0], (BATCH, SEQ, D_MODEL), 1.0),
        "attn_pre_g": gain(ks[1], (DEPTH, D_MODEL)),
        "w_in": nrm(ks[2], (DEPTH, D_MODEL, IN_COLS), D_MODEL ** -0.5),
        "swa_sinks": nrm(ks[3], (DEPTH, SWA_Q_HEADS), 0.5),
        "swa_out_g": gain(ks[4], (DEPTH, SWA_WIDTH)),
        "diff_lq1": nrm(ks[5], (DEPTH, HEAD_DIM), 0.1),
        "diff_lk1": nrm(ks[6], (DEPTH, HEAD_DIM), 0.1),
        "diff_lq2": nrm(ks[7], (DEPTH, HEAD_DIM), 0.1),
        "diff_lk2": nrm(ks[8], (DEPTH, HEAD_DIM), 0.1),
        "diff_subln_g": gain(ks[9], (DEPTH, DIFF_V_DIM)),
        "w_out": nrm(ks[10], (DEPTH, MIX_WIDTH, D_MODEL), MIX_WIDTH ** -0.5),
        "attn_post_g": gain(ks[11], (DEPTH, D_MODEL)),
        "ffn_pre_g": gain(ks[12], (DEPTH, D_MODEL)),
        "w_up": nrm(ks[13], (DEPTH, D_MODEL, 2 * D_FF), D_MODEL ** -0.5),
        "conv_w": nrm(ks[14], (DEPTH, CONV_WIDTH, 2 * D_FF), CONV_WIDTH ** -0.5),
        "conv_b": nrm(ks[15], (DEPTH, 2 * D_FF), 0.02),
        "w_down": nrm(ks[16], (DEPTH, D_FF, D_MODEL), D_FF ** -0.5),
        "ffn_post_g": gain(ks[17], (DEPTH, D_MODEL)),
    }

def first_block(x, attn_pre_g, w_in, swa_sinks, swa_out_g, diff_lq1, diff_lk1, diff_lq2,
              diff_lk2, diff_subln_g, w_out, attn_post_g, ffn_pre_g, w_up, conv_w, conv_b,
              w_down, ffn_post_g):
    B, S = x.shape[0], x.shape[1]
    slopes = jnp.asarray(alibi_slopes(SWA_Q_HEADS + DIFF_HEADS))
    swa_slopes = slopes[:SWA_Q_HEADS]
    diff_slopes = slopes[SWA_Q_HEADS:]
    for layer in range(DEPTH):
        lambda_init = 0.8 - 0.6 * math.exp(-0.3 * layer)
        h = rms_norm(x, attn_pre_g[layer])
        proj = jnp.einsum("bsd,de->bse", h, w_in[layer])
        q_a, k_a, v_a, q_b, k_b, v_b = jnp.split(proj, IN_SPLITS, axis=-1)
        y_a = swa_sink_attention(
            q_a.reshape(B, S, SWA_Q_HEADS, HEAD_DIM),
            k_a.reshape(B, S, SWA_KV_HEADS, HEAD_DIM),
            v_a.reshape(B, S, SWA_KV_HEADS, HEAD_DIM),
            swa_sinks[layer], swa_slopes)
        y_a = rms_norm(y_a, swa_out_g[layer])
        lam = (jnp.exp(jnp.sum(diff_lq1[layer].astype(jnp.float32) * diff_lk1[layer].astype(jnp.float32)))
               - jnp.exp(jnp.sum(diff_lq2[layer].astype(jnp.float32) * diff_lk2[layer].astype(jnp.float32)))
               + lambda_init)
        y_b = diff_attention(
            q_b.reshape(B, S, DIFF_HEADS, 2, HEAD_DIM),
            k_b.reshape(B, S, DIFF_HEADS, 2, HEAD_DIM),
            v_b.reshape(B, S, DIFF_HEADS, DIFF_V_DIM),
            lam, diff_slopes, diff_subln_g[layer], lambda_init)
        mix = jnp.concatenate([y_a, y_b], axis=-1)
        x = x + rms_norm(jnp.einsum("bse,ed->bsd", mix, w_out[layer]), attn_post_g[layer])
        h2 = rms_norm(x, ffn_pre_g[layer])
        f = conv_ffn(h2, w_up[layer], conv_w[layer], conv_b[layer], w_down[layer])
        x = x + rms_norm(f, ffn_post_g[layer])
    return x


N_HEADS_DIL = 8
N_HEADS_SB = 8
D_DIL = N_HEADS_DIL * HEAD_DIM
D_SB = N_HEADS_SB * HEAD_DIM
D_MIX = D_DIL + D_SB
DILATION_PATTERNS = ((128, 1), (512, 4), (2048, 16))
SB_BLOCK = 128
N_GROUPS = 4
EXPERTS_PER_GROUP = 8
N_EXPERTS = N_GROUPS * EXPERTS_PER_GROUP
TOP_K = 2
D_FF_EXPERT = D_MODEL // 2
MOE_BLOCK = 128
NORM_EPS = 1e-6


def _rmsnorm(x, g):
    xf = x.astype(jnp.float32)
    y = xf * lax.rsqrt(jnp.mean(xf * xf, axis=-1, keepdims=True) + NORM_EPS)
    return (y * g.astype(jnp.float32)).astype(x.dtype)

def _modulate(h, shift, scale):
    return h * (1 + scale[:, None, :]) + shift[:, None, :]

def _alibi_slopes(n_heads):
    return np.array([2.0 ** (-8.0 * (i + 1) / n_heads) for i in range(n_heads)], dtype=np.float32)

def _dilated_window_attention(q, k, v, window, dilation, slopes):
    b, s, h, e = q.shape
    n = window // dilation
    unit = n * dilation
    s_pad = -(-s // unit) * unit
    nb = s_pad // unit
    pad = ((0, 0), (0, s_pad - s), (0, 0), (0, 0))

    def split(t):
        return jnp.pad(t, pad).reshape(b, nb, n, dilation, h, e)

    def with_prev(t):
        prev = jnp.pad(t[:, :-1], ((0, 0), (1, 0), (0, 0), (0, 0), (0, 0), (0, 0)))
        return jnp.concatenate([prev, t], axis=2)

    qb = split(q)
    kc = with_prev(split(k))
    vc = with_prev(split(v)).astype(jnp.float32)
    scores = jnp.einsum('bgidhe,bgjdhe->bgdhij', qb, kc,
                        preferred_element_type=jnp.float32) * (e ** -0.5)
    i_idx = np.arange(n)[:, None]
    j_idx = np.arange(2 * n)[None, :]
    steps = i_idx + n - j_idx
    blk = np.arange(nb)[:, None, None]
    valid = (steps >= 0) & (steps <= n) & (blk * n + j_idx - n >= 0)
    bias = -slopes[:, None, None] * (steps * dilation).astype(np.float32)[None]
    logits = jnp.where(valid[None, :, None, None], scores + jnp.asarray(bias)[None, None, None], -jnp.inf)
    m = jnp.max(logits, axis=-1)
    p = jnp.exp(logits - m[..., None])
    den = jnp.sum(p, axis=-1)
    den_t = den.transpose(0, 1, 4, 2, 3)
    o = jnp.einsum('bgdhij,bgjdhe->bgidhe', p, vc) / den_t[..., None]
    o = o.reshape(b, s_pad, h, e)[:, :s]
    m = m.transpose(0, 1, 4, 2, 3).reshape(b, s_pad, h)[:, :s]
    den = den_t.reshape(b, s_pad, h)[:, :s]
    return o, m, den

def _dilated_mixture(q, k, v):
    slopes = _alibi_slopes(q.shape[2])
    outs, maxes, dens = [], [], []
    for window, dilation in DILATION_PATTERNS:
        o, m, den = _dilated_window_attention(q, k, v, window, dilation, slopes)
        outs.append(o)
        maxes.append(m)
        dens.append(den)
    outs = jnp.stack(outs)
    maxes = jnp.stack(maxes)
    dens = jnp.stack(dens)
    w = dens * jnp.exp(maxes - jnp.max(maxes, axis=0, keepdims=True))
    w = w / jnp.sum(w, axis=0, keepdims=True)
    return jnp.sum(w[..., None] * outs, axis=0).astype(q.dtype)

def _stick_breaking_attention(q, k, v):
    b, s, h, e = q.shape
    nb = s // SB_BLOCK
    qblocks = q.reshape(b, nb, SB_BLOCK, h, e).transpose(1, 0, 2, 3, 4)
    key_pos = jnp.arange(s)
    vf = v.astype(jnp.float32)

    def block(args):
        qb, idx = args
        z = jnp.einsum('bqhe,bshe->bhqs', qb, k, preferred_element_type=jnp.float32) * (e ** -0.5)
        q_pos = idx * SB_BLOCK + jnp.arange(SB_BLOCK)
        causal = key_pos[None, :] < q_pos[:, None]
        log_beta = jax.nn.log_sigmoid(z)
        log_keep = jnp.where(causal, jax.nn.log_sigmoid(-z), 0.0)
        between = lax.cumsum(log_keep, axis=3, reverse=True) - log_keep
        weights = jnp.where(causal, jnp.exp(log_beta + between), 0.0)
        return jnp.einsum('bhqs,bshe->bqhe', weights, vf)

    out = lax.map(block, (qblocks, jnp.arange(nb)))
    return out.transpose(1, 0, 2, 3, 4).reshape(b, s, h, e).astype(q.dtype)

def _hierarchical_moe(h, w_group, w_expert, w_gate, w_up, w_down):
    n, d = h.shape
    group_prob = jax.nn.softmax((h @ w_group).astype(jnp.float32), axis=-1)
    group = jnp.argmax(group_prob, axis=-1)
    group_gate = jnp.take_along_axis(group_prob, group[:, None], axis=1)
    exp_logits = (h @ w_expert).astype(jnp.float32).reshape(n, N_GROUPS, EXPERTS_PER_GROUP)
    exp_logits = jnp.take_along_axis(exp_logits, group[:, None, None], axis=1)[:, 0]
    top_p, top_local = lax.top_k(jax.nn.softmax(exp_logits, axis=-1), TOP_K)
    top_p = top_p / jnp.sum(top_p, axis=-1, keepdims=True)
    weight = (group_gate * top_p).reshape(-1)
    expert = (group[:, None] * EXPERTS_PER_GROUP + top_local).reshape(-1)
    token = jnp.repeat(jnp.arange(n), TOP_K)

    order = jnp.argsort(expert)
    e_sorted = expert[order]
    tok_sorted = token[order]
    w_sorted = weight[order]
    counts = jnp.zeros((N_EXPERTS,), jnp.int32).at[expert].add(1)
    padded = (counts + MOE_BLOCK - 1) // MOE_BLOCK * MOE_BLOCK
    start = jnp.cumsum(counts) - counts
    pad_end = jnp.cumsum(padded)
    pad_start = pad_end - padded
    nk = n * TOP_K
    dest = pad_start[e_sorted] + jnp.arange(nk) - start[e_sorted]
    cap = -(-nk // MOE_BLOCK) * MOE_BLOCK + N_EXPERTS * MOE_BLOCK
    n_blocks = cap // MOE_BLOCK
    buf = jnp.zeros((cap, d), h.dtype).at[dest].set(h[tok_sorted])
    block_expert = jnp.minimum(
        jnp.searchsorted(pad_end, jnp.arange(n_blocks) * MOE_BLOCK, side='right'), N_EXPERTS - 1)

    def expert_block(args):
        xb, e = args
        return (jax.nn.silu(xb @ w_gate[e]) * (xb @ w_up[e])) @ w_down[e]

    y = lax.map(expert_block, (buf.reshape(n_blocks, MOE_BLOCK, d), block_expert)).reshape(cap, d)
    contrib = y[dest] * w_sorted[:, None].astype(y.dtype)
    return jnp.zeros((n, d), y.dtype).at[tok_sorted].add(contrib)

def second_inputs(seed: int = 0) -> dict:
    key = jax.random.key(seed)
    ks = jax.random.split(key, 16)
    d = D_MODEL

    def nrm(k, shape, std):
        return jax.random.normal(k, shape, jnp.float32) * std

    return {
        "x": nrm(ks[0], (BATCH, SEQ, d), 1.0),
        "c": nrm(ks[1], (BATCH, d), 1.0),
        "w_ada": nrm(ks[2], (DEPTH, d, 6 * d), 0.5 * d ** -0.5),
        "b_ada": nrm(ks[3], (DEPTH, 6 * d), 0.02),
        "g_mix": 1.0 + nrm(ks[4], (DEPTH, d), 0.02),
        "w_in": nrm(ks[5], (DEPTH, d, 3 * D_MIX), d ** -0.5),
        "g_dil_out": 1.0 + nrm(ks[6], (DEPTH, D_DIL), 0.02),
        "g_sb_out": 1.0 + nrm(ks[7], (DEPTH, D_SB), 0.02),
        "w_out": nrm(ks[8], (DEPTH, D_MIX, d), D_MIX ** -0.5),
        "g_ffn": 1.0 + nrm(ks[9], (DEPTH, d), 0.02),
        "w_group": nrm(ks[10], (DEPTH, d, N_GROUPS), d ** -0.5),
        "w_expert": nrm(ks[11], (DEPTH, d, N_EXPERTS), d ** -0.5),
        "w_gate": nrm(ks[12], (DEPTH, N_EXPERTS, d, D_FF_EXPERT), d ** -0.5),
        "w_up": nrm(ks[13], (DEPTH, N_EXPERTS, d, D_FF_EXPERT), d ** -0.5),
        "w_down": nrm(ks[14], (DEPTH, N_EXPERTS, D_FF_EXPERT, d), D_FF_EXPERT ** -0.5),
        "g_final": 1.0 + nrm(ks[15], (d,), 0.02),
    }

def second_block(x, c, w_ada, b_ada, g_mix, w_in, g_dil_out, g_sb_out, w_out, g_ffn,
              w_group, w_expert, w_gate, w_up, w_down, g_final):
    b, s, d = x.shape
    cond = jax.nn.silu(c)
    for layer in range(DEPTH):
        mod = cond @ w_ada[layer] + b_ada[layer]
        shift_mix, scale_mix, gate_mix, shift_ffn, scale_ffn, gate_ffn = jnp.split(mod, 6, axis=-1)

        h = _modulate(_rmsnorm(x, g_mix[layer]), shift_mix, scale_mix)
        qkv = h @ w_in[layer]
        q_d, k_d, v_d, q_s, k_s, v_s = jnp.split(
            qkv, [D_DIL, 2 * D_DIL, 3 * D_DIL, 3 * D_DIL + D_SB, 3 * D_DIL + 2 * D_SB], axis=-1)
        heads_d = lambda t: t.reshape(b, s, N_HEADS_DIL, HEAD_DIM)
        heads_s = lambda t: t.reshape(b, s, N_HEADS_SB, HEAD_DIM)
        o_dil = _dilated_mixture(heads_d(q_d), heads_d(k_d), heads_d(v_d)).reshape(b, s, D_DIL)
        o_sb = _stick_breaking_attention(heads_s(q_s), heads_s(k_s), heads_s(v_s)).reshape(b, s, D_SB)
        mixed = jnp.concatenate([_rmsnorm(o_dil, g_dil_out[layer]),
                                 _rmsnorm(o_sb, g_sb_out[layer])], axis=-1)
        x = x + gate_mix[:, None, :] * (mixed @ w_out[layer])

        h2 = _modulate(_rmsnorm(x, g_ffn[layer]), shift_ffn, scale_ffn).reshape(b * s, d)
        y = _hierarchical_moe(h2, w_group[layer], w_expert[layer],
                              w_gate[layer], w_up[layer], w_down[layer]).reshape(b, s, d)
        x = x + gate_ffn[:, None, :] * y
    return _rmsnorm(x, g_final)


def setup_inputs(seed=0):
    out = dict(first_inputs(seed))
    for name, value in second_inputs(seed + 1).items():
        if name != "x":
            out[name + "_2"] = value
    return out


def reference(
    x, attn_pre_g, w_in, swa_sinks, swa_out_g, diff_lq1, diff_lk1, diff_lq2, diff_lk2,
    diff_subln_g, w_out, attn_post_g, ffn_pre_g, w_up, conv_w, conv_b, w_down, ffn_post_g, c_2,
    w_ada_2, b_ada_2, g_mix_2, w_in_2, g_dil_out_2, g_sb_out_2, w_out_2, g_ffn_2, w_group_2,
    w_expert_2, w_gate_2, w_up_2, w_down_2, g_final_2,
):
    x = first_block(
        x, attn_pre_g, w_in, swa_sinks, swa_out_g, diff_lq1, diff_lk1, diff_lq2, diff_lk2,
        diff_subln_g, w_out, attn_post_g, ffn_pre_g, w_up, conv_w, conv_b, w_down, ffn_post_g,
    )
    return second_block(
        x, c_2, w_ada_2, b_ada_2, g_mix_2, w_in_2, g_dil_out_2, g_sb_out_2, w_out_2, g_ffn_2,
        w_group_2, w_expert_2, w_gate_2, w_up_2, w_down_2, g_final_2,
    )


_drawn_inputs = setup_inputs


def setup_inputs(seed=0):
    import zlib

    import numpy as np

    out = dict(_drawn_inputs(seed))
    spreads = {}
    factors = {'diff_lq1': 8.0,
     'conv_b': 3.266,
     'b_ada_2': 3.531,
     'g_mix_2': 8.0,
     'g_dil_out_2': 8.0,
     'g_sb_out_2': 8.0,
     'g_ffn_2': 7.718,
     'g_final_2': 2.86}
    for name, (base, spread) in spreads.items():
        noise = np.random.default_rng([zlib.crc32(name.encode()), seed]).standard_normal(out[name].shape)
        drawn = base * np.exp(spread * noise) if base else spread * noise
        out[name] = __import__('jax').numpy.asarray(drawn.astype(out[name].dtype))
    for name, factor in factors.items():
        out[name] = (out[name] * factor).astype(out[name].dtype)
    return out
```

```python
import math
from contextlib import ExitStack

import numpy as np

import concourse.bass as bass
from concourse import mybir


def alibi_slopes(n):
    def pow2(m):
        return [2.0 ** (-8.0 * (i + 1) / m) for i in range(m)]
    if math.log2(n).is_integer():
        return pow2(n)
    c = 2 ** int(math.floor(math.log2(n)))
    return sorted(pow2(c) + pow2(2 * c)[0::2][: n - c], reverse=True)


def two_block_kernel(nc, a, out):
    f32 = mybir.dt.float32
    bf16 = mybir.dt.bfloat16
    i32 = mybir.dt.int32
    ALU = mybir.AluOpType
    ACT = mybir.ActivationFunctionType
    X = mybir.AxisListType.X
    ds = bass.ds

    P = 128
    D = a["x"].shape[2]
    S = a["x"].shape[1]
    T = S // P
    KD = D // P
    HD = 64
    HALF = 512
    FF = a["w_down"].shape[1]
    FT = 2 * FF // P
    CHUNKS = FF // HALF
    NEXP = a["w_gate_2"].shape[1]
    FE = a["w_gate_2"].shape[3]
    KE = FE // P
    NGRP = a["w_group_2"].shape[2]
    EPG = NEXP // NGRP
    SLOTS = 64
    PAIRS = NEXP // 2
    PASSES = S // SLOTS
    ADA = a["w_ada_2"].shape[2]
    ADA_W = 256
    ADA_PIECES = ADA // ADA_W
    EPS = 1e-6
    SCALE = HD ** -0.5
    NEG = -1e30
    LAMBDA_INIT = 0.8 - 0.6 * math.exp(-0.3 * 0)
    SWA_Q, SWA_KV, DIFF_H, DIL_H, SB_H, WINDOW = 8, 2, 4, 8, 8, 128
    slopes12 = alibi_slopes(SWA_Q + DIFF_H)
    swa_slopes, diff_slopes = slopes12[:SWA_Q], slopes12[SWA_Q:]
    dil_slopes = [2.0 ** (-8.0 * (i + 1) / DIL_H) for i in range(DIL_H)]

    SLOT_N = 6
    SLOT_W = 4096
    N_IN = 0
    IN_CHUNKS = -(-a["w_in"].shape[2] // HALF)
    N_OUT = N_IN + IN_CHUNKS
    N_FFN = N_OUT + 2
    N_IN2 = N_FFN + 3 * CHUNKS
    IN2_CHUNKS = a["w_in_2"].shape[2] // HALF
    N_OUT2 = N_IN2 + IN2_CHUNKS
    N_MOE = N_OUT2 + 2

    def seq_gate(i):
        return N_FFN if i == 0 else N_FFN + 2 + 3 * (i - 1)

    def seq_down(i):
        return N_FFN + 2 + 3 * i + 2 if i < CHUNKS - 1 else N_FFN + 3 * CHUNKS - 1

    ctx = ExitStack()
    with ctx:
        def sb(name, shape, dt=f32):
            return ctx.enter_context(nc.sbuf_tensor(name, shape, dt))

        def sem(name):
            return ctx.enter_context(nc.semaphore(name))

        ring = sb("ring", [P, SLOT_N, SLOT_W])
        x = sb("x_tok", [P, T, D])
        hn = sb("hn", [P, T, D])
        hT = sb("hT", [P, KD, S])
        mix = sb("mix", [P, T, D])
        scratch = sb("scratch", [P, 7168])
        kT = sb("kT", [P, 8, S])
        vt = sb("v_tok", [P, T, D])
        bias = sb("bias", [P, 12, S])
        post_attn = sb("post_attn", [P, D])
        post_ffn = sb("post_ffn", [P, D])
        final_g = sb("final_g", [P, D])
        vec = sb("vec", [P, 3, P])
        ident = sb("ident", [P, P])
        from_here = sb("from_here", [P, P])
        before = sb("before", [P, P])
        ones = sb("ones", [P, P])
        negdist = sb("negdist", [P, S])
        lncount = sb("lncount", [P, S])
        iota = sb("iota", [P, SLOTS])
        zrow = sb("zrow", [P, HALF], bf16)
        small = sb("small", [P, 400])
        n_pairs_i = sb("n_pairs_i", [P, 1], i32)

        place = [0]

        def cell(*shape):
            n = int(np.prod(shape))
            v = small[:, place[0]:place[0] + n]
            place[0] += n
            if len(shape) == 2:
                v = v.rearrange("p (a b) -> p a b", a=shape[0])
            return v

        ms = cell(10)
        rstd = cell(10)
        minus_half = cell(10)
        ROOTS = [2, 10, 2, 2, 2, 2, 4, 2, 2]
        tiny = cell(1)
        tiny2 = cell(1)
        sq = cell(4)
        nm = cell(2 * T, 8)
        den = cell(2 * T, 8)
        rden = cell(2 * T, 8)
        sinks = cell(8)
        negsink = cell(8)
        esink = cell(T, 8)
        lamv = mix[:, 0, 0:256].rearrange("p (a b) -> p a b", a=4)
        lam2 = cell(2)
        lam = cell(1)
        rl = cell(T, 4)
        modc = cell(4, KD)
        gmixc = cell(KD)
        gffnc = cell(KD)
        siluc = cell(KD)
        subc = cell(1)

        qz = scratch[:, 0:4096].rearrange("p (h s) -> p h s", s=S)
        Lb = scratch[:, 4096:5120].rearrange("p (r n) -> p r n", r=2)
        Eb = scratch[:, 5120:6144].rearrange("p (r n) -> p r n", r=2)
        PT = scratch[:, 6144:7168].rearrange("p (r n) -> p r n", r=2)
        ada = scratch[:, 0:ADA]
        ada_buf = [kT[:, :, :], vt[:, :, :].rearrange("p t (k n) -> p (t k) n", n=ADA_W)]
        conv = mix[:, :, :].rearrange("p c (f s) -> p c f s", s=S)
        act = hn[:, :, :].rearrange("p c (f s) -> p c f s", s=S)
        off = [0]

        def piece(*shape):
            n = int(np.prod(shape))
            v = scratch[:, off[0]:off[0] + n]
            off[0] += n
            if len(shape) == 2:
                return v.rearrange("p (a b) -> p a b", a=shape[0])
            if len(shape) == 3:
                return v.rearrange("p (a b c) -> p a b c", a=shape[0], b=shape[1])
            return v

        oneh = piece(T, P)
        onehw = piece(T, P)
        xeT = piece(KD, P)
        eact = piece(HALF)
        eactT = piece(KE, P)
        combT = piece(T, P)
        ye = piece(D)
        lg = piece(T, NGRP + NEXP)
        sel = piece(T, NGRP, EPG)
        el, esh, el2, c8, oh1 = (piece(T, EPG) for _ in range(5))
        gsh, gexp, c4, ohg = (piece(T, NGRP) for _ in range(4))
        gmax, gsum, ggate, gidx, m1, i1, m2, i2, ed, p1, p2, id1, id2 = (piece(T) for _ in range(13))
        A1, A2, Aa, Wt, Wt2 = (piece(T, NEXP) for _ in range(5))
        rank1 = piece(T, NEXP)
        ranks = piece(T, PASSES * NEXP + 2)
        wsel = piece(T, PASSES * NEXP)
        wr = piece(KD, NGRP + NEXP)
        cmax, over = piece(1), piece(1)
        SB_ADD = bias[:, 8:10, :].rearrange("p a s -> p (a s)")[:, 0:384]
        SB_NEG = bias[:, 10:12, :].rearrange("p a s -> p (a s)")[:, 0:384]
        stage = hn[:, 0, 0:384].rearrange("p (a b) -> p a b", a=3)

        PS = [ctx.enter_context(nc.psum_tensor(f"bank{i}", [P, HALF], f32)) for i in range(8)]

        def v_c(k): return vec[:, 2, k:k + 1]
        R_C, R_PRE, R_FPRE, R_MIX, R_FFN, R_SWA, R_DIL, R_SB, R_SUB = 0, 8, 16, 24, 32, 40, 44, 48, 52

        loaded = [sem(f"loaded{i}") for i in range(SLOT_N)]
        s_x = sem("s_x")
        s_stage = sem("s_stage")
        s_rows = sem("s_rows")
        s_sink = sem("s_sink")
        s_lamv = sem("s_lamv")
        s_const = sem("s_const")
        s_mask = sem("s_mask")
        s_qzero = sem("s_qzero")
        s_pool = sem("s_pool")
        s_vecT = sem("s_vecT")
        s_vec = sem("s_vec")
        s_lamx = sem("s_lamx")
        s_lame = sem("s_lame")
        s_c = sem("s_c")
        s_ms = sem("s_ms")
        s_rs = sem("s_rs")
        s_link = sem("s_link")
        s_alink = sem("s_alink")
        TURNS = ["attn1", "mix1", "ffn", "attn2", "mix2", "moe"]
        s_src = {t: sem("s_src_" + t) for t in TURNS}
        s_turn = {t: sem("s_turn_" + t) for t in TURNS}
        s_hT = {t: sem("s_hT_" + t) for t in TURNS}
        s_gemm = [sem("s_gemm1"), sem("s_gemm2")]
        s_evA = [sem("s_evA1"), sem("s_evA2")]
        s_evV = [sem("s_evV1"), sem("s_evV2")]
        s_sc = [sem("s_sc1"), sem("s_sc2")]
        s_log = [sem("s_log1"), sem("s_log2")]
        s_max = [sem("s_max1"), sem("s_max2")]
        s_exp = [sem("s_exp1"), sem("s_exp2")]
        s_dif = sem("s_dif")
        s_tr = [sem("s_tr1"), sem("s_tr2")]
        s_pt = [sem("s_pt1"), sem("s_pt2")]
        s_pv = [sem("s_pv1"), sem("s_pv2")]
        s_sk = sem("s_sk")
        s_ske = sem("s_ske")
        s_att = [sem("s_att1"), sem("s_att2")]
        s_proj = [sem("s_proj1"), sem("s_proj2")]
        s_sq = [sem("s_sq1"), sem("s_sq2"), sem("s_sq3")]
        s_up = sem("s_up")
        s_tap = sem("s_tap")
        s_cv1 = sem("s_cv1")
        s_conv = sem("s_conv")
        s_sum = sem("s_sum")
        s_gelu = sem("s_gelu")
        s_act = sem("s_act")
        s_down = sem("s_down")
        s_adab = [sem("s_adab0"), sem("s_adab1")]
        s_adau = sem("s_adau")
        s_ada0 = sem("s_ada0")
        s_adam = sem("s_adam")
        s_mod = sem("s_mod")
        s_modc = sem("s_modc")
        s_bias2 = sem("s_bias2")
        s_z = sem("s_z")
        s_zm = sem("s_zm")
        s_sb1 = sem("s_sb1")
        s_sb2 = sem("s_sb2")
        s_lk = sem("s_lk")
        s_R = sem("s_R")
        s_t = sem("s_t")
        s_w = sem("s_w")
        s_sbo = sem("s_sbo")
        s_wr = sem("s_wr")
        s_back = sem("s_back")
        s_h2 = sem("s_h2")
        s_lg = sem("s_lg")
        s_r1 = sem("s_r1")
        s_r2 = sem("s_r2")
        s_A = sem("s_A")
        s_rank = sem("s_rank")
        s_np = sem("s_np")
        s_oneh = sem("s_oneh")
        s_onehw = sem("s_onehw")
        s_disp = sem("s_disp")
        s_xeA = sem("s_xeA")
        s_xeV = sem("s_xeV")
        s_eg = sem("s_eg")
        s_eu = sem("s_eu")
        s_silu = sem("s_silu")
        s_eact = sem("s_eact")
        s_etr = sem("s_etr")
        s_eactT = sem("s_eactT")
        s_ctr = sem("s_ctr")
        s_combT = sem("s_combT")
        s_edn = sem("s_edn")
        s_yA = sem("s_yA")
        s_yV = sem("s_yV")
        s_comb = sem("s_comb")
        s_fin = sem("s_fin")
        s_out = sem("s_out")

        def chunk_view(slot):
            return ring[:, slot, :].rearrange("p (k n) -> p k n", n=HALF)

        items1 = []
        for j in range(4):
            items1.append((0, "q", ("swa", j)))
        items1.append((1, "k", (0, 0)))
        items1.append((1, "v", (128, 128, 0)))
        QB0 = SWA_Q * HD + 2 * SWA_KV * HD
        for h in range(DIFF_H):
            c = QB0 + h * P
            items1.append((c // HALF, "q", ("pair", c % HALF, 8 + 2 * h)))
        for h in range(DIFF_H):
            c = QB0 + HALF + h * P
            items1.append((c // HALF, "k", (c % HALF, 1 + h)))
        items1.append((3, "v", (256, 256, 128)))
        items1.append((4, "v", (0, 256, 384)))
        items2 = []
        for part in range(2):
            for j in range(4):
                items2.append((3 * part, "q", ("pair", j * P, 8 * part + 2 * j)))
            for j in range(4):
                items2.append((3 * part + 1, "k", (j * P, 4 * part + j)))
            for t in range(T):
                items2.append((3 * part + 2, "vt", (t, 512 * part)))
        ITEMS = [items1, items2]
        FIRST_BANK = [4, 4]

        def item_bank(blk, n):
            return PS[(FIRST_BANK[blk] + n) % 8]

        def consumed(n):
            if n < N_OUT:
                return s_gemm[0], sum(c <= n - N_IN for c, _, _ in items1)
            if n < N_FFN:
                return s_proj[0], T * (n - N_OUT + 1)
            if n < N_IN2:
                for i in range(CHUNKS):
                    if n in (seq_gate(i), seq_gate(i) + 1):
                        return s_up, 4 * i + 2 * (n - seq_gate(i) + 1)
                    if n == seq_down(i):
                        return s_down, i + 1
            if n < N_OUT2:
                return s_gemm[1], sum(c <= n - N_IN2 for c, _, _ in items2)
            return s_proj[1], T * (n - N_OUT2 + 1)

        def unit(kind, t, maps):
            return dict(kind=kind, t=t, maps=maps, w=P * (t + 1))
        swa_unit = lambda h: dict(q=2 * (h % 4) + h // 4, k=0, b=h, v=(h // 4) * HD, vw=HD, o=h * HD, h=h)
        diff_unit = lambda h, m: dict(q=8 + 2 * h + m, k=1 + h, b=8 + h, v=128 + h * 128, vw=128, o=h * 128, h=h)
        dil_unit = lambda h: dict(q=h, k=h // 2, b=h, v=h * HD, vw=HD, o=h * HD, h=h)
        units1 = [unit("swa", 0, [swa_unit(h) for h in range(4 * u, 4 * u + 4)]) for u in range(2)]
        units1 += [unit("swa", 1, [swa_unit(2 * u), swa_unit(2 * u + 1)]) for u in range(4)]
        units1 += [unit("diff", 0, [diff_unit(2 * u + i // 2, i % 2) for i in range(4)]) for u in range(2)]
        units1 += [unit("diff", 1, [diff_unit(u, 0), diff_unit(u, 1)]) for u in range(4)]
        units2 = [unit("dil", 0, [dil_unit(h) for h in range(4 * u, 4 * u + 4)]) for u in range(2)]
        units2 += [unit("dil", 1, [dil_unit(2 * u), dil_unit(2 * u + 1)]) for u in range(4)]
        UNITS = [units1, units2]

        def row_of(u):
            return (2 if u["kind"] == "diff" else 0) + u["t"]

        def col_of(u):
            m = u["maps"][0]
            return (4 * (m["h"] // 2) if u["t"] == 0 else 2 * m["h"]) if u["kind"] == "diff" else m["h"]

        def out_bank(u):
            return PS[(6 if u["kind"] == "diff" else 4) + u["t"]]

        def turned(u):
            maps = u["maps"][0::2] if u["kind"] == "diff" else u["maps"]
            return [(i * u["w"] + kb * P, kb, m) for i, m in enumerate(maps) for kb in range(u["t"] + 1)]

        def finishes(blk):
            units = UNITS[blk]
            return [n for n in range(len(units)) if n + 1 == len(units) or row_of(units[n + 1]) != row_of(units[n])]

        def taken(blk, kind, where, bank):
            if kind == "q":
                q0 = 2 * where[1] if where[0] == "swa" else where[2]
                return [(qz[64 * g:64 * g + 64, q0 + g, :], bank[64 * g:64 * g + 64, 0:S]) for g in range(2)]
            if kind == "k":
                return [(kT[:, where[1], :], bank[:, 0:S])]
            if kind == "v":
                _, cw, c0 = where
                return [(vt[:, :, c0:c0 + cw], bank[:, 0:T * cw].rearrange("p (t n) -> p t n", t=T))]
            t, c0 = where
            return [(vt[:, t, c0:c0 + HALF], bank[:, :])]

        block = ctx.enter_context(nc.Block())

        @block.sync
        def _(sp):
            w_in = a["w_in"].rearrange("o (k p) n -> p (o k) n", p=P)
            w_out = a["w_out"].rearrange("o (k p) n -> p (o k) n", p=P)
            w_up = a["w_up"].rearrange("o (k p) n -> p (o k) n", p=P)
            w_down = a["w_down"].rearrange("o (k p) n -> p (o k) n", p=P)
            w_in2 = a["w_in_2"].rearrange("o (k p) n -> p (o k) n", p=P)
            w_out2 = a["w_out_2"].rearrange("o (k p) n -> p (o k) n", p=P)
            w_gate = a["w_gate_2"].rearrange("o e (k p) n -> p (o e) k n", p=P)
            w_eup = a["w_up_2"].rearrange("o e (k p) n -> p (o e) k n", p=P)
            w_edown = a["w_down_2"].rearrange("o e (k p) n -> p (o e) k n", p=P)

            def load(slot, src, free):
                if free is not None:
                    sp.wait_ge(*free)
                dst = ring[:, slot, :].rearrange("p (k n) -> p k n", k=src.shape[1])
                if src.shape[2] < dst.shape[2]:
                    dst = dst[:, :, 0:src.shape[2]]
                sp.dma_start(dst, src).then_inc(loaded[slot], 16)

            def straight(n, src):
                load(n % SLOT_N, src, consumed(n - SLOT_N) if n >= SLOT_N else None)

            sp.dma_start(x[:, :, :], a["x"].rearrange("o (t p) d -> p (o t) d", p=P)).then_inc(s_x, 16)
            for c in range(IN_CHUNKS):
                straight(N_IN + c, w_in[:, :, c * HALF:min((c + 1) * HALF, w_in.shape[2])])
            for c in range(2):
                straight(N_OUT + c, w_out[:, :, c * HALF:(c + 1) * HALF])
            for c in range(2):
                straight(N_FFN + c, w_up[:, :, c * FF:c * FF + HALF])

            def ffn_chunks(i):
                return (w_up[:, :, ds(i * HALF, HALF)], w_up[:, :, ds(FF + i * HALF, HALF)],
                        w_down[:, ds((i - 1) * KE, KE), :])

            for i in (1, 2):
                for c, src in enumerate(ffn_chunks(i)):
                    straight(seq_gate(i) + c, src)
            with sp.Fori(1, (CHUNKS - 2) // 2) as j:
                for r in range(2):
                    i = 2 * j + 1 + r
                    for c, (src, free) in enumerate(zip(ffn_chunks(i), ((s_up, 4 * (i - 2) + 2), (s_up, 4 * (i - 2) + 4),
                                                                        (s_down, i - 2)))):
                        load((seq_gate(1 + r) + c) % SLOT_N, src, free)
            for c, src in enumerate(ffn_chunks(CHUNKS - 1)):
                straight(seq_gate(CHUNKS - 1) + c, src)
            straight(seq_down(CHUNKS - 1), w_down[:, (CHUNKS - 1) * KE:CHUNKS * KE, :])
            for c in range(IN2_CHUNKS):
                straight(N_IN2 + c, w_in2[:, :, c * HALF:(c + 1) * HALF])
            for c in range(2):
                straight(N_OUT2 + c, w_out2[:, :, c * HALF:(c + 1) * HALF])

            def expert_pair(p, q):
                for c, (w, done) in enumerate(((w_gate, s_eg), (w_eup, s_eu), (w_edown, s_edn))):
                    for e in range(2):
                        src = w[:, ds(2 * q + e, 1), :, :].rearrange("p o k n -> p (o k) n")
                        n = N_MOE + 2 * c + e
                        if isinstance(p, int):
                            straight(n, src)
                        else:
                            load(n % SLOT_N, src, (done, p))

            expert_pair(0, 0)
            with sp.Fori(1, PAIRS) as p:
                expert_pair(p, p)
            sp.wait_ge(s_np, 1)
            n_pairs = sp.value_load(n_pairs_i[0:1, 0:1], min_val=PAIRS, max_val=PAIRS * PASSES)
            with sp.If(n_pairs > PAIRS):
                with sp.Fori(1, PASSES) as r:
                    with sp.Fori(0, PAIRS) as q:
                        expert_pair(r * PAIRS + q, q)
            sp.wait_ge(s_fin, T)
            sp.dma_start(out.rearrange("o (t p) d -> p (o t) d", p=P), hn[:, :, :]).then_inc(s_out, 16)
            sp.wait_ge(s_out, 16)

        @block.gpsimd
        def _(pool):
            step = [0]
            norms = [0]

            def inverse_roots(count):
                for _ in range(count):
                    n, w = norms[0], ROOTS[norms[0]]
                    norms[0] += 1
                    pool.wait_ge(s_ms, n + 1)
                    pool.tensor_tensor(rstd[:, 0:w], ms[:, 0:w], minus_half[:, 0:w], ALU.pow).then_inc(s_rs, 1)

            def then(ins):
                step[0] += 1
                ins.then_inc(s_pool, 1)
                pool.wait_ge(s_pool, step[0])

            pool.memset(minus_half, -0.5)
            then(pool.memset(ident[:, :], 0.0))
            pool.affine_select(out=ident[:, :], in_=ident[:, :], compare_op=ALU.not_equal, fill=1.0, base=0,
                               pattern=[[-1, P]], channel_multiplier=1).then_inc(s_const, 1)
            pool.dma_start(post_attn[:, :], a["attn_post_g"][0].partition_broadcast(P)).then_inc(s_rows, 16)
            pool.dma_start(post_ffn[:, :], a["ffn_post_g"][0].partition_broadcast(P)).then_inc(s_rows, 16)
            pool.dma_start(final_g[:, :], a["g_final_2"].partition_broadcast(P)).then_inc(s_rows, 16)
            pool.memset(ones[:, :], 1.0).then_inc(s_const, 1)
            pool.memset(zrow[:, :], 0.0).then_inc(s_const, 1)
            then(pool.memset(from_here[:, :], 1.0))
            pool.affine_select(out=from_here[:, :], in_=from_here[:, :], compare_op=ALU.is_ge, fill=0.0, base=0,
                               pattern=[[-1, P]], channel_multiplier=1).then_inc(s_const, 1)
            then(pool.memset(before[:, :], 1.0))
            pool.affine_select(out=before[:, :], in_=before[:, :], compare_op=ALU.is_gt, fill=0.0, base=0,
                               pattern=[[1, P]], channel_multiplier=-1).then_inc(s_const, 1)
            pool.iota(iota[:, :], [[1, SLOTS]], base=0, channel_multiplier=0,
                      allow_small_or_imprecise_dtypes=True).then_inc(s_const, 1)
            then(pool.iota(negdist[:, :], [[1, S]], base=-P, channel_multiplier=-1,
                           allow_small_or_imprecise_dtypes=True))
            pool.memset(qz[:, :, :], 0.0).then_inc(s_qzero, 1)
            for h in range(SWA_Q):
                pool.tensor_scalar(bias[:, h, :], negdist[:, :], float(np.float32(swa_slopes[h])), None, ALU.mult)
            for h in range(DIFF_H):
                last = pool.tensor_scalar(bias[:, SWA_Q + h, :], negdist[:, :], float(np.float32(diff_slopes[h])),
                                          None, ALU.mult)
            then(last)
            then(pool.affine_select(out=bias[:, :, :], in_=bias[:, :, :], compare_op=ALU.is_ge, fill=NEG, base=P,
                                    pattern=[[0, 12], [-1, S]], channel_multiplier=1))
            pool.affine_select(out=bias[:, 0:SWA_Q, :], in_=bias[:, 0:SWA_Q, :], compare_op=ALU.is_ge, fill=NEG,
                               base=WINDOW - 1 - P, pattern=[[0, SWA_Q], [1, S]],
                               channel_multiplier=-1).then_inc(s_mask, 1)
            inverse_roots(1)

            inverse_roots(1)
            pool.wait_ge(s_att[0], 1)
            then(pool.memset(ada, 0.0))
            pool.dma_start(ada[0:1, :], a["b_ada_2"]).then_inc(s_ada0, 16)
            then(pool.memset(SB_ADD, 0.0))
            then(pool.memset(SB_NEG, -1.0))
            for m, fill in ((SB_ADD, NEG), (SB_NEG, 0.0)):
                for c in (0, 256):
                    then(pool.affine_select(out=m[:, c:c + P], in_=m[:, c:c + P], compare_op=ALU.is_gt, fill=fill,
                                            base=0, pattern=[[1, P]], channel_multiplier=-1))
            pool.memset(tiny, 0.0).then_inc(s_bias2, 1)
            inverse_roots(2)
            w_ada = a["w_ada_2"].rearrange("o (k p) n -> p (o k) n", p=P)
            with pool.Fori(0, ADA_PIECES // 8) as j:
                for c in range(8):
                    pool.wait_ge(s_adau, 8 * j + c + 1)
                    pool.dma_start(ada_buf[c % 2], w_ada[:, :, ds((8 * j + c) * ADA_W, ADA_W)])\
                        .then_inc(s_adab[c % 2], 16)
            inverse_roots(1)
            pool.wait_ge(s_adam, 5)
            pool.memset(qz[:, :, :], 0.0).then_inc(s_qzero, 1)
            inverse_roots(2)
            pool.wait_ge(s_att[1], 1)
            pool.dma_start(wr[:, :, 0:NGRP], a["w_group_2"].rearrange("o (k p) n -> p (o k) n", p=P),
                           allow_slow_non_contiguous=True).then_inc(s_wr, 16)
            pool.dma_start(wr[:, :, NGRP:NGRP + NEXP], a["w_expert_2"].rearrange("o (k p) n -> p (o k) n", p=P),
                           allow_slow_non_contiguous=True).then_inc(s_wr, 16)
            inverse_roots(2)

        @block.tensor
        def _(pe):
            def arrived(n):
                pe.wait_ge(loaded[n % SLOT_N], 16 * (n // SLOT_N + 1))

            def turn(tag, src, rows_each):
                pe.wait_ge(s_src[tag], rows_each)
                for k in range(KD):
                    for t in range(T):
                        c = (k % 2) * S + t * P
                        last = pe.transpose(PS[k // 2][:, c:c + P], src[:, t, k * P:(k + 1) * P], ident[:, :])
                    if k % 2:
                        last.then_inc(s_turn[tag], 1)

            def project(blk, n_base):
                items = ITEMS[blk]
                tag = ("attn1", "attn2")[blk]
                pe.wait_ge(s_hT[tag], KD)
                chunk = -1
                for n, (c, kind, where) in enumerate(items):
                    if c != chunk:
                        arrived(n_base + c)
                        chunk = c
                    bank = item_bank(blk, n)
                    w = chunk_view((n_base + c) % SLOT_N)
                    if n >= 8:
                        m = n - 8
                        pe.wait_ge((s_evA, s_evV)[m % 2][blk], m // 2 + 1)
                    for k in range(KD):
                        flags = dict(start=(k == 0), stop=(k == KD - 1))
                        if kind == "q" and where[0] == "swa":
                            j = where[1]
                            for g in range(2):
                                c0 = (4 * g + j) * HD
                                last = pe.matmul(bank[HD * g:HD * g + HD, 0:S], w[:, k, c0:c0 + HD], hT[:, k, :],
                                                 **flags)
                        elif kind == "q":
                            last = pe.matmul(bank[:, 0:S], w[:, k, where[1]:where[1] + P], hT[:, k, :], **flags)
                        elif kind == "k":
                            last = pe.matmul(bank[:, 0:S], w[:, k, where[0]:where[0] + P], hT[:, k, :], **flags)
                        elif kind == "vt":
                            t = where[0]
                            last = pe.matmul(bank[:, :], hT[:, k, t * P:(t + 1) * P], w[:, k, :], **flags)
                    if kind == "v":
                        c0, cw, _ = where
                        for t in range(T):
                            for k in range(KD):
                                last = pe.matmul(bank[:, t * cw:(t + 1) * cw], hT[:, k, t * P:(t + 1) * P],
                                                 w[:, k, c0:c0 + cw], start=(k == 0), stop=(k == KD - 1))
                    last.then_inc(s_gemm[blk], 1)

            def attention(blk):
                units = UNITS[blk]
                n_items = len(ITEMS[blk])
                pe.wait_ge(s_evA[blk], (n_items + 1) // 2)
                pe.wait_ge(s_evV[blk], n_items // 2)
                for i in range(len(units) + 2):
                    if i < len(units):
                        u = units[i]
                        if i >= 2:
                            pe.wait_ge(s_log[blk], i - 1)
                        for j, m in enumerate(u["maps"]):
                            last = pe.matmul(PS[i % 2][:, j * u["w"]:(j + 1) * u["w"]],
                                             qz[:, m["q"], u["t"] * P:(u["t"] + 1) * P], kT[:, m["k"], 0:u["w"]],
                                             start=True, stop=True)
                        last.then_inc(s_sc[blk], 1)
                    if 1 <= i <= len(units):
                        n = i - 1
                        u = units[n]
                        if u["kind"] == "diff":
                            pe.wait_ge(s_dif, n - len(units) // 2 + 1)
                        else:
                            pe.wait_ge(s_exp[blk], n + 1)
                        if n >= 2:
                            pe.wait_ge(s_pt[blk], n - 1)
                        for b, (c, kb, m) in enumerate(turned(u)):
                            last = pe.transpose(PS[2 + n % 2][:, b * P:(b + 1) * P], Eb[:, n % 2, c:c + P],
                                                ident[:, :])
                        last.then_inc(s_tr[blk], 1)
                    if i >= 2:
                        n = i - 2
                        u = units[n]
                        pe.wait_ge(s_pt[blk], n + 1)
                        for b, (c, kb, m) in enumerate(turned(u)):
                            last = pe.matmul(out_bank(u)[:, m["o"]:m["o"] + m["vw"]], PT[:, n % 2, b * P:(b + 1) * P],
                                             vt[:, kb, m["v"]:m["v"] + m["vw"]],
                                             start=(kb == 0), stop=(kb == u["t"]))
                        last.then_inc(s_pv[blk], 1)

            def out_projection(blk, n_base):
                tag = ("mix1", "mix2")[blk]
                pe.wait_ge(s_hT[tag], KD)
                for c in range(2):
                    n = n_base + c
                    arrived(n)
                    w = chunk_view(n % SLOT_N)
                    for t in range(T):
                        for k in range(KD):
                            last = pe.matmul(PS[4 + 2 * t + c][:, :], hT[:, k, t * P:(t + 1) * P], w[:, k, :],
                                             start=(k == 0), stop=(k == KD - 1))
                        last.then_inc(s_proj[blk], 1)

            pe.wait_ge(s_const, 6)
            pe.wait_ge(s_stage, 16 * 12)
            pe.transpose(PS[7][:, 0:P], stage[:, 0, :], ident[:, :])
            pe.transpose(PS[7][:, P:2 * P], stage[:, 1, :], ident[:, :])
            pe.transpose(PS[7][:, 2 * P:2 * P + 53], stage[0:53, 2, :], ident[0:53, 0:53]).then_inc(s_vecT, 1)

            turn("attn1", hn, T)
            pe.wait_ge(s_vec, 1)
            project(0, N_IN)
            attention(0)
            turn("mix1", mix, T)
            out_projection(0, N_OUT)
            turn("ffn", hn, T)

            def zero_sums():
                for b in range(4, 8):
                    pe.matmul(PS[b][:, :], zrow[:, 0:P], zrow[:, :], start=True, stop=False, skip_group_check=True)

            def up(i, base, j):
                for part in range(2):
                    n = base + part
                    pe.wait_ge(loaded[n % SLOT_N], 16 * (n // SLOT_N + 1 + j))
                    w = chunk_view(n % SLOT_N)
                    for b in range(2):
                        if not isinstance(i, int) or i > 0:
                            pe.wait_ge(s_conv, 4 * (i - 1) + 2 * part + b + 1)
                        for f in range(2):
                            c = (2 * b + f) * P
                            for k in range(KD):
                                last = pe.matmul(PS[2 * part + b][:, f * S:(f + 1) * S], w[:, k, c:c + P],
                                                 hT[:, k, :], start=(k == 0), stop=(k == KD - 1))
                        last.then_inc(s_up, 1)

            def down(i, par, n, j):
                pe.wait_ge(loaded[n % SLOT_N], 16 * (n // SLOT_N + 1 + j))
                pe.wait_ge(s_act, i + 1)
                w = ring[:, n % SLOT_N, :].rearrange("p (k n) -> p k n", n=D)
                for k in range(KE):
                    for t in range(T):
                        for c in range(2):
                            last = pe.matmul(PS[4 + 2 * t + c][:, :], act[:, par, k, t * P:(t + 1) * P],
                                             w[:, k, c * HALF:(c + 1) * HALF], start=False, stop=False,
                                             skip_group_check=True)
                last.then_inc(s_down, 1)

            pe.wait_ge(s_hT["ffn"], KD)
            zero_sums()
            up(0, seq_gate(0), 0)
            with pe.Fori(0, (CHUNKS - 2) // 2) as j:
                for r in range(2):
                    i = 2 * j + 1 + r
                    up(i, seq_gate(1 + r), j)
                    down(i - 1, r, seq_down(r), j)
            up(CHUNKS - 1, seq_gate(CHUNKS - 1), 0)
            down(CHUNKS - 2, 0, seq_down(CHUNKS - 2), 0)
            down(CHUNKS - 1, 1, seq_down(CHUNKS - 1), 0)

            pe.wait_ge(s_adau, ADA_PIECES + 2)
            pe.wait_ge(s_conv, 4 * CHUNKS)
            for n, part in enumerate((0, 1, 3, 4)):
                for k in range(KD):
                    c = part * D + k * P
                    last = pe.matmul(PS[0][:, n * KD + k:n * KD + k + 1], ada[:, c:c + P], ones[:, 0:1],
                                     start=True, stop=True)
            last.then_inc(s_adam, 1)
            for n in range(4):
                c = (2, 5)[n // 2] * D + (n % 2) * HALF
                if n == 3:
                    pe.wait_ge(s_mod, 1)
                pe.matmul(PS[(1, 2, 3, 0)[n]][:, :], ones[:, :], ada[:, c:c + HALF],
                          start=True, stop=True).then_inc(s_adam, 1)

            pe.wait_ge(s_mod, 5)
            turn("attn2", hn, T)
            project(1, N_IN2)
            attention(1)

            for i in range(SB_H + 2):
                if i < SB_H:
                    if i >= 2:
                        pe.wait_ge(s_zm, i - 1)
                    z = PS[i % 2]
                    pe.matmul(z[:, 0:S], kT[:, 4 + i // 2, 0:P], qz[:, 8 + i, :], start=True, stop=True)
                    pe.matmul(z[:, S:S + P], kT[:, 4 + i // 2, P:S], qz[:, 8 + i, P:S],
                              start=True, stop=True).then_inc(s_z, 1)
                if 1 <= i <= SB_H:
                    n = i - 1
                    pe.wait_ge(s_lk, n + 1)
                    R = PS[2 + n % 2]
                    lk = Eb[:, n % 2, :]
                    pe.matmul(R[:, 0:S], from_here[:, :], lk[:, 0:S], start=True, stop=False)
                    pe.matmul(R[:, P:S], ones[:, :], lk[:, S:S + P], start=False, stop=True)
                    pe.matmul(R[:, S:S + P], from_here[:, :], lk[:, S:S + P], start=True, stop=True).then_inc(s_R, 1)
                if i >= 2:
                    n = i - 2
                    pe.wait_ge(s_w, n + 1)
                    w = PT[:, n % 2, :]
                    c = n * HD
                    v = lambda kb: vt[:, kb, HALF + c:HALF + c + HD]
                    pe.matmul(PS[6][:, c:c + HD], w[:, 0:P], v(0), start=True, stop=True)
                    pe.matmul(PS[7][:, c:c + HD], w[:, P:S], v(0), start=True, stop=False)
                    pe.matmul(PS[7][:, c:c + HD], w[:, S:S + P], v(1), start=False, stop=True).then_inc(s_sbo, 1)

            turn("mix2", mix, T)
            out_projection(1, N_OUT2)
            turn("moe", hn, T)

            pe.wait_ge(s_hT["moe"], KD)
            pe.wait_ge(s_wr, 32)
            for t in range(T):
                for k in range(KD):
                    last = pe.matmul(PS[4][:, t * 36:(t + 1) * 36], hT[:, k, t * P:(t + 1) * P], wr[:, k, :],
                                     start=(k == 0), stop=(k == KD - 1))
            last.then_inc(s_lg, 1)
            for t in range(T):
                for k in range(KD):
                    last = pe.transpose(PS[2 * t + k // 4][:, (k % 4) * P:(k % 4 + 1) * P], hT[:, k, t * P:(t + 1) * P],
                                        ident[:, :])
                    if k % 4 == 3:
                        last.then_inc(s_back, 1)
            pe.wait_ge(s_A, 1)
            rk = PS[5]
            pe.matmul(rk[:, 0:NEXP], before[:, :], Aa[:, 0, :], start=True, stop=True)
            pe.matmul(rk[:, NEXP:2 * NEXP], before[:, :], Aa[:, 1, :], start=True, stop=False)
            pe.matmul(rk[:, NEXP:2 * NEXP], ones[:, :], Aa[:, 0, :], start=False, stop=True)
            pe.matmul(rk[:, 2 * NEXP:3 * NEXP], ones[:, :], Aa[:, 0, :], start=True, stop=False)
            pe.matmul(rk[:, 2 * NEXP:3 * NEXP], ones[:, :], Aa[:, 1, :], start=False, stop=True).then_inc(s_rank, 1)

            ACC = [PS[0], PS[1], PS[2], PS[3]]
            XB = [PS[4], PS[5]]
            GB, UB = PS[6], PS[7]

            def dispatch(p):
                pe.wait_ge(s_oneh, p + 1)
                for k in range(KD):
                    for t in range(T):
                        last = pe.matmul(XB[k // 4][:, (k % 4) * P:(k % 4 + 1) * P], hn[:, t, k * P:(k + 1) * P],
                                         oneh[:, t, :], start=(t == 0), stop=(t == T - 1))
                last.then_inc(s_disp, 1)

            def combine(p, first=False):
                pe.wait_ge(s_combT, p + 2)
                pe.wait_ge(s_yA, p + 2)
                pe.wait_ge(s_yV, p + 2)
                for t in range(T):
                    for c in range(2):
                        last = pe.matmul(ACC[2 * t + c][:, :], combT[:, t, :], ye[:, c * HALF:(c + 1) * HALF],
                                         start=False, stop=False, skip_group_check=True)
                last.then_inc(s_comb, 1)

            def pair(p):
                def ready(c):
                    n = N_MOE + c
                    pe.wait_ge(loaded[n % SLOT_N], 16 * (n // SLOT_N + 1) + 16 * p)

                pe.wait_ge(s_xeA, p + 1)
                pe.wait_ge(s_xeV, p + 1)
                pe.wait_ge(s_eactT, p + 1)
                ready(0)
                ready(1)
                for k in range(KD):
                    for e in range(2):
                        w = chunk_view((N_MOE + e) % SLOT_N)
                        last = pe.matmul(GB[64 * e:64 * e + 64, :], xeT[:, k, 64 * e:64 * e + 64], w[:, k, :],
                                         start=(k == 0), stop=(k == KD - 1))
                last.then_inc(s_eg, 1)
                ready(2)
                ready(3)
                pe.wait_ge(s_combT, p + 1)
                for k in range(KD):
                    for e in range(2):
                        w = chunk_view((N_MOE + 2 + e) % SLOT_N)
                        last = pe.matmul(UB[64 * e:64 * e + 64, :], xeT[:, k, 64 * e:64 * e + 64], w[:, k, :],
                                         start=(k == 0), stop=(k == KD - 1))
                last.then_inc(s_eu, 1)
                pe.wait_ge(s_yA, p + 1)
                pe.wait_ge(s_yV, p + 1)
                dispatch(p + 1)
                pe.wait_ge(s_eact, p + 1)
                for f in range(KE):
                    last = pe.transpose(GB[:, f * P:(f + 1) * P], eact[:, f * P:(f + 1) * P], ident[:, :])
                last.then_inc(s_etr, 1)
                combine(p - 1)
                pe.wait_ge(s_onehw, p + 1)
                for t in range(T):
                    last = pe.transpose(UB[:, t * P:(t + 1) * P], onehw[:, t, :], ident[:, :])
                last.then_inc(s_ctr, 1)
                pe.wait_ge(s_eactT, p + 2)
                pe.wait_ge(s_xeA, p + 2)
                pe.wait_ge(s_xeV, p + 2)
                ready(4)
                ready(5)
                for c in range(2):
                    for f in range(KE):
                        for e in range(2):
                            w = ring[:, (N_MOE + 4 + e) % SLOT_N, :].rearrange("p (k n) -> p k n", n=D)
                            last = pe.matmul(XB[c][64 * e:64 * e + 64, :], eactT[:, f, 64 * e:64 * e + 64],
                                             w[:, f, c * HALF:(c + 1) * HALF], start=(f == 0), stop=(f == KE - 1))
                last.then_inc(s_edn, 1)

            pe.wait_ge(s_h2, 4)
            pe.wait_ge(s_np, 1)
            for b in range(4):
                pe.matmul(ACC[b][:, :], zrow[:, 0:P], zrow[:, :], start=True, stop=False, skip_group_check=True)
            dispatch(0)
            with pe.Fori(0, PAIRS) as p:
                pair(p)
            n_pairs = pe.value_load(n_pairs_i[0:1, 0:1], min_val=PAIRS, max_val=PAIRS * PASSES)
            with pe.If(n_pairs > PAIRS):
                with pe.Fori(PAIRS, PAIRS * PASSES) as p:
                    pair(p)
            combine(n_pairs - 1)


        @block.scalar
        def _(sc):
            order = [0]

            def then(ins):
                order[0] += 1
                ins.then_inc(s_alink, 1)
                sc.wait_ge(s_alink, order[0])

            cw = a["conv_w"].rearrange("o j (f p) -> (o j f) p", p=P)
            cb = a["conv_b"].rearrange("o (f p) -> (o f) p", p=P)
            sc.dma_start(stage[:, 0, :], cw[0:P, :]).then_inc(s_stage, 16)
            sc.dma_start(stage[0:FT, 1, :], cw[P:P + FT, :]).then_inc(s_stage, 16)
            sc.dma_start(stage[FT:2 * FT, 1, :], cb).then_inc(s_stage, 16)
            for name, row in (("c_2", R_C), ("attn_pre_g", R_PRE), ("ffn_pre_g", R_FPRE), ("g_mix_2", R_MIX),
                              ("g_ffn_2", R_FFN), ("swa_out_g", R_SWA), ("g_dil_out_2", R_DIL),
                              ("g_sb_out_2", R_SB), ("diff_subln_g", R_SUB)):
                v = a[name].rearrange("o (f p) -> (o f) p", p=P)
                sc.dma_start(stage[row:row + v.shape[0], 2, :], v).then_inc(s_stage, 16)
            sc.dma_start(sinks, a["swa_sinks"][0].partition_broadcast(P)).then_inc(s_sink, 16)
            for n, name in enumerate(("diff_lq1", "diff_lk1", "diff_lq2", "diff_lk2")):
                sc.dma_start(lamv[:, n, :], a[name][0].partition_broadcast(P)).then_inc(s_lamv, 16)

            def scaled(tag, scale, shift=None):
                for k in (2, 3, 6, 7):
                    sc.wait_ge(s_turn[tag], k // 2 + 1)
                    sc.activation(hT[:, k, :], PS[k // 2][:, (k % 2) * S:(k % 2 + 1) * S], ACT.Identity,
                                  scale=scale(k), bias=0.0 if shift is None else shift(k)).then_inc(s_hT[tag], 1)

            def take(blk):
                for n, (c, kind, where) in enumerate(ITEMS[blk]):
                    if n % 2:
                        continue
                    sc.wait_ge(s_gemm[blk], n + 1)
                    if n == 0:
                        sc.wait_ge(s_qzero, blk + 1)
                    bank = item_bank(blk, n)
                    for dst, src in taken(blk, kind, where, bank):
                        last = sc.activation(dst, src, ACT.Copy)
                    last.then_inc(s_evA[blk], 1)

            def softmaxes(blk):
                units = UNITS[blk]
                for i in range(len(units) + 1):
                    if i < len(units):
                        u = units[i]
                        sc.wait_ge(s_max[blk], i + 1)
                        if i >= 2:
                            sc.wait_ge(s_tr[blk], i - 1)
                        r, c, w = row_of(u), col_of(u), u["w"]
                        for j in range(len(u["maps"])):
                            last = sc.activation(Eb[:, i % 2, j * w:(j + 1) * w], Lb[:, i % 2, j * w:(j + 1) * w],
                                                 ACT.Exp, bias=nm[:, r, c + j:c + j + 1],
                                                 accum_out=den[:, r, c + j:c + j + 1])
                        last.then_inc(s_exp[blk], 1)
                    if i >= 1:
                        n = i - 1
                        w = P * len(turned(units[n]))
                        sc.wait_ge(s_tr[blk], n + 1)
                        if n >= 2:
                            sc.wait_ge(s_pv[blk], n - 1)
                        sc.activation(PT[:, n % 2, 0:w], PS[2 + n % 2][:, 0:w], ACT.Copy).then_inc(s_pt[blk], 1)
                if blk == 0:
                    sc.wait_ge(s_sk, 1)
                    sc.activation(esink, esink, ACT.Exp).then_inc(s_ske, 1)

            def squares(m, sem_in, count):
                sc.wait_ge(sem_in, count)
                for t in range(T):
                    for c in range(2):
                        last = sc.activation(hn[:, t, c * HALF:(c + 1) * HALF], PS[4 + 2 * t + c][:, :], ACT.Square,
                                             scale=D ** -0.5, accum_out=sq[:, 2 * t + c:2 * t + c + 1])
                last.then_inc(s_sq[m], 1)

            sc.wait_ge(s_lamx, 1)
            sc.activation(lam2, lam2, ACT.Exp).then_inc(s_lame, 1)
            sc.wait_ge(s_vec, 1)
            scaled("attn1", lambda k: vec[:, 2, R_PRE + k:R_PRE + k + 1])
            take(0)
            softmaxes(0)
            scaled("mix1", lambda k: vec[:, 2, R_SWA + k:R_SWA + k + 1] if k < 4 else subc)
            squares(0, s_proj[0], 4)
            scaled("ffn", lambda k: vec[:, 2, R_FPRE + k:R_FPRE + k + 1])
            sc.activation(siluc, vec[:, 2, R_C:R_C + KD], ACT.Silu).then_inc(s_c, 1)

            def taps(i, part):
                for b in range(2):
                    sc.wait_ge(s_up, 4 * i + 2 * part + b + 1)
                    if (not isinstance(i, int) or i > 0) and b == 0:
                        sc.wait_ge(s_act, i)
                    for f in range(2):
                        ft = KE * i + (FT // 2) * part + 2 * b + f
                        last = sc.activation(conv[:, part, 2 * b + f, :], PS[2 * part + b][:, f * S:(f + 1) * S],
                                             ACT.Identity, scale=vec[:, 1, ds(ft, 1)], bias=vec[:, 1, ds(ft + FT, 1)])
                    last.then_inc(s_tap, 1)

            def ffn(i):
                taps(i, 0)
                sc.wait_ge(s_conv, 4 * i + 2)
                sc.activation(conv[:, 0, :, :], conv[:, 0, :, :], ACT.Gelu_apprx_tanh).then_inc(s_gelu, 1)
                taps(i, 1)

            ffn(0)
            with sc.Fori(0, (CHUNKS - 2) // 2) as j:
                for r in range(2):
                    ffn(2 * j + 1 + r)
            ffn(CHUNKS - 1)
            squares(1, s_down, CHUNKS)
            sc.wait_ge(s_adam, 1)
            sc.activation(modc, PS[0][:, 0:4 * KD].rearrange("p (a b) -> p a b", a=4), ACT.Copy).then_inc(s_mod, 1)
            sc.wait_ge(s_modc, 1)
            for n in range(4):
                sc.wait_ge(s_adam, n + 2)
                dst = (post_attn, post_ffn)[n // 2][:, (n % 2) * HALF:(n % 2 + 1) * HALF]
                sc.activation(dst, PS[(1, 2, 3, 0)[n]][:, :], ACT.Copy).then_inc(s_mod, 1)
            sc.wait_ge(s_modc, 2)
            scaled("attn2", lambda k: gmixc[:, k:k + 1], lambda k: modc[:, 0, k:k + 1])
            take(1)
            softmaxes(1)
            for i in range(SB_H + 1):
                if i < SB_H:
                    sc.wait_ge(s_zm, i + 1)
                    if i >= 1:
                        sc.wait_ge(s_lk, i)
                    then(sc.activation(Lb[:, 0, 0:384], Lb[:, 1, 0:384], ACT.Abs))
                    then(sc.activation(Lb[:, 0, 0:384], Lb[:, 0, 0:384], ACT.Exp, scale=-1.0))
                    sc.activation(Lb[:, 0, 0:384], Lb[:, 0, 0:384], ACT.Ln, bias=1.0).then_inc(s_sb1, 1)
                if i >= 1:
                    n = i - 1
                    sc.wait_ge(s_t, n + 1)
                    sc.activation(PT[:, n % 2, 0:384], PT[:, n % 2, 0:384], ACT.Exp).then_inc(s_w, 1)
            scaled("mix2", lambda k: vec[:, 2, R_DIL + k:R_DIL + k + 1])
            scaled("moe", lambda k: gffnc[:, k:k + 1], lambda k: modc[:, 2, k:k + 1])
            for n in (1, 3):
                sc.wait_ge(s_back, n + 1)
                sc.activation(hn[:, n // 2, HALF:D], PS[n][:, :], ACT.Copy).then_inc(s_h2, 1)
            sc.wait_ge(s_r1, 1)
            sc.activation(gexp, gsh, ACT.Exp).then_inc(s_r2, 1)
            sc.wait_ge(s_r1, 2)
            sc.activation(ed, m2, ACT.Exp).then_inc(s_r2, 1)

            def tokens(p):
                sc.wait_ge(s_disp, p + 1)
                sc.activation(xeT[:, 0:4, :], PS[4][:, :].rearrange("p (a b) -> p a b", a=4), ACT.Copy)\
                    .then_inc(s_xeA, 1)

            def pair(p):
                sc.wait_ge(s_eg, p + 1)
                sc.wait_ge(s_etr, p + 1)
                sc.activation(eact, PS[6][:, :], ACT.Silu).then_inc(s_silu, 1)
                tokens(p + 1)
                sc.wait_ge(s_etr, p + 2)
                sc.activation(eactT, PS[6][:, :].rearrange("p (a b) -> p a b", a=KE), ACT.Copy).then_inc(s_eactT, 1)
                sc.wait_ge(s_edn, p + 1)
                sc.activation(ye[:, 0:HALF], PS[4][:, :], ACT.Copy).then_inc(s_yA, 1)

            sc.wait_ge(s_np, 1)
            tokens(0)
            with sc.Fori(0, PAIRS) as p:
                pair(p)
            n_pairs = sc.value_load(n_pairs_i[0:1, 0:1], min_val=PAIRS, max_val=PAIRS * PASSES)
            with sc.If(n_pairs > PAIRS):
                with sc.Fori(PAIRS, PAIRS * PASSES) as p:
                    pair(p)

        @block.vector
        def _(ve):
            order = [0]

            def then(ins):
                order[0] += 1
                ins.then_inc(s_link, 1)
                ve.wait_ge(s_link, order[0])

            norms = [0]

            def rooted(ins):
                norms[0] += 1
                ins.then_inc(s_ms, 1)
                ve.wait_ge(s_rs, norms[0])

            def mean_squares(src, junk, at):
                return ve.tensor_tensor_reduce(junk, src, src, 1.0 / src.shape[1], EPS, ALU.mult, ALU.add,
                                               ms[:, at:at + 1])

            def norm(tag, src, dst, junk):
                for t in range(T):
                    last = mean_squares(src[:, t, :], junk[:, t, :], t)
                rooted(last)
                for t in range(T):
                    ve.tensor_scalar(dst[:, t, :], src[:, t, :], rstd[:, t:t + 1], None, ALU.mult)\
                        .then_inc(s_src[tag], 1)

            def scaled(tag, scale, shift=None):
                for k in (0, 1, 4, 5):
                    ve.wait_ge(s_turn[tag], k // 2 + 1)
                    src = PS[k // 2][:, (k % 2) * S:(k % 2 + 1) * S]
                    if shift is None:
                        ins = ve.tensor_scalar(hT[:, k, :], src, scale(k), None, ALU.mult)
                    else:
                        ins = ve.tensor_scalar(hT[:, k, :], src, scale(k), shift(k), ALU.mult, ALU.add)
                    ins.then_inc(s_hT[tag], 1)

            def take(blk):
                for n, (c, kind, where) in enumerate(ITEMS[blk]):
                    if n % 2 == 0:
                        continue
                    ve.wait_ge(s_gemm[blk], n + 1)
                    if n == 1:
                        ve.wait_ge(s_qzero, blk + 1)
                    for dst, src in taken(blk, kind, where, item_bank(blk, n)):
                        last = ve.tensor_copy(dst, src)
                    last.then_inc(s_evV[blk], 1)

            def softmaxes(blk):
                units = UNITS[blk]
                half = len(units) // 2
                ends = finishes(blk)

                def logits(i):
                    u = units[i]
                    w, n = u["w"], len(u["maps"])
                    ve.wait_ge(s_sc[blk], i + 1)
                    if i >= 2:
                        ve.wait_ge(s_exp[blk], i - 1)
                    b0 = u["maps"][0]["b"]
                    S3 = PS[i % 2][:, 0:n * w].rearrange("p (a b) -> p a b", a=n)
                    L3 = Lb[:, i % 2, 0:n * w].rearrange("p (a b) -> p a b", a=n)
                    if u["kind"] == "diff":
                        for h in range(n // 2):
                            bb = bias[:, b0 + h, S - w:S].unsqueeze(1).broadcast_to([P, 2, w])
                            last = ve.scalar_tensor_tensor(L3[:, 2 * h:2 * h + 2, :], S3[:, 2 * h:2 * h + 2, :], SCALE,
                                                           bb, ALU.mult, ALU.add)
                    else:
                        last = ve.scalar_tensor_tensor(L3, S3, SCALE, bias[:, b0:b0 + n, S - w:S], ALU.mult, ALU.add)
                    last.then_inc(s_log[blk], 1)
                    ve.wait_ge(s_log[blk], i + 1)
                    r, c = row_of(u), col_of(u)
                    red = ve.tensor_reduce(nm[:, r, c:c + n], L3, X, ALU.max, negate=True)
                    if u["kind"] == "swa":
                        then(red)
                        red = ve.tensor_tensor(nm[:, r, c:c + n], nm[:, r, c:c + n], negsink[:, c:c + n], ALU.min)
                    red.then_inc(s_max[blk], 1)

                def difference(i):
                    u = units[i]
                    r, c, w, n = row_of(u), col_of(u), u["w"], len(u["maps"])
                    ve.wait_ge(s_exp[blk], i + 1)
                    then(ve.reciprocal(rden[:, r, c:c + n], den[:, r, c:c + n]))
                    for h in range(n // 2):
                        k = c + 2 * h
                        then(ve.tensor_scalar(rl[:, u["t"], h:h + 1], rden[:, r, k + 1:k + 2], lam, None, ALU.mult))
                        e0 = Eb[:, i % 2, 2 * h * w:(2 * h + 1) * w]
                        e1 = Eb[:, i % 2, (2 * h + 1) * w:(2 * h + 2) * w]
                        then(ve.tensor_scalar(e1, e1, rl[:, u["t"], h:h + 1], None, ALU.mult))
                        dst = Eb[:, i % 2, h * w:(h + 1) * w]
                        then(ve.scalar_tensor_tensor(dst, e0, rden[:, r, k:k + 1], e1, ALU.mult, ALU.subtract))
                    ve.memset(tiny2, 0.0).then_inc(s_dif, 1)

                for i in range(len(units) + 1):
                    if i < len(units):
                        logits(i)
                    if i >= 1 and units[i - 1]["kind"] == "diff":
                        difference(i - 1)

                for n in ends:
                    u = units[n]
                    r, t = row_of(u), u["t"]
                    ve.wait_ge(s_pv[blk], n + 1)
                    if u["kind"] == "diff":
                        then(ve.tensor_copy(mix[:, t, HALF:D], out_bank(u)[:, :]))
                        continue
                    if u["kind"] == "swa":
                        if t == 0:
                            ve.wait_ge(s_exp[blk], ends[1] + 1)
                            for q in range(T):
                                last = ve.tensor_tensor(esink[:, q, :], nm[:, q, :], sinks, ALU.add)
                            last.then_inc(s_sk, 1)
                            ve.wait_ge(s_ske, 1)
                        then(ve.tensor_tensor(den[:, r, :], den[:, r, :], esink[:, t, :], ALU.add))
                    then(ve.reciprocal(rden[:, r, :], den[:, r, :]))
                    last = ve.tensor_tensor(mix[:, t, 0:HALF].rearrange("p (h d) -> p h d", d=HD),
                                            out_bank(u)[:, :].rearrange("p (h d) -> p h d", d=HD),
                                            rden[:, r, :].unsqueeze(2).broadcast_to([P, 8, HD]), ALU.mult)
                    then(last)

            def post_norm(m, rows):
                ve.wait_ge(s_sq[m], 1)
                rooted(ve.scalar_tensor_tensor(ms[:, 0:2], sq[:, 0::2], EPS, sq[:, 1::2], ALU.add, ALU.add))
                for t in range(T):
                    for c in range(2):
                        last = ve.scalar_tensor_tensor(mix[:, t, c * HALF:(c + 1) * HALF], PS[4 + 2 * t + c][:, :],
                                                       rstd[:, t:t + 1], rows[:, c * HALF:(c + 1) * HALF],
                                                       ALU.mult, ALU.mult)
                then(last)
                for t in range(T):
                    last = ve.tensor_tensor(x[:, t, :], x[:, t, :], mix[:, t, :], ALU.add)
                then(last)

            ve.wait_ge(s_lamv, 64)
            for n in range(2):
                last = ve.tensor_tensor_reduce(mix[:, 1, n * HD:(n + 1) * HD], lamv[:, 2 * n, :], lamv[:, 2 * n + 1, :],
                                               1.0, 0.0, ALU.mult, ALU.add, lam2[:, n:n + 1])
            last.then_inc(s_lamx, 1)
            ve.wait_ge(s_vecT, 1)
            ve.tensor_copy(vec[:, 0:2, :], PS[7][:, 0:2 * P].rearrange("p (a b) -> p a b", a=2))
            then(ve.tensor_copy(vec[:, 2, 0:53], PS[7][:, 2 * P:2 * P + 53]))
            then(ve.tensor_scalar(subc, vec[:, 2, R_SUB:R_SUB + 1], 1.0 - LAMBDA_INIT, None, ALU.mult))
            ve.wait_ge(s_sink, 16)
            then(ve.tensor_scalar(negsink, sinks, -1.0, None, ALU.mult))
            ve.memset(rl, 0.0).then_inc(s_vec, 1)
            ve.wait_ge(s_x, 16)
            norm("attn1", x, hn, mix)
            ve.wait_ge(s_lame, 1)
            ve.tensor_scalar(lam, lam2[:, 0:1], lam2[:, 1:2], LAMBDA_INIT, ALU.subtract, ALU.add)
            scaled("attn1", lambda k: vec[:, 2, R_PRE + k:R_PRE + k + 1])
            dist = scratch[:, 4096:4352].bitcast(i32)
            masked = scratch[:, 4352:4608].bitcast(i32)
            four = scratch[:, 4608:4864]
            sixteen = scratch[:, 4864:5120]
            count = scratch[:, 5120:5376]
            term = scratch[:, 5376:5632]
            ve.wait_ge(s_qzero, 1)
            then(ve.tensor_scalar(dist, negdist[:, :], -1.0, None, ALU.mult))
            then(ve.tensor_scalar(masked, dist, 3, None, ALU.bitwise_and))
            then(ve.tensor_scalar(four, masked, 0.0, None, ALU.is_equal))
            then(ve.tensor_scalar(masked, dist, 15, None, ALU.bitwise_and))
            then(ve.tensor_scalar(sixteen, masked, 0.0, None, ALU.is_equal))
            then(ve.tensor_tensor(four, four, sixteen, ALU.add))
            then(ve.tensor_scalar(sixteen, negdist[:, :], -128.0, None, ALU.is_ge))
            then(ve.tensor_tensor(count, four, sixteen, ALU.add))
            then(ve.tensor_scalar(lncount[:, :], count, 2.0, math.log(2.0), ALU.is_ge, ALU.mult))
            then(ve.tensor_scalar(term, count, 3.0, math.log(3.0) - math.log(2.0), ALU.is_ge, ALU.mult))
            then(ve.tensor_tensor(lncount[:, :], lncount[:, :], term, ALU.add))
            then(ve.tensor_scalar(term, count, 1.0, NEG, ALU.is_lt, ALU.mult))
            then(ve.tensor_tensor(lncount[:, :], lncount[:, :], term, ALU.add))
            then(ve.tensor_scalar(term, negdist[:, :], 0.0, NEG, ALU.is_gt, ALU.mult))
            then(ve.tensor_tensor(lncount[:, :], lncount[:, :], term, ALU.add))

            take(0)
            ve.wait_ge(s_mask, 1)
            softmaxes(0)
            heads = lambda v, t: v[:, t, HALF:D].rearrange("p (h d) -> p h d", d=P)
            for t in range(T):
                mean_squares(mix[:, t, 0:HALF], hn[:, t, 0:HALF], 5 * t)
                last = ve.tensor_tensor(heads(hn, t), heads(mix, t), heads(mix, t), ALU.mult)
            then(last)
            for t in range(T):
                last = ve.tensor_reduce(ms[:, 5 * t + 1:5 * t + 5], heads(hn, t), X, ALU.add)
            then(last)
            for t in range(T):
                last = ve.tensor_scalar(ms[:, 5 * t + 1:5 * t + 5], ms[:, 5 * t + 1:5 * t + 5], 1.0 / P, EPS,
                                        ALU.mult, ALU.add)
            rooted(last)
            for t in range(T):
                ve.tensor_scalar(mix[:, t, 0:HALF], mix[:, t, 0:HALF], rstd[:, 5 * t:5 * t + 1], None, ALU.mult)
                ve.tensor_tensor(heads(mix, t), heads(mix, t),
                                 rstd[:, 5 * t + 1:5 * t + 5].unsqueeze(2).broadcast_to([P, 4, P]), ALU.mult)\
                    .then_inc(s_src["mix1"], 1)
            ve.wait_ge(s_src["mix1"], T)
            ve.memset(tiny2, 0.0).then_inc(s_att[0], 1)
            scaled("mix1", lambda k: vec[:, 2, R_SWA + k:R_SWA + k + 1] if k < 4 else subc)
            for h in range(DIL_H):
                last = ve.scalar_tensor_tensor(bias[:, h, :], negdist[:, :], float(np.float32(dil_slopes[h])),
                                               lncount[:, :], ALU.mult, ALU.add)
            then(last)
            ve.wait_ge(s_rows, 48)
            post_norm(0, post_attn)
            norm("ffn", x, hn, mix)
            scaled("ffn", lambda k: vec[:, 2, R_FPRE + k:R_FPRE + k + 1])

            def convolve(i, part):
                for b in range(2):
                    ve.wait_ge(s_tap, 4 * i + 2 * part + b + 1)
                    for back in (1, 2):
                        for f in range(2):
                            ft = KE * i + (FT // 2) * part + 2 * b + f
                            tap = vec[:, 0, ds(ft + FT * (2 - back), 1)]
                            c = conv[:, part, 2 * b + f, back:S]
                            n = 8 * i + 4 * part + 2 * b + f + 1
                            if back == 2:
                                ve.wait_ge(s_cv1, n)
                            last = ve.scalar_tensor_tensor(c, PS[2 * part + b][:, f * S:(f + 1) * S - back], tap, c,
                                                           ALU.mult, ALU.add)
                            if back == 1:
                                last.then_inc(s_cv1, 1)
                    last.then_inc(s_conv, 1)

            def gate(i, par):
                ve.wait_ge(s_conv, 4 * i + 4)
                ve.wait_ge(s_gelu, i + 1)
                ve.tensor_tensor(act[:, par, :, :], conv[:, 0, :, :], conv[:, 1, :, :], ALU.mult).then_inc(s_act, 1)

            def modulation(j, c):
                ve.wait_ge(s_adab[c % 2], 16 * (4 * j + c // 2 + 1))
                for k in range(KD):
                    for h in range(2):
                        dst = ada[:, ds((8 * j + c) * ADA_W + h * P, P)]
                        if k > 0:
                            ve.wait_ge(s_sum, 14 * (8 * j + c) + 2 * (k - 1) + h + 1)
                        last = ve.scalar_tensor_tensor(dst, ada_buf[c % 2][:, k, h * P:(h + 1) * P], siluc[:, k:k + 1],
                                                       dst, ALU.mult, ALU.add)
                        if k < KD - 1:
                            last.then_inc(s_sum, 1)
                last.then_inc(s_adau, 1)

            convolve(0, 0)
            convolve(0, 1)
            gate(0, 0)
            ve.wait_ge(s_ada0, 16)
            ve.wait_ge(s_c, 1)
            for _ in range(2):
                ve.nop().then_inc(s_adau, 1)
            with ve.Fori(0, (CHUNKS - 2) // 2) as j:
                for r in range(2):
                    i = 2 * j + 1 + r
                    convolve(i, 0)
                    modulation(j, 4 * r)
                    modulation(j, 4 * r + 1)
                    convolve(i, 1)
                    gate(i, (1 + r) % 2)
                    modulation(j, 4 * r + 2)
                    modulation(j, 4 * r + 3)
            convolve(CHUNKS - 1, 0)
            convolve(CHUNKS - 1, 1)
            gate(CHUNKS - 1, 1)
            post_norm(1, post_ffn)
            ve.memset(tiny2, 0.0).then_inc(s_modc, 1)
            norm("attn2", x, hn, mix)
            ve.wait_ge(s_mod, 1)
            ve.scalar_tensor_tensor(gmixc, modc[:, 1, :], 1.0, vec[:, 2, R_MIX:R_MIX + KD], ALU.add, ALU.mult)
            then(ve.scalar_tensor_tensor(gffnc, modc[:, 3, :], 1.0, vec[:, 2, R_FFN:R_FFN + KD], ALU.add, ALU.mult))
            ve.memset(tiny2, 0.0).then_inc(s_modc, 1)
            scaled("attn2", lambda k: gmixc[:, k:k + 1], lambda k: modc[:, 0, k:k + 1])
            take(1)
            softmaxes(1)

            ve.wait_ge(s_bias2, 1)
            for i in range(SB_H + 1):
                if i < SB_H:
                    zs = Lb[:, 1, 0:384]
                    r = mix[:, 0, HALF:HALF + 384]
                    ve.wait_ge(s_z, i + 1)
                    ve.tensor_scalar(zs, PS[i % 2][:, 0:384], SCALE, None, ALU.mult).then_inc(s_zm, 1)
                    ve.wait_ge(s_zm, i + 1)
                    ve.tensor_scalar(r, zs, 0.0, None, ALU.max)
                    dst = PT[:, i % 2, 0:384]
                    if i >= 2:
                        ve.wait_ge(s_sbo, i - 1)
                    then(ve.tensor_tensor(dst, zs, SB_ADD, ALU.add))
                    ve.wait_ge(s_sb1, i + 1)
                    then(ve.tensor_tensor(r, r, Lb[:, 0, 0:384], ALU.add))
                    if i >= 2:
                        ve.wait_ge(s_R, i - 1)
                    ve.tensor_tensor(Eb[:, i % 2, 0:384], r, SB_NEG, ALU.mult).then_inc(s_lk, 1)
                if i >= 1:
                    n = i - 1
                    ve.wait_ge(s_R, n + 1)
                    dst = PT[:, n % 2, 0:384]
                    ve.tensor_tensor(dst, PS[2 + n % 2][:, 0:384], dst, ALU.add).then_inc(s_t, 1)
            ve.wait_ge(s_sbo, SB_H)
            for t in range(T):
                last = ve.tensor_copy(mix[:, t, HALF:D], PS[6 + t][:, :])
            then(last)
            for t in range(T):
                for c in range(2):
                    last = mean_squares(mix[:, t, c * HALF:(c + 1) * HALF], hn[:, t, c * HALF:(c + 1) * HALF],
                                        2 * t + c)
            rooted(last)
            for t in range(T):
                for c in range(2):
                    last = ve.tensor_scalar(mix[:, t, c * HALF:(c + 1) * HALF], mix[:, t, c * HALF:(c + 1) * HALF],
                                            rstd[:, 2 * t + c:2 * t + c + 1], None, ALU.mult)
                last.then_inc(s_src["mix2"], 1)
            ve.wait_ge(s_src["mix2"], T)
            ve.memset(ranks[:, :, PASSES * NEXP:], -1.0).then_inc(s_att[1], 1)
            scaled("mix2", lambda k: vec[:, 2, R_DIL + k:R_DIL + k + 1])
            ve.wait_ge(s_proj[1], 4)
            ve.wait_ge(s_mod, 5)
            for t in range(T):
                for c in range(2):
                    last = ve.tensor_tensor(mix[:, t, c * HALF:(c + 1) * HALF], PS[4 + 2 * t + c][:, :],
                                            post_attn[:, c * HALF:(c + 1) * HALF], ALU.mult)
            then(last)
            for t in range(T):
                last = ve.tensor_tensor(x[:, t, :], x[:, t, :], mix[:, t, :], ALU.add)
            then(last)
            norm("moe", x, hn, mix)
            scaled("moe", lambda k: gffnc[:, k:k + 1], lambda k: modc[:, 2, k:k + 1])

            def over_t(v, n):
                return v.unsqueeze(1).broadcast_to([P, T, n])

            def over_n(v, n):
                return v.unsqueeze(2).broadcast_to([P, T, n])

            i4, i8, i32c = iota[:, 0:NGRP], iota[:, 0:EPG], iota[:, 0:NEXP]
            ve.wait_ge(s_lg, 1)
            then(ve.tensor_copy(lg, PS[4][:, 0:72].rearrange("p (t n) -> p t n", t=T)))
            then(ve.tensor_reduce(gmax, lg[:, :, 0:NGRP], X, ALU.max))
            ve.tensor_tensor(gsh, lg[:, :, 0:NGRP], over_n(gmax, NGRP), ALU.subtract).then_inc(s_r1, 1)
            ve.wait_ge(s_r1, 1)
            for n in (0, 2):
                ve.wait_ge(s_back, n + 1)
                ve.tensor_copy(hn[:, n // 2, 0:HALF], PS[n][:, :]).then_inc(s_h2, 1)
            then(ve.tensor_scalar(c4, gsh, 0.0, 64.0, ALU.is_lt, ALU.mult))
            then(ve.tensor_tensor(c4, c4, over_t(i4, NGRP), ALU.add))
            then(ve.tensor_reduce(gidx, c4, X, ALU.min))
            then(ve.tensor_tensor(ohg, over_t(i4, NGRP), over_n(gidx, NGRP), ALU.is_equal))
            ve.wait_ge(s_r2, 1)
            then(ve.tensor_reduce(gsum, gexp, X, ALU.add))
            then(ve.reciprocal(ggate, gsum))
            for t in range(T):
                last = ve.tensor_tensor(sel[:, t, :, :], lg[:, t, NGRP:].rearrange("p (g j) -> p g j", j=EPG),
                                        ohg[:, t, :].unsqueeze(2).broadcast_to([P, NGRP, EPG]), ALU.mult)
            then(last)
            for t in range(T):
                last = ve.tensor_reduce(el[:, t, :], sel[:, t, :, :].rearrange("p g j -> p j g"), X, ALU.add)
            then(last)
            then(ve.tensor_reduce(m1, el, X, ALU.max))
            then(ve.tensor_tensor(esh, el, over_n(m1, EPG), ALU.subtract))
            then(ve.tensor_scalar(c8, esh, 0.0, 64.0, ALU.is_lt, ALU.mult))
            then(ve.tensor_tensor(c8, c8, over_t(i8, EPG), ALU.add))
            then(ve.tensor_reduce(i1, c8, X, ALU.min))
            then(ve.tensor_tensor(oh1, over_t(i8, EPG), over_n(i1, EPG), ALU.is_equal))
            then(ve.scalar_tensor_tensor(el2, oh1, NEG, esh, ALU.mult, ALU.add))
            ve.tensor_reduce(m2, el2, X, ALU.max).then_inc(s_r1, 1)
            ve.wait_ge(s_r1, 2)
            then(ve.tensor_tensor(c8, el2, over_n(m2, EPG), ALU.is_lt))
            then(ve.scalar_tensor_tensor(c8, c8, 64.0, over_t(i8, EPG), ALU.mult, ALU.add))
            then(ve.tensor_reduce(i2, c8, X, ALU.min))
            then(ve.scalar_tensor_tensor(id1, gidx, float(EPG), i1, ALU.mult, ALU.add))
            then(ve.scalar_tensor_tensor(id2, gidx, float(EPG), i2, ALU.mult, ALU.add))
            then(ve.tensor_tensor(A1, over_t(i32c, NEXP), over_n(id1, NEXP), ALU.is_equal))
            then(ve.tensor_tensor(A2, over_t(i32c, NEXP), over_n(id2, NEXP), ALU.is_equal))
            ve.tensor_tensor(Aa, A1, A2, ALU.add).then_inc(s_A, 1)
            ve.wait_ge(s_r2, 2)
            then(ve.tensor_scalar(p1, ed, 1.0, None, ALU.add))
            then(ve.reciprocal(p1, p1))
            then(ve.tensor_tensor(p1, p1, ggate, ALU.mult))
            then(ve.tensor_tensor(p2, p1, ed, ALU.mult))
            then(ve.tensor_tensor(Wt, A1, over_n(p1, NEXP), ALU.mult))
            then(ve.tensor_tensor(Wt2, A2, over_n(p2, NEXP), ALU.mult))
            then(ve.tensor_tensor(Wt, Wt, Wt2, ALU.add))
            for q in range(PASSES):
                last = ve.tensor_copy(wsel[:, :, q * NEXP:(q + 1) * NEXP], Wt)
            then(last)
            ve.wait_ge(s_rank, 1)
            then(ve.scalar_tensor_tensor(rank1, PS[5][:, 0:2 * NEXP].rearrange("p (t n) -> p t n", t=T), 1.0, Aa,
                                         ALU.add, ALU.mult))
            for q in range(PASSES):
                last = ve.tensor_scalar(ranks[:, :, q * NEXP:(q + 1) * NEXP], rank1, -1.0 - SLOTS * q, None, ALU.add)
            then(last)
            then(ve.tensor_reduce(cmax, PS[5][:, 2 * NEXP:3 * NEXP], X, ALU.max))
            then(ve.tensor_scalar(over, cmax, float(SLOTS), float(PAIRS * (PASSES - 1)), ALU.is_gt, ALU.mult))
            ve.memset(combT, 0.0)
            ve.memset(ye, 0.0)
            then(ve.tensor_scalar(n_pairs_i[:, :], over, float(PAIRS), None, ALU.add))

            def pick(p):
                for e in range(2):
                    for t in range(T):
                        last = ve.tensor_scalar(oneh[:, t, e * SLOTS:(e + 1) * SLOTS], iota[:, :],
                                                ranks[:, t, ds(2 * p + e, 1)], None, ALU.is_equal)
                last.then_inc(s_oneh, 1)

            def tokens(p):
                ve.wait_ge(s_disp, p + 1)
                ve.tensor_copy(xeT[:, 4:8, :], PS[5][:, :].rearrange("p (a b) -> p a b", a=4)).then_inc(s_xeV, 1)

            def pair(p):
                ve.wait_ge(s_disp, p + 1)
                pick(p + 1)
                ve.wait_ge(s_ctr, p + 1)
                for e in range(2):
                    for t in range(T):
                        last = ve.tensor_scalar(onehw[:, t, e * SLOTS:(e + 1) * SLOTS], iota[:, :],
                                                ranks[:, t, ds(2 * p + e, 1)], wsel[:, t, ds(2 * p + e, 1)],
                                                ALU.is_equal, ALU.mult)
                last.then_inc(s_onehw, 1)
                ve.wait_ge(s_eu, p + 1)
                ve.wait_ge(s_silu, p + 1)
                ve.tensor_tensor(eact, eact, PS[7][:, :], ALU.mult).then_inc(s_eact, 1)
                tokens(p + 1)
                ve.wait_ge(s_ctr, p + 2)
                ve.wait_ge(s_comb, p + 1)
                ve.tensor_copy(combT, PS[7][:, 0:S].rearrange("p (t n) -> p t n", t=T)).then_inc(s_combT, 1)
                ve.wait_ge(s_edn, p + 1)
                ve.tensor_copy(ye[:, HALF:D], PS[5][:, :]).then_inc(s_yV, 1)

            for place_free in (s_eactT, s_combT, s_yA, s_yV, s_ctr, s_etr):
                ve.nop().then_inc(place_free, 1)
            pick(0)
            ve.wait_ge(s_oneh, 1)
            ve.wait_ge(s_h2, 4)
            ve.memset(tiny2, 0.0).then_inc(s_np, 1)
            tokens(0)
            with ve.Fori(0, PAIRS) as p:
                pair(p)
            n_pairs = ve.value_load(n_pairs_i[0:1, 0:1], min_val=PAIRS, max_val=PAIRS * PASSES)
            with ve.If(n_pairs > PAIRS):
                with ve.Fori(PAIRS, PAIRS * PASSES) as p:
                    pair(p)

            ve.wait_ge(s_comb, n_pairs + 1)
            for t in range(T):
                for c in range(2):
                    last = ve.tensor_tensor(mix[:, t, c * HALF:(c + 1) * HALF], PS[2 * t + c][:, :],
                                            post_ffn[:, c * HALF:(c + 1) * HALF], ALU.mult)
            then(last)
            for t in range(T):
                last = ve.tensor_tensor(x[:, t, :], x[:, t, :], mix[:, t, :], ALU.add)
            then(last)
            for t in range(T):
                last = mean_squares(x[:, t, :], mix[:, t, :], t)
            rooted(last)
            for t in range(T):
                ve.scalar_tensor_tensor(hn[:, t, :], x[:, t, :], rstd[:, t:t + 1], final_g[:, :], ALU.mult, ALU.mult)\
                    .then_inc(s_fin, 1)


_INS = ["x", "attn_pre_g", "w_in", "swa_sinks", "swa_out_g", "diff_lq1", "diff_lk1", "diff_lq2", "diff_lk2",
        "diff_subln_g", "w_out", "attn_post_g", "ffn_pre_g", "w_up", "conv_w", "conv_b", "w_down", "ffn_post_g",
        "c_2", "w_ada_2", "b_ada_2", "g_mix_2", "w_in_2", "g_dil_out_2", "g_sb_out_2", "w_out_2", "g_ffn_2",
        "w_group_2", "w_expert_2", "w_gate_2", "w_up_2", "w_down_2", "g_final_2"]


def kernel(**inputs):
    import concourse.bacc as bacc
    from concourse.bass_utils import run_bass_kernel_spmd

    nc = bacc.Bacc("TRN2", target_bir_lowering=False, num_devices=1)
    arrays, args = {}, {}
    for name in _INS:
        array = np.ascontiguousarray(inputs[name])
        arrays["in_" + name] = array
        args[name] = nc.dram_tensor("in_" + name, array.shape, mybir.dt.from_np(array.dtype),
                                    kind="ExternalInput").ap()
    out = nc.dram_tensor("out_0", inputs["x"].shape, mybir.dt.float32, kind="ExternalOutput").ap()
    two_block_kernel(nc, args, out)
    result = run_bass_kernel_spmd(nc, [arrays], core_ids=[0])
    return result.results[0]["out_0"]
```

```python
import math
from contextlib import ExitStack

import numpy as np

import concourse.bass as bass
from concourse import mybir


def alibi_slopes(n):
    def pow2(m):
        return [2.0 ** (-8.0 * (i + 1) / m) for i in range(m)]
    if math.log2(n).is_integer():
        return pow2(n)
    c = 2 ** int(math.floor(math.log2(n)))
    return sorted(pow2(c) + pow2(2 * c)[0::2][: n - c], reverse=True)


def two_block_kernel(nc, a, out):
    f32 = mybir.dt.float32
    f32r = mybir.dt.float32r
    bf16 = mybir.dt.bfloat16
    i32 = mybir.dt.int32
    ALU = mybir.AluOpType
    ACT = mybir.ActivationFunctionType
    X = mybir.AxisListType.X
    ds = bass.ds

    P = 128
    D = a["x"].shape[2]
    S = a["x"].shape[1]
    T = S // P
    KD = D // P
    HD = 64
    HALF = 512
    FF = a["w_down"].shape[1]
    FT = 2 * FF // P
    CHUNKS = FF // HALF
    NEXP = a["w_gate_2"].shape[1]
    FE = a["w_gate_2"].shape[3]
    KE = FE // P
    NGRP = a["w_group_2"].shape[2]
    EPG = NEXP // NGRP
    SLOTS = 64
    PAIRS = NEXP // 2
    PASSES = S // SLOTS
    ADA = a["w_ada_2"].shape[2]
    ADA_W = 256
    ADA_UNITS = ADA // (2 * ADA_W) * KD // 2
    ADA_EACH = ADA_UNITS // (CHUNKS - 2)
    EPS = 1e-6
    SCALE = HD ** -0.5
    NEG = -1e30
    LAMBDA_INIT = 0.8 - 0.6 * math.exp(-0.3 * 0)
    SWA_Q, SWA_KV, DIFF_H, DIL_H, SB_H, WINDOW = 8, 2, 4, 8, 8, 128
    slopes12 = alibi_slopes(SWA_Q + DIFF_H)
    swa_slopes, diff_slopes = slopes12[:SWA_Q], slopes12[SWA_Q:]
    dil_slopes = [2.0 ** (-8.0 * (i + 1) / DIL_H) for i in range(DIL_H)]

    LANES = 3
    SLOT_N = 2 * LANES
    SLOT_W = 4096
    N_IN = 0
    IN_CHUNKS = -(-a["w_in"].shape[2] // HALF)
    N_OUT = N_IN + IN_CHUNKS
    N_FFN = N_OUT + 2
    N_IN2 = N_FFN + 3 * CHUNKS
    IN2_CHUNKS = a["w_in_2"].shape[2] // HALF
    N_OUT2 = N_IN2 + IN2_CHUNKS
    N_MOE = N_OUT2 + 2

    def seq_gate(i):
        return N_FFN if i == 0 else N_FFN + 2 + 3 * (i - 1)

    def seq_down(i):
        return N_FFN + 2 + 3 * i + 2 if i < CHUNKS - 1 else N_FFN + 3 * CHUNKS - 1

    POOL_SHARE = [SLOT_W] * N_MOE
    POOL_SHARE[N_IN:N_IN + 3] = [SLOT_W // 2, 0, 0]
    POOL_SHARE[N_FFN + 1:N_IN2 + 3] = [2560] * (N_IN2 + 2 - N_FFN)

    ctx = ExitStack()
    with ctx:
        places = {}

        def sb(name, shape, dt=f32):
            tensor = ctx.enter_context(nc.sbuf_tensor(name, shape, dt))
            places[name] = nc.sbuf_base - int(np.prod(shape[1:])) * mybir.dt.size(dt)
            return tensor

        def rounded_view(name, shape):
            return nc.alloc_sbuf_tensor_at(name + "_r", shape, f32r, offset=places[name])

        def sem(name):
            return ctx.enter_context(nc.semaphore(name))

        ring = sb("ring", [P, SLOT_N, SLOT_W])
        x = sb("x_tok", [P, T, D])
        hn = sb("hn", [P, T, D])
        hT = sb("hT", [P, KD, S])
        mix = sb("mix", [P, T, D])
        scratch = sb("scratch", [P, 7168])
        kT = sb("kT", [P, 8, S])
        vt = sb("v_tok", [P, T, D])
        bias = sb("bias", [P, 12, S])
        post_attn = sb("post_attn", [P, D])
        post_ffn = sb("post_ffn", [P, D])
        final_g = sb("final_g", [P, D])
        vec = sb("vec", [P, 3, P])
        ident = sb("ident", [P, P])
        from_here = sb("from_here", [P, P])
        before = sb("before", [P, P])
        ones = sb("ones", [P, P])
        negdist = sb("negdist", [P, S])
        lncount = sb("lncount", [P, S])
        iota = sb("iota", [P, SLOTS])
        zrow = sb("zrow", [P, HALF], bf16)
        small = sb("small", [P, 400])
        n_pairs_i = sb("n_pairs_i", [P, 1], i32)

        place = [0]

        def cell(*shape):
            n = int(np.prod(shape))
            v = small[:, place[0]:place[0] + n]
            place[0] += n
            if len(shape) == 2:
                v = v.rearrange("p (a b) -> p a b", a=shape[0])
            return v

        ms = cell(10)
        rstd = cell(10)
        minus_half = cell(10)
        ROOTS = [(t, 1) for t in range(T)]
        ROOTS += [(5 * t, 5) for t in range(T)]
        ROOTS += [(0, 1), (1, 1)] * (2 * T)
        ROOTS += [(2 * t, 2) for t in range(T)]
        ROOTS += [(t, 1) for t in range(T)] * 2
        tiny = cell(1)
        sq = cell(4)
        nm = cell(2 * T, 8)
        den = cell(2 * T, 8)
        rden = cell(2 * T, 8)
        sinks = cell(8)
        negsink = cell(8)
        esink = cell(T, 8)
        lamv = vt[:, 0, 0:256].rearrange("p (a b) -> p a b", a=4)
        lam2 = cell(2)
        lam = cell(1)
        rl = cell(T, 4)
        modc = cell(4, KD)
        gmixc = cell(KD)
        gffnc = cell(KD)
        siluc = cell(KD)
        subc = cell(1)

        qz = scratch[:, 0:4096].rearrange("p (h s) -> p h s", s=S)
        Lb = scratch[:, 4096:5120].rearrange("p (r n) -> p r n", r=2)
        Eb = scratch[:, 5120:6144].rearrange("p (r n) -> p r n", r=2)
        PT = scratch[:, 6144:7168].rearrange("p (r n) -> p r n", r=2)
        ada = scratch[:, 0:ADA]
        ada_buf = kT[:, :, :].rearrange("p (b k n) s -> p b k (n s)", b=2, k=2)
        conv = mix[:, :, :].rearrange("p c (f s) -> p c f s", s=S)
        hi_T = rounded_view("hT", [P, KD, S])
        lo_T = {"attn1": rounded_view("hn", [P, KD, S]), "mix1": rounded_view("kT", [P, KD, S]),
                "ffn": rounded_view("v_tok", [P, KD, S]), "mix2": rounded_view("bias", [P, KD, S])}
        lo_T["attn2"] = lo_T["attn1"]
        act_r = lo_T["attn1"][:, :, :].rearrange("p (c f) s -> p c f s", c=2)
        ring_r = rounded_view("ring", [P, SLOT_N, SLOT_W])
        shifted = hn[:, :, :].rearrange("p t (k s) -> p (t k) s", s=S)
        junk = final_g[:, :]
        rows2 = kT[:, :, :].rearrange("p (t k) s -> p t (k s)", t=T)
        off = [0]

        def piece(*shape):
            n = int(np.prod(shape))
            v = scratch[:, off[0]:off[0] + n]
            off[0] += n
            if len(shape) == 2:
                return v.rearrange("p (a b) -> p a b", a=shape[0])
            if len(shape) == 3:
                return v.rearrange("p (a b c) -> p a b c", a=shape[0], b=shape[1])
            return v

        oneh = piece(T, P)
        onehw = piece(T, P)
        xeT = piece(KD, P)
        eact = piece(HALF)
        eactT = piece(KE, P)
        combT = piece(T, P)
        ye = piece(D)
        lg = piece(T, NGRP + NEXP)
        sel = piece(T, NGRP, EPG)
        el, esh, el2, c8, oh1 = (piece(T, EPG) for _ in range(5))
        gsh, gexp, c4, ohg = (piece(T, NGRP) for _ in range(4))
        gmax, gsum, ggate, gidx, m1, i1, m2, i2, ed, p1, p2, id1, id2 = (piece(T) for _ in range(13))
        A1, A2, Aa, Wt, Wt2 = (piece(T, NEXP) for _ in range(5))
        rank1 = piece(T, NEXP)
        ranks = piece(T, PASSES * NEXP + 2)
        wsel = piece(T, PASSES * NEXP)
        wr = piece(KD, NGRP + NEXP)
        cmax, over = piece(1), piece(1)
        SB_ADD = bias[:, 8:10, :].rearrange("p a s -> p (a s)")[:, 0:384]
        SB_NEG = bias[:, 10:12, :].rearrange("p a s -> p (a s)")[:, 0:384]
        stage = kT[:, 0:2, :].rearrange("p k s -> p (k s)")[:, 0:384].rearrange("p (a b) -> p a b", a=3)

        PS = [ctx.enter_context(nc.psum_tensor(f"bank{i}", [P, HALF], f32)) for i in range(8)]

        def v_c(k): return vec[:, 2, k:k + 1]
        R_C, R_PRE, R_FPRE, R_MIX, R_FFN, R_SWA, R_DIL, R_SB, R_SUB = 0, 8, 16, 24, 32, 40, 44, 48, 52

        loaded = [sem(f"loaded{i}") for i in range(SLOT_N)]
        s_x = [sem(f"s_x{t}") for t in range(T)]
        s_stage = sem("s_stage")
        s_rows = sem("s_rows")
        s_sink = sem("s_sink")
        s_lamv = sem("s_lamv")
        s_const = sem("s_const")
        s_mask = sem("s_mask")
        s_qzero = sem("s_qzero")
        s_pool = sem("s_pool")
        s_vecT = sem("s_vecT")
        s_vec = sem("s_vec")
        s_lamx = sem("s_lamx")
        s_lame = sem("s_lame")
        s_c = sem("s_c")
        s_ms = sem("s_ms")
        s_rs = sem("s_rs")
        s_link = sem("s_link")
        s_alink = sem("s_alink")
        s_whi = sem("s_whi")
        s_wloP = sem("s_wloP")
        s_wloV = sem("s_wloV")
        s_hhi = {t: sem("s_hhi_" + t) for t in ("attn1", "mix1", "ffn", "attn2", "mix2")}
        s_shift = sem("s_shift")
        s_prod = sem("s_prod")
        s_ahi = sem("s_ahi")
        TURNS = ["attn1", "mix1", "ffn", "attn2", "mix2", "moe"]
        s_src = {t: sem("s_src_" + t) for t in TURNS}
        s_turn = {t: sem("s_turn_" + t) for t in TURNS}
        s_hT = {t: sem("s_hT_" + t) for t in TURNS}
        s_gemm = [sem("s_gemm1"), sem("s_gemm2")]
        s_evA = [sem("s_evA1"), sem("s_evA2")]
        s_evV = [sem("s_evV1"), sem("s_evV2")]
        s_sc = [sem("s_sc1"), sem("s_sc2")]
        s_log = [sem("s_log1"), sem("s_log2")]
        s_max = [sem("s_max1"), sem("s_max2")]
        s_exp = [sem("s_exp1"), sem("s_exp2")]
        s_dif = sem("s_dif")
        s_tr = [sem("s_tr1"), sem("s_tr2")]
        s_pt = [sem("s_pt1"), sem("s_pt2")]
        s_pv = [sem("s_pv1"), sem("s_pv2")]
        s_sk = sem("s_sk")
        s_ske = sem("s_ske")
        s_done = [sem("s_done1"), sem("s_done2")]
        s_mixed = sem("s_mixed")
        s_proj = [sem("s_proj1"), sem("s_proj2")]
        s_sq = [sem("s_sq1"), sem("s_sq2"), sem("s_sq3")]
        s_up = sem("s_up")
        s_tap = sem("s_tap")
        s_cv1 = sem("s_cv1")
        s_conv = sem("s_conv")
        s_sum = sem("s_sum")
        s_gelu = sem("s_gelu")
        s_act = sem("s_act")
        s_down = sem("s_down")
        s_down0 = sem("s_down0")
        s_rfree = sem("s_rfree")
        s_adab = [sem("s_adab0"), sem("s_adab1")]
        s_ada0 = sem("s_ada0")
        s_adam = sem("s_adam")
        s_mod = sem("s_mod")
        s_modc = sem("s_modc")
        s_bias2 = sem("s_bias2")
        s_z = sem("s_z")
        s_zm = sem("s_zm")
        s_sb1 = sem("s_sb1")
        s_sb2 = sem("s_sb2")
        s_lk = sem("s_lk")
        s_R = sem("s_R")
        s_t = sem("s_t")
        s_w = sem("s_w")
        s_sbo = sem("s_sbo")
        s_wr = sem("s_wr")
        s_back = sem("s_back")
        s_h2 = sem("s_h2")
        s_lg = sem("s_lg")
        s_r1 = sem("s_r1")
        s_r2 = sem("s_r2")
        s_A = sem("s_A")
        s_rank = sem("s_rank")
        s_np = sem("s_np")
        s_oneh = sem("s_oneh")
        s_onehw = sem("s_onehw")
        s_disp = sem("s_disp")
        s_xeA = sem("s_xeA")
        s_xeV = sem("s_xeV")
        s_eg = sem("s_eg")
        s_eu = sem("s_eu")
        s_silu = sem("s_silu")
        s_eact = sem("s_eact")
        s_etr = sem("s_etr")
        s_eactT = sem("s_eactT")
        s_ctr = sem("s_ctr")
        s_combT = sem("s_combT")
        s_edn = sem("s_edn")
        s_yA = sem("s_yA")
        s_yV = sem("s_yV")
        s_comb = sem("s_comb")
        s_comb0 = sem("s_comb0")
        s_fin = sem("s_fin")
        s_out = [sem(f"s_out{t}") for t in range(T)]

        def chunk_view(slot):
            return ring[:, slot, :].rearrange("p (k n) -> p k n", n=HALF)

        def split_view(lane, n=HALF):
            return [ring_r[:, place, :].rearrange("p (k n) -> p k n", n=n) for place in (LANES + lane, lane)]

        def split_part(n, part):
            lane = n % LANES

            def view(tensor, place):
                if n == N_IN + IN_CHUNKS - 1:
                    tiles = tensor[:, place, :].rearrange("p (k n) -> p k n", n=HALF)
                    return tiles[:, part * KD // 2:(part + 1) * KD // 2, 0:S]
                cut = POOL_SHARE[n] if 0 < POOL_SHARE[n] < SLOT_W else SLOT_W // 2
                a0, a1 = ((0, cut), (cut, SLOT_W))[part]
                return tensor[:, place, a0:a1]

            return view(ring, lane), view(ring_r, LANES + lane), view(ring_r, lane)

        def parts_of(n):
            cut = 0 if POOL_SHARE[n] == 0 else 2 if POOL_SHARE[n] == SLOT_W else 1
            return (0, 1)[:cut], (0, 1)[cut:]

        def split_by(engine, n):
            return sum(len(parts_of(m)[engine]) > 0 for m in range(n + 1))

        QB0 = SWA_Q * HD + 2 * SWA_KV * HD
        KB0 = QB0 + DIFF_H * P
        items1 = [(0, "q", ("pair", j * P, 2 * j)) for j in range(4)]
        items1 += [(1, "ka", (0, 0)), (1, "v", (P, P, 0))]
        for pair_of in range(2):
            for h in (2 * pair_of, 2 * pair_of + 1):
                items1.append(((QB0 + h * P) // HALF, "q", ("pair", (QB0 + h * P) % HALF, 8 + 2 * h)))
                items1.append(((KB0 + h * P) // HALF, "k", ((KB0 + h * P) % HALF, 1 + h)))
            items1.append((3 + pair_of, "v", (S * (1 - pair_of), S, P + S * pair_of)))
        items2 = []
        for part in range(2):
            mine = 1 - part
            items2 += [(3 * part, "q", ("pair", j * P, 8 * mine + 2 * j)) for j in range(4)]
            items2 += [(3 * part + 1, "k", (j * P, 4 * mine + j)) for j in range(4)]
            items2 += [(3 * part + 2, "vt", (t, HALF * mine)) for t in range(T)]
        ITEMS = [items1, items2]
        AHEAD = [6, 10]

        def item_bank(blk, n):
            return PS[(4 + n) % 8] if n < AHEAD[blk] else PS[6 + n % 2]

        def item_waits(blk, n):
            return n - 8 if n < AHEAD[blk] else n - 2 if n >= AHEAD[blk] + 2 else None

        BETWEEN = [{0: [6], 1: [7], 2: [8], 3: [9], 4: [10], 5: [11], 6: [12, 13], 7: [14], 8: [15]},
                   {0: [10, 11], 1: [12], 2: [13], 3: [14], 4: [15, 16], 5: [17], 6: [18], 7: [19]}]

        SPLITS = [{1: [N_IN + 3], 4: [N_IN + 4], 8: [N_OUT], 9: [N_OUT + 1], 10: [N_FFN]},
                  {1: [N_IN2 + 4], 3: [N_IN2 + 5], 6: [N_OUT2], 7: [N_OUT2 + 1]}]

        def consumed(n):
            if n < N_OUT:
                return s_gemm[0], 1 + max(m for m, it in enumerate(items1) if it[0] <= n - N_IN)
            if n < N_FFN:
                return s_proj[0], 2 * (T - 1) + n - N_OUT + 1
            if n < N_IN2:
                for i in range(CHUNKS):
                    if n in (seq_gate(i), seq_gate(i) + 1):
                        return s_up, 4 * i + 2 * (n - seq_gate(i) + 1)
                    if n == seq_down(i):
                        return s_down, i + 1
            if n < N_OUT2:
                return s_gemm[1], 1 + max(m for m, it in enumerate(items2) if it[0] <= n - N_IN2)
            return s_proj[1], 2 * (T - 1) + n - N_OUT2 + 1

        def expert_slot(c, e):
            return c + LANES * e

        def expert_loads(c, e):
            return 0 if e else N_MOE // LANES

        KA = (0, 5)

        def unit(kind, t, maps):
            return dict(kind=kind, t=t, maps=maps, w=P * (t + 1))
        swa_unit = lambda h: dict(q=h, k=KA[h // 4], b=h, v=(h // 4) * HD, vw=HD, o=h * HD, h=h)
        diff_unit = lambda h, m: dict(q=8 + 2 * h + m, k=1 + h, b=8 + h, v=128 + h * 128, vw=128, o=h * 128, h=h)
        dil_unit = lambda h: dict(q=h, k=h // 2, b=h, v=h * HD, vw=HD, o=h * HD, h=h)
        units1 = [unit("swa", 0, [swa_unit(h) for h in range(4 * u, 4 * u + 4)]) for u in range(2)]
        units1 += [unit("swa", 1, [swa_unit(2 * u), swa_unit(2 * u + 1)]) for u in range(4)]
        for u in range(2):
            units1.append(unit("diff", 0, [diff_unit(2 * u + i // 2, i % 2) for i in range(4)]))
            units1 += [unit("diff", 1, [diff_unit(h, 0), diff_unit(h, 1)]) for h in (2 * u, 2 * u + 1)]
        units2 = [unit("dil", 0, [dil_unit(h) for h in range(4 * u, 4 * u + 4)]) for u in range(2)]
        units2 += [unit("dil", 1, [dil_unit(2 * u), dil_unit(2 * u + 1)]) for u in range(4)]
        UNITS = [units1, units2]

        def row_of(u):
            return (2 if u["kind"] == "diff" else 0) + u["t"]

        def col_of(u):
            m = u["maps"][0]
            return (4 * (m["h"] // 2) if u["t"] == 0 else 2 * m["h"]) if u["kind"] == "diff" else m["h"]

        def out_bank(u):
            return PS[(6 if u["kind"] == "dil" else 4) + u["t"]]

        def needs(blk, i):
            return AHEAD[0] + (5 * ((i - 3) // 3) if i >= 6 else 0) if blk == 0 else len(items2)

        def turned(u):
            maps = u["maps"][0::2] if u["kind"] == "diff" else u["maps"]
            return [(i * u["w"] + kb * P, kb, m) for i, m in enumerate(maps) for kb in range(u["t"] + 1)]

        def finishes(blk):
            last = {}
            for n, u in enumerate(UNITS[blk]):
                last[(u["kind"], u["t"])] = n
            return last

        def taken(blk, kind, where, bank):
            if kind == "q":
                return [(qz[HD * g:HD * g + HD, where[2] + g, :], bank[HD * g:HD * g + HD, 0:S]) for g in range(2)]
            if kind == "ka":
                return [(kT[HD * half:HD * half + HD, KA[g], :], bank[HD * g:HD * g + HD, 0:S])
                        for g in range(2) for half in range(2)]
            if kind == "k":
                return [(kT[:, where[1], :], bank[:, 0:S])]
            if kind == "v":
                _, cw, c0 = where
                return [(vt[:, :, c0:c0 + cw], bank[:, 0:T * cw].rearrange("p (t n) -> p t n", t=T))]
            t, c0 = where
            return [(vt[:, t, c0:c0 + HALF], bank[:, :])]

        block = ctx.enter_context(nc.Block())

        @block.sync
        def _(sp):
            w_in = a["w_in"].rearrange("o (k p) n -> p (o k) n", p=P)
            w_ada = a["w_ada_2"].rearrange("o (k p) n -> p (o k) n", p=P)
            w_out = a["w_out"].rearrange("o (k p) n -> p (o k) n", p=P)
            w_up = a["w_up"].rearrange("o (k p) n -> p (o k) n", p=P)
            w_down = a["w_down"].rearrange("o (k p) n -> p (o k) n", p=P)
            w_in2 = a["w_in_2"].rearrange("o (k p) n -> p (o k) n", p=P)
            w_out2 = a["w_out_2"].rearrange("o (k p) n -> p (o k) n", p=P)
            w_gate = a["w_gate_2"].rearrange("o e (k p) n -> p (o e) k n", p=P)
            w_eup = a["w_up_2"].rearrange("o e (k p) n -> p (o e) k n", p=P)
            w_edown = a["w_down_2"].rearrange("o e (k p) n -> p (o e) k n", p=P)

            def load(slot, src, free):
                if free is not None:
                    sp.wait_ge(*free)
                dst = ring[:, slot, :].rearrange("p (k n) -> p k n", k=src.shape[1])
                if src.shape[2] < dst.shape[2]:
                    dst = dst[:, :, 0:src.shape[2]]
                sp.dma_start(dst, src).then_inc(loaded[slot], 16)

            def straight(n, src):
                load(n % LANES, src, consumed(n - LANES) if n >= LANES else None)

            xr = a["x"].rearrange("o (t p) d -> p (o t) d", p=P)
            for t in range(T):
                sp.dma_start(x[:, t, :], xr[:, t, :]).then_inc(s_x[t], 16)
            for c in range(IN_CHUNKS):
                if c == 1:
                    sp.wait_ge(s_stage, 16 * 12)
                    sp.wait_ge(s_lamv, 16 * 4)
                    sp.wait_ge(s_sink, 16)
                straight(N_IN + c, w_in[:, :, c * HALF:min((c + 1) * HALF, w_in.shape[2])])
            for c in range(2):
                straight(N_OUT + c, w_out[:, :, c * HALF:(c + 1) * HALF])
            for c in range(2):
                straight(N_FFN + c, w_up[:, :, c * FF:c * FF + HALF])

            def ffn_chunks(i):
                return (w_up[:, :, ds(i * HALF, HALF)], w_up[:, :, ds(FF + i * HALF, HALF)],
                        w_down[:, ds((i - 1) * KE, KE), :])

            def modulation(r, *units):
                for c in units:
                    sp.wait_ge(s_sum, 4 * (ADA_EACH * r + c) + 4)
                    sp.dma_start(ada_buf[:, c % 2, :, :],
                                 w_ada[:, 2 * (c % 4):2 * (c % 4) + 2, ds(1024 * r + 2 * ADA_W * (c // 4), 2 * ADA_W)])\
                        .then_inc(s_adab[c % 2], 16)

            for c, src in enumerate(ffn_chunks(1)):
                straight(seq_gate(1) + c, src)
            modulation(0, 0, 1, 2, 3)
            due = ((4, 5), (6, 7), (0, 1, 2, 3))
            with sp.Fori(2, CHUNKS - 1) as i:
                for c, (src, free) in enumerate(zip(ffn_chunks(i), ((s_up, 4 * (i - 1) + 2), (s_up, 4 * (i - 1) + 4),
                                                                    (s_down, i - 1)))):
                    load((seq_gate(1) + c) % LANES, src, free)
                    modulation(i - 2 if c < 2 else i - 1, *due[c])
            for c, src in enumerate(ffn_chunks(CHUNKS - 1)):
                straight(seq_gate(CHUNKS - 1) + c, src)
                if c < 2:
                    modulation(CHUNKS - 3, *due[c])
            straight(seq_down(CHUNKS - 1), w_down[:, (CHUNKS - 1) * KE:CHUNKS * KE, :])
            for c in range(IN2_CHUNKS):
                first = (c + IN2_CHUNKS // 2) % IN2_CHUNKS * HALF
                straight(N_IN2 + c, w_in2[:, :, first:first + HALF])
            for c in range(2):
                straight(N_OUT2 + c, w_out2[:, :, c * HALF:(c + 1) * HALF])

            def expert_pair(p, q):
                for c, (w, done) in enumerate(((w_gate, s_eg), (w_eup, s_eu), (w_edown, s_edn))):
                    for e in range(2):
                        src = w[:, ds(2 * q + e, 1), :, :].rearrange("p o k n -> p (o k) n")
                        free = consumed(N_MOE - LANES + c) if isinstance(p, int) else (done, p)
                        load(expert_slot(c, e), src, free)

            expert_pair(0, 0)
            with sp.Fori(1, PAIRS) as p:
                expert_pair(p, p)
            sp.wait_ge(s_np, 1)
            n_pairs = sp.value_load(n_pairs_i[0:1, 0:1], min_val=PAIRS, max_val=PAIRS * PASSES)
            with sp.If(n_pairs > PAIRS):
                with sp.Fori(1, PASSES) as r:
                    with sp.Fori(0, PAIRS) as q:
                        expert_pair(r * PAIRS + q, q)
            rows = out.rearrange("o (t p) d -> p (o t) d", p=P)
            for t in range(T):
                sp.wait_ge(s_fin, t + 1)
                sp.dma_start(rows[:, t, :], hn[:, t, :]).then_inc(s_out[t], 16)
            for t in range(T):
                sp.wait_ge(s_out[t], 16)

        @block.gpsimd
        def _(pool):
            step = [0]
            norms = [0]

            def inverse_roots(count):
                for _ in range(count):
                    first, w = ROOTS[norms[0]]
                    norms[0] += 1
                    pool.wait_ge(s_ms, norms[0])
                    pool.tensor_tensor(rstd[:, first:first + w], ms[:, first:first + w], minus_half[:, 0:w],
                                       ALU.pow).then_inc(s_rs, 1)

            def then(ins):
                step[0] += 1
                ins.then_inc(s_pool, 1)
                pool.wait_ge(s_pool, step[0])

            def split(n, more=0):
                for part in parts_of(n)[0]:
                    pool.wait_ge(s_whi, 2 * n + 1 + part + 2 * more)
                    raw, hi, lo = split_part(n, part)
                    last = pool.tensor_tensor(lo, raw, hi, ALU.subtract)
                last.then_inc(s_wloP, 1)

            pool.memset(minus_half, -0.5)
            then(pool.memset(ident[:, :], 0.0))
            pool.affine_select(out=ident[:, :], in_=ident[:, :], compare_op=ALU.not_equal, fill=1.0, base=0,
                               pattern=[[-1, P]], channel_multiplier=1).then_inc(s_const, 1)
            pool.memset(ones[:, :], 1.0).then_inc(s_const, 1)
            pool.memset(zrow[:, :], 0.0).then_inc(s_const, 1)
            inverse_roots(T)
            pool.memset(qz[:, :, :], 0.0).then_inc(s_qzero, 1)
            split(N_IN)
            then(pool.memset(from_here[:, :], 1.0))
            pool.affine_select(out=from_here[:, :], in_=from_here[:, :], compare_op=ALU.is_ge, fill=0.0, base=0,
                               pattern=[[-1, P]], channel_multiplier=1).then_inc(s_const, 1)
            then(pool.memset(before[:, :], 1.0))
            pool.affine_select(out=before[:, :], in_=before[:, :], compare_op=ALU.is_gt, fill=0.0, base=0,
                               pattern=[[1, P]], channel_multiplier=-1).then_inc(s_const, 1)
            pool.iota(iota[:, :], [[1, SLOTS]], base=0, channel_multiplier=0,
                      allow_small_or_imprecise_dtypes=True).then_inc(s_const, 1)
            then(pool.iota(negdist[:, :], [[1, S]], base=-P, channel_multiplier=-1,
                           allow_small_or_imprecise_dtypes=True))
            for h in range(SWA_Q):
                pool.tensor_scalar(bias[:, h, :], negdist[:, :], float(np.float32(swa_slopes[h])), None, ALU.mult)
            for h in range(DIFF_H):
                last = pool.tensor_scalar(bias[:, SWA_Q + h, :], negdist[:, :], float(np.float32(diff_slopes[h])),
                                          None, ALU.mult)
            then(last)
            then(pool.affine_select(out=bias[:, :, :], in_=bias[:, :, :], compare_op=ALU.is_ge, fill=NEG, base=P,
                                    pattern=[[0, 12], [-1, S]], channel_multiplier=1))
            pool.affine_select(out=bias[:, 0:SWA_Q, :], in_=bias[:, 0:SWA_Q, :], compare_op=ALU.is_ge, fill=NEG,
                               base=WINDOW - 1 - P, pattern=[[0, SWA_Q], [1, S]],
                               channel_multiplier=-1).then_inc(s_mask, 1)
            pool.dma_start(post_attn[:, :], a["attn_post_g"][0].partition_broadcast(P)).then_inc(s_rows, 16)
            pool.dma_start(post_ffn[:, :], a["ffn_post_g"][0].partition_broadcast(P)).then_inc(s_rows, 16)
            for n in range(N_IN + 3, N_FFN + 1):
                split(n)
            inverse_roots(T)
            pool.wait_ge(s_src["mix1"], T)
            then(pool.memset(ada, 0.0))
            pool.dma_start(ada[0:1, :], a["b_ada_2"]).then_inc(s_ada0, 16)
            then(pool.memset(SB_ADD, 0.0))
            then(pool.memset(SB_NEG, -1.0))
            for m, fill in ((SB_ADD, NEG), (SB_NEG, 0.0)):
                for c in (0, 256):
                    then(pool.affine_select(out=m[:, c:c + P], in_=m[:, c:c + P], compare_op=ALU.is_gt, fill=fill,
                                            base=0, pattern=[[1, P]], channel_multiplier=-1))
            pool.memset(tiny, 0.0).then_inc(s_bias2, 1)
            inverse_roots(2 * T)

            split(seq_gate(0) + 1)
            split(seq_gate(1))
            split(seq_gate(1) + 1)
            with pool.Fori(1, CHUNKS - 1) as i:
                split(seq_gate(1) + 2, 3 * (i - 1))
                split(seq_gate(2), 3 * (i - 1))
                split(seq_gate(2) + 1, 3 * (i - 1))
            for n in range(seq_gate(CHUNKS - 1) + 2, N_IN2 + 1):
                split(n)
            pool.wait_ge(s_adam, 5)
            pool.memset(qz[:, :, :], 0.0).then_inc(s_qzero, 1)
            inverse_roots(2 * T)
            for n in range(N_IN2 + 1, N_MOE):
                split(n)
            inverse_roots(T)
            pool.wait_ge(s_mixed, 1)
            pool.dma_start(wr[:, :, 0:NGRP], a["w_group_2"].rearrange("o (k p) n -> p (o k) n", p=P),
                           allow_slow_non_contiguous=True).then_inc(s_wr, 16)
            pool.dma_start(wr[:, :, NGRP:NGRP + NEXP], a["w_expert_2"].rearrange("o (k p) n -> p (o k) n", p=P),
                           allow_slow_non_contiguous=True).then_inc(s_wr, 16)
            pool.wait_ge(s_mixed, 1)
            pool.dma_start(final_g[:, :], a["g_final_2"].partition_broadcast(P)).then_inc(s_rows, 16)
            inverse_roots(2 * T)

        @block.tensor
        def _(pe):
            def arrived(n):
                pe.wait_ge(loaded[n % SLOT_N], 16 * (n // SLOT_N + 1))

            def turn(tag, src):
                for t in range(T):
                    pe.wait_ge(s_src[tag], t + 1)
                    for k in range(KD):
                        c = (k % 2) * S + t * P
                        last = pe.transpose(PS[k // 2][:, c:c + P], src[:, t, k * P:(k + 1) * P], ident[:, :])
                        if k % 2 and t == T - 1:
                            last.then_inc(s_turn[tag], 1)

            def split_ready(n, more=0):
                for engine, done in enumerate((s_wloP, s_wloV)):
                    if parts_of(n)[engine]:
                        pe.wait_ge(done, split_by(engine, n) + more)

            def product(dst, lhs, rhs, start, stop, **flags):
                pe.matmul(dst, lhs[0], rhs[0], start=start, stop=False, **flags)
                pe.matmul(dst, lhs[0], rhs[1], start=False, stop=False, **flags)
                return pe.matmul(dst, lhs[1], rhs[0], start=False, stop=stop, **flags)

            def tiles(tag, k, n0=0, n=S):
                return [hi_T[:, k, n0:n0 + n], lo_T[tag][:, k, n0:n0 + n]]

            def both(w, k, c0, n):
                return [v[:, k, c0:c0 + n] for v in w]

            def piece_taken(blk, n):
                pe.wait_ge(s_evA[blk], (n + 1) // 2)
                pe.wait_ge(s_evV[blk], n // 2)

            def project(blk, n_base, n):
                items = ITEMS[blk]
                c, kind, where = items[n]
                tag = ("attn1", "attn2")[blk]
                split_ready(n_base + c)
                bank = item_bank(blk, n)
                w = split_view((n_base + c) % LANES)
                m = item_waits(blk, n)
                if m is not None and m >= 0:
                    pe.wait_ge((s_evA, s_evV)[m % 2][blk], m // 2 + 1)
                for k in range(KD):
                    if n == 0:
                        pe.wait_ge(s_hT[tag], k + 1)
                    flags = dict(start=(k == 0), stop=(k == KD - 1))
                    if kind in ("q", "k", "ka"):
                        c0 = where[1] if kind == "q" else where[0]
                        last = product(bank[:, 0:S], both(w, k, c0, P), tiles(tag, k), **flags)
                    elif kind == "vt":
                        last = product(bank[:, :], tiles(tag, k, where[0] * P, P), both(w, k, 0, HALF), **flags)
                if kind == "v":
                    c0, cw, _ = where
                    for t in range(T):
                        for k in range(KD):
                            last = product(bank[:, t * cw:(t + 1) * cw], tiles(tag, k, t * P, P), both(w, k, c0, cw),
                                           start=(k == 0), stop=(k == KD - 1))
                last.then_inc(s_gemm[blk], 1)

            def attention(blk, n_base, fill):
                units = UNITS[blk]
                for i in range(len(units) + 2):
                    if i < len(units):
                        u = units[i]
                        if i == 0 or needs(blk, i) > needs(blk, i - 1):
                            piece_taken(blk, needs(blk, i))
                        if i >= 2:
                            pe.wait_ge(s_log[blk], i - 1)
                        for j, m in enumerate(u["maps"]):
                            last = pe.matmul(PS[i % 2][:, j * u["w"]:(j + 1) * u["w"]],
                                             qz[:, m["q"], u["t"] * P:(u["t"] + 1) * P], kT[:, m["k"], 0:u["w"]],
                                             start=True, stop=True)
                        last.then_inc(s_sc[blk], 1)
                    if 1 <= i <= len(units):
                        n = i - 1
                        u = units[n]
                        if u["kind"] == "diff":
                            pe.wait_ge(s_dif, n - len(units) // 2 + 1)
                        else:
                            pe.wait_ge(s_exp[blk], n + 1)
                        if n >= 2:
                            pe.wait_ge(s_pt[blk], n - 1)
                        for b, (c, kb, m) in enumerate(turned(u)):
                            last = pe.transpose(PS[2 + n % 2][:, b * P:(b + 1) * P], Eb[:, n % 2, c:c + P],
                                                ident[:, :])
                        last.then_inc(s_tr[blk], 1)
                    if i >= 2:
                        n = i - 2
                        u = units[n]
                        pe.wait_ge(s_pt[blk], n + 1)
                        if u["kind"] == "diff":
                            pe.wait_ge(s_done[blk], u["t"] + 1)
                        for b, (c, kb, m) in enumerate(turned(u)):
                            last = pe.matmul(out_bank(u)[:, m["o"]:m["o"] + m["vw"]], PT[:, n % 2, b * P:(b + 1) * P],
                                             vt[:, kb, m["v"]:m["v"] + m["vw"]],
                                             start=(kb == 0), stop=(kb == u["t"]))
                        last.then_inc(s_pv[blk], 1)
                    for n in fill.get(i, []):
                        project(blk, n_base, n)

            def out_projection(blk, n_base):
                tag = ("mix1", "mix2")[blk]
                for t in range(T):
                    for c in range(2):
                        split_ready(n_base + c)
                        w = split_view((n_base + c) % LANES)
                        for k in range(KD):
                            if t == 0 and c == 0:
                                pe.wait_ge(s_hT[tag], k + 1)
                            last = product(PS[4 + 2 * t + c][:, :], tiles(tag, k, t * P, P), both(w, k, 0, HALF),
                                           start=(k == 0), stop=(k == KD - 1))
                        last.then_inc(s_proj[blk], 1)

            pe.wait_ge(s_const, 1)
            turn("attn1", hn)
            pe.wait_ge(s_stage, 16 * 12)
            pe.transpose(PS[7][:, 0:P], stage[:, 0, :], ident[:, :])
            pe.transpose(PS[7][:, P:2 * P], stage[:, 1, :], ident[:, :])
            pe.transpose(PS[7][:, 2 * P:2 * P + 53], stage[0:53, 2, :], ident[0:53, 0:53]).then_inc(s_vecT, 1)
            pe.wait_ge(s_vec, 1)
            for n in range(AHEAD[0]):
                project(0, N_IN, n)
            attention(0, N_IN, BETWEEN[0])
            turn("mix1", mix)
            out_projection(0, N_OUT)
            turn("ffn", hn)

            def zero_sums():
                for b in range(4, 8):
                    pe.matmul(PS[b][:, :], zrow[:, 0:P], zrow[:, :], start=True, stop=False, skip_group_check=True)

            def up(i, n, more=0):
                for part in range(2):
                    split_ready(n + part, more)
                    w = split_view((n + part) % LANES)
                    for b in range(2):
                        if not isinstance(i, int):
                            pe.wait_ge(s_conv, 4 * (i - 1) + 2 * part + b + 1)
                        for f in range(2):
                            c = (2 * b + f) * P
                            for k in range(KD):
                                if isinstance(i, int) and part == b == f == 0:
                                    pe.wait_ge(s_hT["ffn"], max(k + 1, 2))
                                last = product(PS[2 * part + b][:, f * S:(f + 1) * S], both(w, k, c, P),
                                               tiles("ffn", k), start=(k == 0), stop=(k == KD - 1))
                        last.then_inc(s_up, 1)

            def down(i, n, more=0):
                split_ready(n, more)
                pe.wait_ge(s_act, i + 1)
                w = split_view(n % LANES, D)
                for t in range(T):
                    for k in range(KE):
                        rows = [act_r[:, h, k, t * P:(t + 1) * P] for h in range(2)]
                        for c in range(2):
                            last = product(PS[4 + 2 * t + c][:, :], rows, both(w, k, c * HALF, HALF),
                                           start=False, stop=False, skip_group_check=True)
                    if t == 0:
                        last.then_inc(s_down0, 1)
                last.then_inc(s_down, 1)

            pe.wait_ge(s_const, 6)
            up(0, seq_gate(0))
            zero_sums()
            with pe.Fori(1, CHUNKS) as i:
                up(i, seq_gate(1), 3 * (i - 1))
                down(i - 1, seq_down(0), 3 * (i - 1))

            pe.wait_ge(s_sum, 4 * ADA_UNITS + 8)
            pe.wait_ge(s_conv, 4 * CHUNKS)
            for n, part in enumerate((0, 1, 3, 4)):
                for k in range(KD):
                    c = part * D + k * P
                    last = pe.matmul(PS[0][:, n * KD + k:n * KD + k + 1], ada[:, c:c + P], ones[:, 0:1],
                                     start=True, stop=True)
            last.then_inc(s_adam, 1)
            for n in range(4):
                c = (2, 5)[n // 2] * D + (n % 2) * HALF
                if n == 3:
                    pe.wait_ge(s_mod, 1)
                pe.matmul(PS[(1, 2, 3, 0)[n]][:, :], ones[:, :], ada[:, c:c + HALF],
                          start=True, stop=True).then_inc(s_adam, 1)

            down(CHUNKS - 1, seq_down(CHUNKS - 1))

            pe.wait_ge(s_mod, 5)
            turn("attn2", rows2)
            for n in range(AHEAD[1]):
                project(1, N_IN2, n)

            piece_taken(1, AHEAD[1])
            for i in range(SB_H + 2):
                if i < SB_H:
                    if i >= 2:
                        pe.wait_ge(s_zm, i - 1)
                    z = PS[i % 2]
                    pe.matmul(z[:, 0:S], kT[:, 4 + i // 2, 0:P], qz[:, 8 + i, :], start=True, stop=True)
                    pe.matmul(z[:, S:S + P], kT[:, 4 + i // 2, P:S], qz[:, 8 + i, P:S],
                              start=True, stop=True).then_inc(s_z, 1)
                if 1 <= i <= SB_H:
                    n = i - 1
                    pe.wait_ge(s_lk, n + 1)
                    R = PS[2 + n % 2]
                    lk = Eb[:, n % 2, :]
                    pe.matmul(R[:, 0:S], from_here[:, :], lk[:, 0:S], start=True, stop=False)
                    pe.matmul(R[:, P:S], ones[:, :], lk[:, S:S + P], start=False, stop=True)
                    pe.matmul(R[:, S:S + P], from_here[:, :], lk[:, S:S + P], start=True, stop=True).then_inc(s_R, 1)
                if i >= 2:
                    n = i - 2
                    pe.wait_ge(s_w, n + 1)
                    w = PT[:, n % 2, :]
                    c = n * HD
                    v = lambda kb: vt[:, kb, HALF + c:HALF + c + HD]
                    pe.matmul(PS[4][:, c:c + HD], w[:, 0:P], v(0), start=True, stop=True)
                    pe.matmul(PS[5][:, c:c + HD], w[:, P:S], v(0), start=True, stop=False)
                    pe.matmul(PS[5][:, c:c + HD], w[:, S:S + P], v(1), start=False, stop=True).then_inc(s_sbo, 1)
                for n in BETWEEN[1].get(i, []):
                    project(1, N_IN2, n)

            attention(1, N_IN2, {})
            turn("mix2", mix)
            out_projection(1, N_OUT2)
            turn("moe", hn)

            pe.wait_ge(s_hT["moe"], KD)
            pe.wait_ge(s_wr, 32)
            for t in range(T):
                for k in range(KD):
                    last = pe.matmul(PS[4][:, t * 36:(t + 1) * 36], hT[:, k, t * P:(t + 1) * P], wr[:, k, :],
                                     start=(k == 0), stop=(k == KD - 1))
            last.then_inc(s_lg, 1)
            for t in range(T):
                for k in range(KD):
                    last = pe.transpose(PS[2 * t + k // 4][:, (k % 4) * P:(k % 4 + 1) * P], hT[:, k, t * P:(t + 1) * P],
                                        ident[:, :])
                    if k % 4 == 3:
                        last.then_inc(s_back, 1)
            pe.wait_ge(s_A, 1)
            rk = PS[5]
            pe.matmul(rk[:, 0:NEXP], before[:, :], Aa[:, 0, :], start=True, stop=True)
            pe.matmul(rk[:, NEXP:2 * NEXP], before[:, :], Aa[:, 1, :], start=True, stop=False)
            pe.matmul(rk[:, NEXP:2 * NEXP], ones[:, :], Aa[:, 0, :], start=False, stop=True)
            pe.matmul(rk[:, 2 * NEXP:3 * NEXP], ones[:, :], Aa[:, 0, :], start=True, stop=False)
            pe.matmul(rk[:, 2 * NEXP:3 * NEXP], ones[:, :], Aa[:, 1, :], start=False, stop=True).then_inc(s_rank, 1)

            ACC = [PS[0], PS[1], PS[2], PS[3]]
            XB = [PS[4], PS[5]]
            GB, UB = PS[6], PS[7]

            def dispatch(p):
                pe.wait_ge(s_oneh, p + 1)
                for k in range(KD):
                    for t in range(T):
                        last = pe.matmul(XB[k // 4][:, (k % 4) * P:(k % 4 + 1) * P], hn[:, t, k * P:(k + 1) * P],
                                         oneh[:, t, :], start=(t == 0), stop=(t == T - 1))
                last.then_inc(s_disp, 1)

            def combine(p, tile_done=None):
                pe.wait_ge(s_combT, p + 2)
                pe.wait_ge(s_yA, p + 2)
                pe.wait_ge(s_yV, p + 2)
                for t in range(T):
                    for c in range(2):
                        last = pe.matmul(ACC[2 * t + c][:, :], combT[:, t, :], ye[:, c * HALF:(c + 1) * HALF],
                                         start=False, stop=False, skip_group_check=True)
                    if tile_done is not None and t == 0:
                        last.then_inc(tile_done, 1)
                last.then_inc(s_comb, 1)

            def pair(p):
                def ready(c):
                    for e in range(2):
                        pe.wait_ge(loaded[expert_slot(c, e)], 16 * (expert_loads(c, e) + 1) + 16 * p)

                pe.wait_ge(s_xeA, p + 1)
                pe.wait_ge(s_xeV, p + 1)
                pe.wait_ge(s_eactT, p + 1)
                ready(0)
                for k in range(KD):
                    for e in range(2):
                        w = chunk_view(expert_slot(0, e))
                        last = pe.matmul(GB[64 * e:64 * e + 64, :], xeT[:, k, 64 * e:64 * e + 64], w[:, k, :],
                                         start=(k == 0), stop=(k == KD - 1))
                last.then_inc(s_eg, 1)
                ready(1)
                pe.wait_ge(s_combT, p + 1)
                for k in range(KD):
                    for e in range(2):
                        w = chunk_view(expert_slot(1, e))
                        last = pe.matmul(UB[64 * e:64 * e + 64, :], xeT[:, k, 64 * e:64 * e + 64], w[:, k, :],
                                         start=(k == 0), stop=(k == KD - 1))
                last.then_inc(s_eu, 1)
                pe.wait_ge(s_yA, p + 1)
                pe.wait_ge(s_yV, p + 1)
                dispatch(p + 1)
                pe.wait_ge(s_eact, p + 1)
                for f in range(KE):
                    last = pe.transpose(GB[:, f * P:(f + 1) * P], eact[:, f * P:(f + 1) * P], ident[:, :])
                last.then_inc(s_etr, 1)
                combine(p - 1)
                pe.wait_ge(s_onehw, p + 1)
                for t in range(T):
                    last = pe.transpose(UB[:, t * P:(t + 1) * P], onehw[:, t, :], ident[:, :])
                last.then_inc(s_ctr, 1)
                pe.wait_ge(s_eactT, p + 2)
                pe.wait_ge(s_xeA, p + 2)
                pe.wait_ge(s_xeV, p + 2)
                ready(2)
                for c in range(2):
                    for f in range(KE):
                        for e in range(2):
                            w = ring[:, expert_slot(2, e), :].rearrange("p (k n) -> p k n", n=D)
                            last = pe.matmul(XB[c][64 * e:64 * e + 64, :], eactT[:, f, 64 * e:64 * e + 64],
                                             w[:, f, c * HALF:(c + 1) * HALF], start=(f == 0), stop=(f == KE - 1))
                last.then_inc(s_edn, 1)

            pe.wait_ge(s_h2, 4)
            pe.wait_ge(s_np, 1)
            for b in range(4):
                pe.matmul(ACC[b][:, :], zrow[:, 0:P], zrow[:, :], start=True, stop=False, skip_group_check=True)
            dispatch(0)
            with pe.Fori(0, PAIRS) as p:
                pair(p)
            n_pairs = pe.value_load(n_pairs_i[0:1, 0:1], min_val=PAIRS, max_val=PAIRS * PASSES)
            with pe.If(n_pairs > PAIRS):
                with pe.Fori(PAIRS, PAIRS * PASSES) as p:
                    pair(p)
            combine(n_pairs - 1, tile_done=s_comb0)

        @block.scalar
        def _(sc):
            order = [0]

            def then(ins):
                order[0] += 1
                ins.then_inc(s_alink, 1)
                sc.wait_ge(s_alink, order[0])

            cw = a["conv_w"].rearrange("o j (f p) -> (o j f) p", p=P)
            cb = a["conv_b"].rearrange("o (f p) -> (o f) p", p=P)
            sc.dma_start(stage[:, 0, :], cw[0:P, :]).then_inc(s_stage, 16)
            sc.dma_start(stage[0:FT, 1, :], cw[P:P + FT, :]).then_inc(s_stage, 16)
            sc.dma_start(stage[FT:2 * FT, 1, :], cb).then_inc(s_stage, 16)
            for name, row in (("c_2", R_C), ("attn_pre_g", R_PRE), ("ffn_pre_g", R_FPRE), ("g_mix_2", R_MIX),
                              ("g_ffn_2", R_FFN), ("swa_out_g", R_SWA), ("g_dil_out_2", R_DIL),
                              ("g_sb_out_2", R_SB), ("diff_subln_g", R_SUB)):
                v = a[name].rearrange("o (f p) -> (o f) p", p=P)
                sc.dma_start(stage[row:row + v.shape[0], 2, :], v).then_inc(s_stage, 16)
            sc.dma_start(sinks, a["swa_sinks"][0].partition_broadcast(P)).then_inc(s_sink, 16)
            for n, name in enumerate(("diff_lq1", "diff_lk1", "diff_lq2", "diff_lk2")):
                sc.dma_start(lamv[:, n, :], a[name][0].partition_broadcast(P)).then_inc(s_lamv, 16)

            def scaled(tag, scale, shift=None):
                for k in (2, 3, 6, 7):
                    sc.wait_ge(s_turn[tag], k // 2 + 1)
                    sc.activation(hT[:, k, :], PS[k // 2][:, (k % 2) * S:(k % 2 + 1) * S], ACT.Identity,
                                  scale=scale(k), bias=0.0 if shift is None else shift(k)).then_inc(s_hT[tag], 1)

            def rounded(tag, scale, shift=None):
                for k in range(KD):
                    sc.wait_ge(s_turn[tag], k // 2 + 1)
                    sc.activation(hi_T[:, k, :], PS[k // 2][:, (k % 2) * S:(k % 2 + 1) * S], ACT.Identity,
                                  scale=scale(k), bias=0.0 if shift is None else shift(k)).then_inc(s_hhi[tag], 1)

            def split(n, more=0):
                sc.wait_ge(loaded[n % LANES], 16 * (n // LANES + 1) + 16 * more)
                for part in range(2):
                    raw, hi, _ = split_part(n, part)
                    sc.activation(hi, raw, ACT.Copy).then_inc(s_whi, 1)

            def take(blk, pieces):
                for n in pieces:
                    if n % 2:
                        continue
                    c, kind, where = ITEMS[blk][n]
                    sc.wait_ge(s_gemm[blk], n + 1)
                    if n == 0:
                        sc.wait_ge(s_qzero, blk + 1)
                    for dst, src in taken(blk, kind, where, item_bank(blk, n)):
                        last = sc.activation(dst, src, ACT.Copy)
                    last.then_inc(s_evA[blk], 1)

            def softmaxes(blk, fill, splits):
                units = UNITS[blk]
                ends = finishes(blk)
                for i in range(len(units) + 1):
                    if i < len(units):
                        u = units[i]
                        sc.wait_ge(s_max[blk], i + 1)
                        if i >= 2:
                            sc.wait_ge(s_tr[blk], i - 1)
                        r, c, w = row_of(u), col_of(u), u["w"]
                        for j in range(len(u["maps"])):
                            last = sc.activation(Eb[:, i % 2, j * w:(j + 1) * w], Lb[:, i % 2, j * w:(j + 1) * w],
                                                 ACT.Exp, bias=nm[:, r, c + j:c + j + 1],
                                                 accum_out=den[:, r, c + j:c + j + 1])
                        last.then_inc(s_exp[blk], 1)
                        if u["kind"] == "swa" and i == ends[("swa", u["t"])]:
                            sc.wait_ge(s_sk, u["t"] + 1)
                            sc.activation(esink[:, u["t"], :], esink[:, u["t"], :], ACT.Exp).then_inc(s_ske, 1)
                    if i >= 1:
                        n = i - 1
                        w = P * len(turned(units[n]))
                        sc.wait_ge(s_tr[blk], n + 1)
                        if n >= 2:
                            sc.wait_ge(s_pv[blk], n - 1)
                        sc.activation(PT[:, n % 2, 0:w], PS[2 + n % 2][:, 0:w], ACT.Copy).then_inc(s_pt[blk], 1)
                    take(blk, fill.get(i, []))
                    for n in splits.get(i, []):
                        split(n)

            def squares(m, done):
                for t in range(T):
                    sc.wait_ge(*done(t))
                    if t > 0:
                        sc.wait_ge(s_sq[m], t)
                    for c in range(2):
                        last = sc.activation(junk[:, c * HALF:(c + 1) * HALF], PS[4 + 2 * t + c][:, :], ACT.Square,
                                             scale=D ** -0.5, accum_out=sq[:, 2 * t + c:2 * t + c + 1])
                    last.then_inc(s_sq[m], 1)

            split(N_IN)
            sc.wait_ge(s_vec, 1)
            rounded("attn1", lambda k: vec[:, 2, R_PRE + k:R_PRE + k + 1])
            split(N_IN + 1)
            sc.wait_ge(s_lamx, 1)
            sc.activation(lam2, lam2, ACT.Exp).then_inc(s_lame, 1)
            take(0, range(3))
            split(N_IN + 2)
            take(0, range(3, AHEAD[0]))
            softmaxes(0, BETWEEN[0], SPLITS[0])
            rounded("mix1", lambda k: vec[:, 2, R_SWA + k:R_SWA + k + 1] if k < 4 else subc)
            squares(0, lambda t: (s_proj[0], 2 * t + 2))
            rounded("ffn", lambda k: vec[:, 2, R_FPRE + k:R_FPRE + k + 1])
            split(seq_gate(0) + 1)
            sc.activation(siluc, vec[:, 2, R_C:R_C + KD], ACT.Silu).then_inc(s_c, 1)

            def taps(i, part, b):
                sc.wait_ge(s_up, 4 * i + 2 * part + b + 1)
                if not isinstance(i, int) and b == 0:
                    sc.wait_ge(s_act, i)
                for f in range(2):
                    ft = KE * i + (FT // 2) * part + 2 * b + f
                    last = sc.activation(conv[:, part, 2 * b + f, :], PS[2 * part + b][:, f * S:(f + 1) * S],
                                         ACT.Identity, scale=vec[:, 1, ds(ft, 1)], bias=vec[:, 1, ds(ft + FT, 1)])
                last.then_inc(s_tap, 1)

            def ffn(i, more=None):
                later = more is not None
                taps(i, 0, 0)
                if later:
                    split(seq_down(0), more)
                taps(i, 0, 1)
                sc.wait_ge(s_conv, 4 * i + 2)
                sc.activation(conv[:, 0, :, :], conv[:, 0, :, :], ACT.Gelu_apprx_tanh).then_inc(s_gelu, 1)
                taps(i, 1, 0)
                split(*((seq_gate(2), more) if later else (seq_gate(1),)))
                taps(i, 1, 1)
                split(*((seq_gate(2) + 1, more) if later else (seq_gate(1) + 1,)))
                sc.wait_ge(s_prod, i + 1)
                if later:
                    sc.wait_ge(s_down, i)
                sc.activation(act_r[:, 0, :, :], conv[:, 0, :, :], ACT.Copy).then_inc(s_ahi, 1)

            ffn(0)
            with sc.Fori(1, CHUNKS) as i:
                ffn(i, i - 1)
            def gate_rows(n):
                sc.wait_ge(s_adam, n + 2)
                dst = (post_attn, post_ffn)[n // 2][:, (n % 2) * HALF:(n % 2 + 1) * HALF]
                sc.activation(dst, PS[(1, 2, 3, 0)[n]][:, :], ACT.Copy).then_inc(s_mod, 1)

            sc.wait_ge(s_adam, 1)
            sc.activation(modc, PS[0][:, 0:4 * KD].rearrange("p (a b) -> p a b", a=4), ACT.Copy).then_inc(s_mod, 1)
            gate_rows(0)
            gate_rows(1)
            squares(1, lambda t: (s_down0, CHUNKS) if t == 0 else (s_down, CHUNKS))
            split(N_IN2 + 1)
            sc.wait_ge(s_rfree, 1)
            gate_rows(2)
            gate_rows(3)
            sc.wait_ge(s_modc, 1)
            rounded("attn2", lambda k: gmixc[:, k:k + 1], lambda k: modc[:, 0, k:k + 1])
            split(N_IN2 + 2)
            take(1, range(8))
            split(N_IN2 + 3)
            take(1, range(8, AHEAD[1]))
            for i in range(SB_H + 1):
                if i < SB_H:
                    sc.wait_ge(s_zm, i + 1)
                    if i >= 1:
                        sc.wait_ge(s_lk, i)
                    then(sc.activation(Lb[:, 0, 0:384], Lb[:, 1, 0:384], ACT.Abs))
                    then(sc.activation(Lb[:, 0, 0:384], Lb[:, 0, 0:384], ACT.Exp, scale=-1.0))
                    sc.activation(Lb[:, 0, 0:384], Lb[:, 0, 0:384], ACT.Ln, bias=1.0).then_inc(s_sb1, 1)
                if i >= 1:
                    n = i - 1
                    sc.wait_ge(s_t, n + 1)
                    sc.activation(PT[:, n % 2, 0:384], PT[:, n % 2, 0:384], ACT.Exp).then_inc(s_w, 1)
                take(1, BETWEEN[1].get(i, []))
                for n in SPLITS[1].get(i, []):
                    split(n)
            softmaxes(1, {}, {})
            rounded("mix2", lambda k: vec[:, 2, R_DIL + k:R_DIL + k + 1])
            scaled("moe", lambda k: gffnc[:, k:k + 1], lambda k: modc[:, 2, k:k + 1])
            for n in (1, 3):
                sc.wait_ge(s_back, n + 1)
                sc.activation(hn[:, n // 2, HALF:D], PS[n][:, :], ACT.Copy).then_inc(s_h2, 1)
            sc.wait_ge(s_r1, 1)
            sc.activation(gexp, gsh, ACT.Exp).then_inc(s_r2, 1)
            sc.wait_ge(s_r1, 2)
            sc.activation(ed, m2, ACT.Exp).then_inc(s_r2, 1)

            def tokens(p):
                sc.wait_ge(s_disp, p + 1)
                sc.activation(xeT[:, 0:4, :], PS[4][:, :].rearrange("p (a b) -> p a b", a=4), ACT.Copy)\
                    .then_inc(s_xeA, 1)

            def pair(p):
                sc.wait_ge(s_eg, p + 1)
                sc.wait_ge(s_etr, p + 1)
                sc.activation(eact, PS[6][:, :], ACT.Silu).then_inc(s_silu, 1)
                tokens(p + 1)
                sc.wait_ge(s_etr, p + 2)
                sc.activation(eactT, PS[6][:, :].rearrange("p (a b) -> p a b", a=KE), ACT.Copy).then_inc(s_eactT, 1)
                sc.wait_ge(s_edn, p + 1)
                sc.activation(ye[:, 0:HALF], PS[4][:, :], ACT.Copy).then_inc(s_yA, 1)

            sc.wait_ge(s_np, 1)
            tokens(0)
            with sc.Fori(0, PAIRS) as p:
                pair(p)
            n_pairs = sc.value_load(n_pairs_i[0:1, 0:1], min_val=PAIRS, max_val=PAIRS * PASSES)
            with sc.If(n_pairs > PAIRS):
                with sc.Fori(PAIRS, PAIRS * PASSES) as p:
                    pair(p)

        @block.vector
        def _(ve):
            order = [0]

            def then(ins):
                order[0] += 1
                ins.then_inc(s_link, 1)
                ve.wait_ge(s_link, order[0])

            asked, answered = [0], [0]

            def column():
                return ROOTS[asked[0]][0]

            def ask_root(ins):
                asked[0] += 1
                ins.then_inc(s_ms, 1)

            def root():
                answered[0] += 1
                ve.wait_ge(s_rs, answered[0])
                first = ROOTS[answered[0] - 1][0]
                return rstd[:, first:first + 1]

            def mean_squares(src, junk, at):
                return ve.tensor_tensor_reduce(junk, src, src, 1.0 / src.shape[1], EPS, ALU.mult, ALU.add,
                                               ms[:, at:at + 1])

            def norm(tag, t, dst):
                ask_root(mean_squares(x[:, t, :], mix[:, t, :], column()))
                ve.tensor_scalar(dst[:, t, :], x[:, t, :], root(), None, ALU.mult).then_inc(s_src[tag], 1)

            def scaled(tag, scale, shift=None):
                for k in (0, 1, 4, 5):
                    ve.wait_ge(s_turn[tag], k // 2 + 1)
                    src = PS[k // 2][:, (k % 2) * S:(k % 2 + 1) * S]
                    if shift is None:
                        ins = ve.tensor_scalar(hT[:, k, :], src, scale(k), None, ALU.mult)
                    else:
                        ins = ve.tensor_scalar(hT[:, k, :], src, scale(k), shift(k), ALU.mult, ALU.add)
                    ins.then_inc(s_hT[tag], 1)

            def low(tag, scale, shift=None):
                dst = lo_T[tag]
                for k in range(KD + 1):
                    if k < KD:
                        ve.wait_ge(s_hhi[tag], k // 2 * 2 + 2)
                        src = PS[k // 2][:, (k % 2) * S:(k % 2 + 1) * S]
                        if shift is None:
                            ve.scalar_tensor_tensor(dst[:, k, :], src, scale(k), hi_T[:, k, :],
                                                    ALU.mult, ALU.subtract).then_inc(s_hT[tag], 1)
                        else:
                            ve.tensor_scalar(shifted[:, k, :], src, scale(k), shift(k), ALU.mult, ALU.add)\
                                .then_inc(s_shift, 1)
                    if shift is not None and k > 0:
                        ve.wait_ge(s_shift, k)
                        ve.tensor_tensor(dst[:, k - 1, :], shifted[:, k - 1, :], hi_T[:, k - 1, :], ALU.subtract)\
                            .then_inc(s_hT[tag], 1)

            def split(n, more=0):
                for part in parts_of(n)[1]:
                    ve.wait_ge(s_whi, 2 * n + 1 + part + 2 * more)
                    raw, hi, lo = split_part(n, part)
                    last = ve.tensor_tensor(lo, raw, hi, ALU.subtract)
                if parts_of(n)[1]:
                    last.then_inc(s_wloV, 1)

            def take(blk, pieces):
                for n in pieces:
                    if n % 2 == 0:
                        continue
                    c, kind, where = ITEMS[blk][n]
                    ve.wait_ge(s_gemm[blk], n + 1)
                    if n == 1:
                        ve.wait_ge(s_qzero, blk + 1)
                    for dst, src in taken(blk, kind, where, item_bank(blk, n)):
                        last = ve.tensor_copy(dst, src)
                    last.then_inc(s_evV[blk], 1)

            def heads(v, t):
                return v[:, t, HALF:D].rearrange("p (h d) -> p h d", d=P)

            def softmaxes(blk, fill, splits):
                units = UNITS[blk]
                ends = finishes(blk)

                def logits(i):
                    u = units[i]
                    w, n = u["w"], len(u["maps"])
                    ve.wait_ge(s_sc[blk], i + 1)
                    if i >= 2:
                        ve.wait_ge(s_exp[blk], i - 1)
                    b0 = u["maps"][0]["b"]
                    S3 = PS[i % 2][:, 0:n * w].rearrange("p (a b) -> p a b", a=n)
                    L3 = Lb[:, i % 2, 0:n * w].rearrange("p (a b) -> p a b", a=n)
                    if u["kind"] == "diff":
                        for h in range(n // 2):
                            bb = bias[:, b0 + h, S - w:S].unsqueeze(1).broadcast_to([P, 2, w])
                            last = ve.scalar_tensor_tensor(L3[:, 2 * h:2 * h + 2, :], S3[:, 2 * h:2 * h + 2, :], SCALE,
                                                           bb, ALU.mult, ALU.add)
                    else:
                        last = ve.scalar_tensor_tensor(L3, S3, SCALE, bias[:, b0:b0 + n, S - w:S], ALU.mult, ALU.add)
                    last.then_inc(s_log[blk], 1)
                    ve.wait_ge(s_log[blk], i + 1)
                    r, c = row_of(u), col_of(u)
                    red = ve.tensor_reduce(nm[:, r, c:c + n], L3, X, ALU.max, negate=True)
                    if u["kind"] == "swa":
                        then(red)
                        red = ve.tensor_tensor(nm[:, r, c:c + n], nm[:, r, c:c + n], negsink[:, c:c + n], ALU.min)
                    red.then_inc(s_max[blk], 1)

                def difference(i):
                    u = units[i]
                    r, c, w, n = row_of(u), col_of(u), u["w"], len(u["maps"])
                    ve.wait_ge(s_exp[blk], i + 1)
                    then(ve.reciprocal(rden[:, r, c:c + n], den[:, r, c:c + n]))
                    for h in range(n // 2):
                        k = c + 2 * h
                        then(ve.tensor_scalar(rl[:, u["t"], h:h + 1], rden[:, r, k + 1:k + 2], lam, None, ALU.mult))
                        e0 = Eb[:, i % 2, 2 * h * w:(2 * h + 1) * w]
                        e1 = Eb[:, i % 2, (2 * h + 1) * w:(2 * h + 2) * w]
                        then(ve.tensor_scalar(e1, e1, rl[:, u["t"], h:h + 1], None, ALU.mult))
                        dst = Eb[:, i % 2, h * w:(h + 1) * w]
                        last = ve.scalar_tensor_tensor(dst, e0, rden[:, r, k:k + 1], e1, ALU.mult, ALU.subtract)
                    last.then_inc(s_dif, 1)

                def finish(n):
                    u = units[n]
                    r, t = row_of(u), u["t"]
                    done = list(ends.values()).index(n) + 1
                    window = mix[:, t, 0:HALF]
                    ve.wait_ge(s_pv[blk], n + 1)
                    if u["kind"] == "diff":
                        ve.tensor_copy(mix[:, t, HALF:D], out_bank(u)[:, :]).then_inc(s_done[blk], 1)
                        ve.wait_ge(s_done[blk], done)
                        squared = junk[:, HALF:D].rearrange("p (h d) -> p h d", d=P)
                        then(ve.tensor_tensor(squared, heads(mix, t), heads(mix, t), ALU.mult))
                        m = ms[:, 5 * t + 1:5 * t + 5]
                        then(ve.tensor_reduce(m, squared, X, ALU.add))
                        ask_root(ve.tensor_scalar(m, m, 1.0 / P, EPS, ALU.mult, ALU.add))
                        ve.tensor_scalar(window, window, root(), None, ALU.mult)
                        ve.tensor_tensor(heads(mix, t), heads(mix, t),
                                         rstd[:, 5 * t + 1:5 * t + 5].unsqueeze(2).broadcast_to([P, DIFF_H, P]),
                                         ALU.mult).then_inc(s_src["mix1"], 1)
                        return
                    if u["kind"] == "swa":
                        ve.wait_ge(s_ske, t + 1)
                        then(ve.tensor_tensor(den[:, r, :], den[:, r, :], esink[:, t, :], ALU.add))
                    then(ve.reciprocal(rden[:, r, :], den[:, r, :]))
                    ve.tensor_tensor(window.rearrange("p (h d) -> p h d", d=HD),
                                     out_bank(u)[:, :].rearrange("p (h d) -> p h d", d=HD),
                                     rden[:, r, :].unsqueeze(2).broadcast_to([P, 8, HD]), ALU.mult)\
                        .then_inc(s_done[blk], 1)
                    ve.wait_ge(s_done[blk], done)
                    if u["kind"] == "swa":
                        mean_squares(window, junk[:, 0:HALF], 5 * t)
                        return
                    ask_root(mean_squares(window, junk[:, 0:HALF], 2 * t))
                    root()
                    for c in range(2):
                        last = ve.tensor_scalar(mix[:, t, c * HALF:(c + 1) * HALF], mix[:, t, c * HALF:(c + 1) * HALF],
                                                rstd[:, 2 * t + c:2 * t + c + 1], None, ALU.mult)
                    last.then_inc(s_src["mix2"], 1)

                for i in range(len(units) + 2):
                    if i < len(units):
                        logits(i)
                        u = units[i]
                        if u["kind"] == "swa" and i == ends[("swa", u["t"])]:
                            ve.wait_ge(s_max[blk], i + 1)
                            ve.tensor_tensor(esink[:, u["t"], :], nm[:, u["t"], :], sinks, ALU.add).then_inc(s_sk, 1)
                    if 1 <= i <= len(units) and units[i - 1]["kind"] == "diff":
                        difference(i - 1)
                    if blk == 1 and i == 0:
                        stick_breaking_out()
                    if i - 2 in ends.values():
                        finish(i - 2)
                    take(blk, fill.get(i, []))
                    for n in splits.get(i, []):
                        split(n)

            def post_norm(m, rows, t, read=None):
                ve.wait_ge(s_sq[m], t + 1)
                at = column()
                ask_root(ve.scalar_tensor_tensor(ms[:, at:at + 1], sq[:, 2 * t:2 * t + 1], EPS,
                                                 sq[:, 2 * t + 1:2 * t + 2], ALU.add, ALU.add))
                r = root()
                for c in range(2):
                    last = ve.scalar_tensor_tensor(mix[:, t, c * HALF:(c + 1) * HALF], PS[4 + 2 * t + c][:, :],
                                                   r, rows[:, c * HALF:(c + 1) * HALF], ALU.mult, ALU.mult)
                if read is None:
                    then(last)
                else:
                    last.then_inc(read, 1)
                    ve.wait_ge(read, 1)
                then(ve.tensor_tensor(x[:, t, :], x[:, t, :], mix[:, t, :], ALU.add))

            def gated(bank, rows, t):
                for c in range(2):
                    last = ve.tensor_tensor(mix[:, t, c * HALF:(c + 1) * HALF], PS[bank + 2 * t + c][:, :],
                                            rows[:, c * HALF:(c + 1) * HALF], ALU.mult)
                then(last)
                then(ve.tensor_tensor(x[:, t, :], x[:, t, :], mix[:, t, :], ALU.add))

            for t in range(T):
                ve.wait_ge(s_x[t], 16)
                ask_root(mean_squares(x[:, t, :], mix[:, t, :], column()))
            for t in range(T):
                ve.tensor_scalar(hn[:, t, :], x[:, t, :], root(), None, ALU.mult).then_inc(s_src["attn1"], 1)
            ve.wait_ge(s_vecT, 1)
            ve.tensor_copy(vec[:, 0:2, :], PS[7][:, 0:2 * P].rearrange("p (a b) -> p a b", a=2))
            then(ve.tensor_copy(vec[:, 2, 0:53], PS[7][:, 2 * P:2 * P + 53]))
            ve.tensor_scalar(subc, vec[:, 2, R_SUB:R_SUB + 1], 1.0 - LAMBDA_INIT, None, ALU.mult).then_inc(s_vec, 1)
            low("attn1", lambda k: vec[:, 2, R_PRE + k:R_PRE + k + 1])
            split(N_IN)
            split(N_IN + 1)
            ve.wait_ge(s_lamv, 64)
            for n in range(2):
                last = ve.tensor_tensor_reduce(mix[:, 1, n * HD:(n + 1) * HD], lamv[:, 2 * n, :], lamv[:, 2 * n + 1, :],
                                               1.0, 0.0, ALU.mult, ALU.add, lam2[:, n:n + 1])
            last.then_inc(s_lamx, 1)
            ve.wait_ge(s_sink, 16)
            ve.tensor_scalar(negsink, sinks, -1.0, None, ALU.mult)
            ve.wait_ge(s_lame, 1)
            then(ve.tensor_scalar(lam, lam2[:, 0:1], lam2[:, 1:2], LAMBDA_INIT, ALU.subtract, ALU.add))
            take(0, range(3))
            split(N_IN + 2)
            take(0, range(3, AHEAD[0]))
            ve.wait_ge(s_mask, 1)
            softmaxes(0, BETWEEN[0], SPLITS[0])
            low("mix1", lambda k: vec[:, 2, R_SWA + k:R_SWA + k + 1] if k < 4 else subc)
            dist = mix[:, 0, 0:S].bitcast(i32)
            masked = mix[:, 0, S:2 * S].bitcast(i32)
            four = mix[:, 0, 2 * S:3 * S]
            sixteen = mix[:, 0, 3 * S:4 * S]
            count = mix[:, 1, 0:S]
            term = mix[:, 1, S:2 * S]
            then(ve.tensor_scalar(dist, negdist[:, :], -1.0, None, ALU.mult))
            then(ve.tensor_scalar(masked, dist, 3, None, ALU.bitwise_and))
            then(ve.tensor_scalar(four, masked, 0.0, None, ALU.is_equal))
            then(ve.tensor_scalar(masked, dist, 15, None, ALU.bitwise_and))
            then(ve.tensor_scalar(sixteen, masked, 0.0, None, ALU.is_equal))
            then(ve.tensor_tensor(four, four, sixteen, ALU.add))
            then(ve.tensor_scalar(sixteen, negdist[:, :], -128.0, None, ALU.is_ge))
            then(ve.tensor_tensor(count, four, sixteen, ALU.add))
            then(ve.tensor_scalar(lncount[:, :], count, 2.0, math.log(2.0), ALU.is_ge, ALU.mult))
            then(ve.tensor_scalar(term, count, 3.0, math.log(3.0) - math.log(2.0), ALU.is_ge, ALU.mult))
            then(ve.tensor_tensor(lncount[:, :], lncount[:, :], term, ALU.add))
            then(ve.tensor_scalar(term, count, 1.0, NEG, ALU.is_lt, ALU.mult))
            then(ve.tensor_tensor(lncount[:, :], lncount[:, :], term, ALU.add))
            then(ve.tensor_scalar(term, negdist[:, :], 0.0, NEG, ALU.is_gt, ALU.mult))
            then(ve.tensor_tensor(lncount[:, :], lncount[:, :], term, ALU.add))
            for h in range(DIL_H):
                last = ve.scalar_tensor_tensor(bias[:, h, :], negdist[:, :], float(np.float32(dil_slopes[h])),
                                               lncount[:, :], ALU.mult, ALU.add)
            then(last)
            ve.wait_ge(s_rows, 32)
            for t in range(T):
                post_norm(0, post_attn, t)
                norm("ffn", t, hn)
            low("ffn", lambda k: vec[:, 2, R_FPRE + k:R_FPRE + k + 1])
            split(seq_gate(0) + 1)

            def convolve(i, part, b):
                ve.wait_ge(s_tap, 4 * i + 2 * part + b + 1)
                for back in (1, 2):
                    for f in range(2):
                        ft = KE * i + (FT // 2) * part + 2 * b + f
                        tap = vec[:, 0, ds(ft + FT * (2 - back), 1)]
                        c = conv[:, part, 2 * b + f, back:S]
                        n = 8 * i + 4 * part + 2 * b + f + 1
                        if back == 2:
                            ve.wait_ge(s_cv1, n)
                        last = ve.scalar_tensor_tensor(c, PS[2 * part + b][:, f * S:(f + 1) * S - back], tap, c,
                                                       ALU.mult, ALU.add)
                        if back == 1:
                            last.then_inc(s_cv1, 1)
                last.then_inc(s_conv, 1)

            def modulation(r, c):
                ve.wait_ge(s_adab[c % 2], 16 * (ADA_EACH // 2 * r + c // 2 + 1))
                for m in range(4):
                    h, k = m % 2, m // 2
                    dst = ada[:, ds(1024 * r + 2 * ADA_W * (c // 4) + ADA_W * h, ADA_W)]
                    ve.wait_ge(s_sum, 4 * (ADA_EACH * r + c) + m + 7)
                    tile = 2 * (c % 4) + k
                    ve.scalar_tensor_tensor(dst, ada_buf[:, c % 2, k, h * ADA_W:(h + 1) * ADA_W], siluc[:, tile:tile + 1], dst,
                                            ALU.mult, ALU.add).then_inc(s_sum, 1)

            def ffn(i, more=None, units=False):
                later = more is not None

                def modulate(*cs):
                    for c in cs:
                        if units:
                            modulation(i - 1, c)

                modulate(0, 1)
                convolve(i, 0, 0)
                modulate(2, 3)
                if later:
                    split(seq_down(0), 3 * more)
                convolve(i, 0, 1)
                modulate(4, 5)
                convolve(i, 1, 0)
                modulate(6)
                split(*((seq_gate(2), 3 * more) if later else (seq_gate(1),)))
                convolve(i, 1, 1)
                ve.wait_ge(s_conv, 4 * i + 4)
                ve.wait_ge(s_gelu, i + 1)
                ve.tensor_tensor(conv[:, 0, :, :], conv[:, 0, :, :], conv[:, 1, :, :], ALU.mult).then_inc(s_prod, 1)
                modulate(7)
                split(*((seq_gate(2) + 1, 3 * more) if later else (seq_gate(1) + 1,)))
                ve.wait_ge(s_ahi, i + 1)
                ve.tensor_tensor(act_r[:, 1, :, :], conv[:, 0, :, :], act_r[:, 0, :, :], ALU.subtract)\
                    .then_inc(s_act, 1)

            ffn(0)
            ve.wait_ge(s_ada0, 16)
            ve.wait_ge(s_c, 1)
            ve.nop().then_inc(s_sum, 8)
            with ve.Fori(1, CHUNKS - 1) as i:
                ffn(i, i - 1, units=True)
            ffn(CHUNKS - 1, CHUNKS - 2)
            ve.wait_ge(s_mod, 1)
            ve.scalar_tensor_tensor(gmixc, modc[:, 1, :], 1.0, vec[:, 2, R_MIX:R_MIX + KD], ALU.add, ALU.mult)
            ve.scalar_tensor_tensor(gffnc, modc[:, 3, :], 1.0, vec[:, 2, R_FFN:R_FFN + KD], ALU.add, ALU.mult)\
                .then_inc(s_modc, 1)
            for t in range(T):
                post_norm(1, post_ffn, t, read=s_rfree if t == T - 1 else None)
                norm("attn2", t, rows2)
            split(N_IN2 + 1)
            ve.wait_ge(s_modc, 1)
            low("attn2", lambda k: gmixc[:, k:k + 1], lambda k: modc[:, 0, k:k + 1])
            split(N_IN2 + 2)
            take(1, range(8))
            split(N_IN2 + 3)
            take(1, range(8, AHEAD[1]))

            ve.wait_ge(s_bias2, 1)
            for i in range(SB_H + 1):
                if i < SB_H:
                    zs = Lb[:, 1, 0:384]
                    r = mix[:, 0, HALF:HALF + 384]
                    ve.wait_ge(s_z, i + 1)
                    ve.tensor_scalar(zs, PS[i % 2][:, 0:384], SCALE, None, ALU.mult).then_inc(s_zm, 1)
                    ve.wait_ge(s_zm, i + 1)
                    ve.tensor_scalar(r, zs, 0.0, None, ALU.max)
                    dst = PT[:, i % 2, 0:384]
                    if i >= 2:
                        ve.wait_ge(s_sbo, i - 1)
                    then(ve.tensor_tensor(dst, zs, SB_ADD, ALU.add))
                    ve.wait_ge(s_sb1, i + 1)
                    then(ve.tensor_tensor(r, r, Lb[:, 0, 0:384], ALU.add))
                    if i >= 2:
                        ve.wait_ge(s_R, i - 1)
                    ve.tensor_tensor(Eb[:, i % 2, 0:384], r, SB_NEG, ALU.mult).then_inc(s_lk, 1)
                if i >= 1:
                    n = i - 1
                    ve.wait_ge(s_R, n + 1)
                    dst = PT[:, n % 2, 0:384]
                    ve.tensor_tensor(dst, PS[2 + n % 2][:, 0:384], dst, ALU.add).then_inc(s_t, 1)
                take(1, BETWEEN[1].get(i, []))
                for n in SPLITS[1].get(i, []):
                    split(n)

            def stick_breaking_out():
                ve.wait_ge(s_sbo, SB_H)
                for t in range(T):
                    last = ve.tensor_copy(mix[:, t, HALF:D], PS[4 + t][:, :])
                then(last)
                for t in range(T):
                    then(mean_squares(mix[:, t, HALF:D], junk[:, HALF:D], 2 * t + 1))

            softmaxes(1, {}, {})
            ve.memset(ranks[:, :, PASSES * NEXP:], -1.0).then_inc(s_mixed, 1)
            low("mix2", lambda k: vec[:, 2, R_DIL + k:R_DIL + k + 1])
            ve.wait_ge(s_mod, 5)
            for t in range(T):
                ve.wait_ge(s_proj[1], 2 * t + 2)
                gated(4, post_attn, t)
                norm("moe", t, hn)
            scaled("moe", lambda k: gffnc[:, k:k + 1], lambda k: modc[:, 2, k:k + 1])

            def over_t(v, n):
                return v.unsqueeze(1).broadcast_to([P, T, n])

            def over_n(v, n):
                return v.unsqueeze(2).broadcast_to([P, T, n])

            i4, i8, i32c = iota[:, 0:NGRP], iota[:, 0:EPG], iota[:, 0:NEXP]
            ve.wait_ge(s_lg, 1)
            then(ve.tensor_copy(lg, PS[4][:, 0:72].rearrange("p (t n) -> p t n", t=T)))
            then(ve.tensor_reduce(gmax, lg[:, :, 0:NGRP], X, ALU.max))
            ve.tensor_tensor(gsh, lg[:, :, 0:NGRP], over_n(gmax, NGRP), ALU.subtract).then_inc(s_r1, 1)
            ve.wait_ge(s_r1, 1)
            for n in (0, 2):
                ve.wait_ge(s_back, n + 1)
                ve.tensor_copy(hn[:, n // 2, 0:HALF], PS[n][:, :]).then_inc(s_h2, 1)
            then(ve.tensor_scalar(c4, gsh, 0.0, 64.0, ALU.is_lt, ALU.mult))
            then(ve.tensor_tensor(c4, c4, over_t(i4, NGRP), ALU.add))
            then(ve.tensor_reduce(gidx, c4, X, ALU.min))
            then(ve.tensor_tensor(ohg, over_t(i4, NGRP), over_n(gidx, NGRP), ALU.is_equal))
            ve.wait_ge(s_r2, 1)
            then(ve.tensor_reduce(gsum, gexp, X, ALU.add))
            then(ve.reciprocal(ggate, gsum))
            for t in range(T):
                last = ve.tensor_tensor(sel[:, t, :, :], lg[:, t, NGRP:].rearrange("p (g j) -> p g j", j=EPG),
                                        ohg[:, t, :].unsqueeze(2).broadcast_to([P, NGRP, EPG]), ALU.mult)
            then(last)
            for t in range(T):
                last = ve.tensor_reduce(el[:, t, :], sel[:, t, :, :].rearrange("p g j -> p j g"), X, ALU.add)
            then(last)
            then(ve.tensor_reduce(m1, el, X, ALU.max))
            then(ve.tensor_tensor(esh, el, over_n(m1, EPG), ALU.subtract))
            then(ve.tensor_scalar(c8, esh, 0.0, 64.0, ALU.is_lt, ALU.mult))
            then(ve.tensor_tensor(c8, c8, over_t(i8, EPG), ALU.add))
            then(ve.tensor_reduce(i1, c8, X, ALU.min))
            then(ve.tensor_tensor(oh1, over_t(i8, EPG), over_n(i1, EPG), ALU.is_equal))
            then(ve.scalar_tensor_tensor(el2, oh1, NEG, esh, ALU.mult, ALU.add))
            ve.tensor_reduce(m2, el2, X, ALU.max).then_inc(s_r1, 1)
            ve.wait_ge(s_r1, 2)
            then(ve.tensor_tensor(c8, el2, over_n(m2, EPG), ALU.is_lt))
            then(ve.scalar_tensor_tensor(c8, c8, 64.0, over_t(i8, EPG), ALU.mult, ALU.add))
            then(ve.tensor_reduce(i2, c8, X, ALU.min))
            then(ve.scalar_tensor_tensor(id1, gidx, float(EPG), i1, ALU.mult, ALU.add))
            then(ve.scalar_tensor_tensor(id2, gidx, float(EPG), i2, ALU.mult, ALU.add))
            then(ve.tensor_tensor(A1, over_t(i32c, NEXP), over_n(id1, NEXP), ALU.is_equal))
            then(ve.tensor_tensor(A2, over_t(i32c, NEXP), over_n(id2, NEXP), ALU.is_equal))
            ve.tensor_tensor(Aa, A1, A2, ALU.add).then_inc(s_A, 1)
            ve.wait_ge(s_r2, 2)
            then(ve.tensor_scalar(p1, ed, 1.0, None, ALU.add))
            then(ve.reciprocal(p1, p1))
            then(ve.tensor_tensor(p1, p1, ggate, ALU.mult))
            then(ve.tensor_tensor(p2, p1, ed, ALU.mult))
            then(ve.tensor_tensor(Wt, A1, over_n(p1, NEXP), ALU.mult))
            then(ve.tensor_tensor(Wt2, A2, over_n(p2, NEXP), ALU.mult))
            then(ve.tensor_tensor(Wt, Wt, Wt2, ALU.add))
            for q in range(PASSES):
                last = ve.tensor_copy(wsel[:, :, q * NEXP:(q + 1) * NEXP], Wt)
            then(last)
            ve.wait_ge(s_rank, 1)
            then(ve.scalar_tensor_tensor(rank1, PS[5][:, 0:2 * NEXP].rearrange("p (t n) -> p t n", t=T), 1.0, Aa,
                                         ALU.add, ALU.mult))
            for q in range(PASSES):
                last = ve.tensor_scalar(ranks[:, :, q * NEXP:(q + 1) * NEXP], rank1, -1.0 - SLOTS * q, None, ALU.add)
            then(last)
            then(ve.tensor_reduce(cmax, PS[5][:, 2 * NEXP:3 * NEXP], X, ALU.max))
            then(ve.tensor_scalar(over, cmax, float(SLOTS), float(PAIRS * (PASSES - 1)), ALU.is_gt, ALU.mult))
            ve.memset(combT, 0.0)
            ve.memset(ye, 0.0)
            then(ve.tensor_scalar(n_pairs_i[:, :], over, float(PAIRS), None, ALU.add))

            def pick(p):
                for e in range(2):
                    for t in range(T):
                        last = ve.tensor_scalar(oneh[:, t, e * SLOTS:(e + 1) * SLOTS], iota[:, :],
                                                ranks[:, t, ds(2 * p + e, 1)], None, ALU.is_equal)
                last.then_inc(s_oneh, 1)

            def tokens(p):
                ve.wait_ge(s_disp, p + 1)
                ve.tensor_copy(xeT[:, 4:8, :], PS[5][:, :].rearrange("p (a b) -> p a b", a=4)).then_inc(s_xeV, 1)

            def pair(p):
                ve.wait_ge(s_disp, p + 1)
                pick(p + 1)
                ve.wait_ge(s_ctr, p + 1)
                for e in range(2):
                    for t in range(T):
                        last = ve.tensor_scalar(onehw[:, t, e * SLOTS:(e + 1) * SLOTS], iota[:, :],
                                                ranks[:, t, ds(2 * p + e, 1)], wsel[:, t, ds(2 * p + e, 1)],
                                                ALU.is_equal, ALU.mult)
                last.then_inc(s_onehw, 1)
                ve.wait_ge(s_eu, p + 1)
                ve.wait_ge(s_silu, p + 1)
                ve.tensor_tensor(eact, eact, PS[7][:, :], ALU.mult).then_inc(s_eact, 1)
                tokens(p + 1)
                ve.wait_ge(s_ctr, p + 2)
                ve.wait_ge(s_comb, p + 1)
                ve.tensor_copy(combT, PS[7][:, 0:S].rearrange("p (t n) -> p t n", t=T)).then_inc(s_combT, 1)
                ve.wait_ge(s_edn, p + 1)
                ve.tensor_copy(ye[:, HALF:D], PS[5][:, :]).then_inc(s_yV, 1)

            for place_free in (s_eactT, s_combT, s_yA, s_yV, s_ctr, s_etr):
                ve.nop().then_inc(place_free, 1)
            pick(0)
            ve.wait_ge(s_oneh, 1)
            ve.wait_ge(s_h2, 4)
            ve.nop().then_inc(s_np, 1)
            tokens(0)
            with ve.Fori(0, PAIRS) as p:
                pair(p)
            n_pairs = ve.value_load(n_pairs_i[0:1, 0:1], min_val=PAIRS, max_val=PAIRS * PASSES)
            with ve.If(n_pairs > PAIRS):
                with ve.Fori(PAIRS, PAIRS * PASSES) as p:
                    pair(p)

            ve.wait_ge(s_rows, 48)
            for t in range(T):
                if t == 0:
                    ve.wait_ge(s_comb0, 1)
                else:
                    ve.wait_ge(s_comb, n_pairs + 1)
                gated(0, post_ffn, t)
                ask_root(mean_squares(x[:, t, :], mix[:, t, :], column()))
                ve.scalar_tensor_tensor(hn[:, t, :], x[:, t, :], root(), final_g[:, :], ALU.mult, ALU.mult)\
                    .then_inc(s_fin, 1)


_INS = ["x", "attn_pre_g", "w_in", "swa_sinks", "swa_out_g", "diff_lq1", "diff_lk1", "diff_lq2", "diff_lk2",
        "diff_subln_g", "w_out", "attn_post_g", "ffn_pre_g", "w_up", "conv_w", "conv_b", "w_down", "ffn_post_g",
        "c_2", "w_ada_2", "b_ada_2", "g_mix_2", "w_in_2", "g_dil_out_2", "g_sb_out_2", "w_out_2", "g_ffn_2",
        "w_group_2", "w_expert_2", "w_gate_2", "w_up_2", "w_down_2", "g_final_2"]


def kernel(**inputs):
    import concourse.bacc as bacc
    from concourse.bass_utils import run_bass_kernel_spmd

    nc = bacc.Bacc("TRN2", target_bir_lowering=False, num_devices=1)
    arrays, args = {}, {}
    for name in _INS:
        array = np.ascontiguousarray(inputs[name])
        arrays["in_" + name] = array
        args[name] = nc.dram_tensor("in_" + name, array.shape, mybir.dt.from_np(array.dtype),
                                    kind="ExternalInput").ap()
    out = nc.dram_tensor("out_0", inputs["x"].shape, mybir.dt.float32, kind="ExternalOutput").ap()
    two_block_kernel(nc, args, out)
    result = run_bass_kernel_spmd(nc, [arrays], core_ids=[0])
    return result.results[0]["out_0"]
```

```python
import math
from contextlib import ExitStack

import numpy as np

import concourse.bass as bass
from concourse import mybir


def alibi_slopes(n):
    def pow2(m):
        return [2.0 ** (-8.0 * (i + 1) / m) for i in range(m)]
    if math.log2(n).is_integer():
        return pow2(n)
    c = 2 ** int(math.floor(math.log2(n)))
    return sorted(pow2(c) + pow2(2 * c)[0::2][: n - c], reverse=True)


def two_block_kernel(nc, a, out):
    f32 = mybir.dt.float32
    f32r = mybir.dt.float32r
    bf16 = mybir.dt.bfloat16
    i32 = mybir.dt.int32
    ALU = mybir.AluOpType
    ACT = mybir.ActivationFunctionType
    X = mybir.AxisListType.X
    ds = bass.ds

    P = 128
    D = a["x"].shape[2]
    S = a["x"].shape[1]
    T = S // P
    KD = D // P
    HD = 64
    HALF = 512
    FF = a["w_down"].shape[1]
    FT = 2 * FF // P
    CHUNKS = FF // HALF
    NEXP = a["w_gate_2"].shape[1]
    FE = a["w_gate_2"].shape[3]
    KE = FE // P
    NGRP = a["w_group_2"].shape[2]
    EPG = NEXP // NGRP
    SLOTS = 64
    PAIRS = NEXP // 2
    PASSES = S // SLOTS
    ADA = a["w_ada_2"].shape[2]
    ADA_W = 256
    ADA_UNITS = ADA // (2 * ADA_W) * KD // 2
    ADA_EACH = ADA_UNITS // (CHUNKS - 2)
    EPS = 1e-6
    SCALE = HD ** -0.5
    NEG = -1e30
    LAMBDA_INIT = 0.8 - 0.6 * math.exp(-0.3 * 0)
    SWA_Q, SWA_KV, DIFF_H, DIL_H, SB_H, WINDOW = 8, 2, 4, 8, 8, 128
    slopes12 = alibi_slopes(SWA_Q + DIFF_H)
    swa_slopes, diff_slopes = slopes12[:SWA_Q], slopes12[SWA_Q:]
    dil_slopes = [2.0 ** (-8.0 * (i + 1) / DIL_H) for i in range(DIL_H)]

    LANES = 3
    SLOT_N = 2 * LANES
    SLOT_W = 4096
    N_IN = 0
    IN_CHUNKS = -(-a["w_in"].shape[2] // HALF)
    N_OUT = N_IN + IN_CHUNKS
    N_FFN = N_OUT + 2
    N_IN2 = N_FFN + 3 * CHUNKS
    IN2_CHUNKS = a["w_in_2"].shape[2] // HALF
    N_OUT2 = N_IN2 + IN2_CHUNKS
    N_MOE = N_OUT2 + 2

    def seq_gate(i):
        return N_FFN if i == 0 else N_FFN + 2 + 3 * (i - 1)

    def seq_down(i):
        return N_FFN + 2 + 3 * i + 2 if i < CHUNKS - 1 else N_FFN + 3 * CHUNKS - 1

    POOL_SHARE = [SLOT_W] * N_MOE
    POOL_SHARE[N_IN:N_IN + 3] = [SLOT_W // 2, 0, 0]
    POOL_SHARE[N_OUT:N_IN2 + 3] = [2560] * (N_IN2 + 3 - N_OUT)

    ctx = ExitStack()
    with ctx:
        places = {}

        def sb(name, shape, dt=f32):
            tensor = ctx.enter_context(nc.sbuf_tensor(name, shape, dt))
            places[name] = nc.sbuf_base - int(np.prod(shape[1:])) * mybir.dt.size(dt)
            return tensor

        def rounded_view(name, shape):
            return nc.alloc_sbuf_tensor_at(name + "_r", shape, f32r, offset=places[name])

        def sem(name):
            return ctx.enter_context(nc.semaphore(name))

        ring = sb("ring", [P, SLOT_N, SLOT_W])
        x = sb("x_tok", [P, T, D])
        hn = sb("hn", [P, T, D])
        hT = sb("hT", [P, KD, S])
        mix = sb("mix", [P, T, D])
        scratch = sb("scratch", [P, 7168])
        kT = sb("kT", [P, 8, S])
        vt = sb("v_tok", [P, T, D])
        bias = sb("bias", [P, 12, S])
        post_attn = sb("post_attn", [P, D])
        post_ffn = sb("post_ffn", [P, D])
        final_g = sb("final_g", [P, D])
        vec = sb("vec", [P, 3, P])
        ident = sb("ident", [P, P])
        from_here = sb("from_here", [P, P])
        before = sb("before", [P, P])
        ones = sb("ones", [P, P])
        negdist = sb("negdist", [P, S])
        lncount = sb("lncount", [P, S])
        iota = sb("iota", [P, SLOTS])
        zrow = sb("zrow", [P, HALF], bf16)
        small = sb("small", [P, 400])
        n_pairs_i = sb("n_pairs_i", [P, 1], i32)

        place = [0]

        def cell(*shape):
            n = int(np.prod(shape))
            v = small[:, place[0]:place[0] + n]
            place[0] += n
            if len(shape) == 2:
                v = v.rearrange("p (a b) -> p a b", a=shape[0])
            return v

        ms = cell(10)
        rstd = cell(10)
        minus_half = cell(10)
        ROOTS = [(t, 1) for t in range(T)]
        ROOTS += [(5 * t, 5) for t in range(T)]
        ROOTS += [(0, 1), (1, 1)] * (2 * T)
        ROOTS += [(2 * t, 2) for t in range(T)]
        ROOTS += [(t, 1) for t in range(T)] * 2
        tiny = cell(1)
        sq = cell(4)
        nm = cell(2 * T, 8)
        den = cell(2 * T, 8)
        rden = cell(2 * T, 8)
        sinks = cell(8)
        negsink = cell(8)
        esink = cell(T, 8)
        lamv = vt[:, 0, 0:256].rearrange("p (a b) -> p a b", a=4)
        lam2 = cell(2)
        lam = cell(1)
        rl = cell(T, 4)
        modc = cell(4, KD)
        gmixc = cell(KD)
        gffnc = cell(KD)
        siluc = cell(KD)
        subc = cell(1)
        hsq = cell(T, DIFF_H)
        frac = cell(NEXP)

        qz = scratch[:, 0:4096].rearrange("p (h s) -> p h s", s=S)
        Lb = scratch[:, 4096:5120].rearrange("p (r n) -> p r n", r=2)
        Eb = scratch[:, 5120:6144].rearrange("p (r n) -> p r n", r=2)
        PT = scratch[:, 6144:7168].rearrange("p (r n) -> p r n", r=2)
        ada = scratch[:, 0:ADA]
        ada_buf = kT[:, :, :].rearrange("p (b k n) s -> p b k (n s)", b=2, k=2)
        conv = mix[:, :, :].rearrange("p c (f s) -> p c f s", s=S)
        hi_T = rounded_view("hT", [P, KD, S])
        lo_T = {"attn1": rounded_view("hn", [P, KD, S]), "mix1": rounded_view("kT", [P, KD, S]),
                "ffn": rounded_view("v_tok", [P, KD, S]), "mix2": rounded_view("bias", [P, KD, S])}
        lo_T["attn2"] = lo_T["attn1"]
        act_r = lo_T["attn1"][:, :, :].rearrange("p (c f) s -> p c f s", c=2)
        ring_r = rounded_view("ring", [P, SLOT_N, SLOT_W])
        shifted = hn[:, :, :].rearrange("p t (k s) -> p (t k) s", s=S)
        junk = final_g[:, :]
        rows2 = kT[:, :, :].rearrange("p (t k) s -> p t (k s)", t=T)
        off = [0]

        def piece(*shape):
            n = int(np.prod(shape))
            v = scratch[:, off[0]:off[0] + n]
            off[0] += n
            if len(shape) == 2:
                return v.rearrange("p (a b) -> p a b", a=shape[0])
            if len(shape) == 3:
                return v.rearrange("p (a b c) -> p a b c", a=shape[0], b=shape[1])
            return v

        oneh = piece(T, P)
        onehw = piece(T, P)
        xeT = piece(KD, P)
        eact = piece(HALF)
        eactT = piece(KE, P)
        combT = piece(T, P)
        ye = piece(D)
        lg = piece(T, NGRP + NEXP)
        el, el2, first = (piece(T, NEXP) for _ in range(3))
        gexp, gfirst, outside = (piece(T, NGRP) for _ in range(3))
        gmax, ngmax, gsum, ggate, gidx, m1, i1, m2, i2, ed, p1, p2 = (piece(T) for _ in range(12))
        A1, A2, Aa, Wt, Wt2 = (piece(T, NEXP) for _ in range(5))
        rank1 = piece(T, NEXP)
        ranks = piece(T, PASSES * NEXP + 2)
        wsel = piece(T, PASSES * NEXP)
        wr = piece(KD, NGRP + NEXP)
        cmax, over = piece(1), piece(1)
        tiles_of = lambda v: v.rearrange("p (k n) -> p k n", n=HALF)
        spare = tiles_of(scratch[:, 7168 - 2 * HALF:])
        assert off[0] <= 7168 - 2 * HALF
        flat_bias = bias[:, :, :].rearrange("p a s -> p (a s)")
        EXTRA = [[(0, tiles_of(kT[:, :, :].rearrange("p k s -> p (k s)"))),
                  (4, tiles_of(vt[:, :, :].rearrange("p t n -> p (t n)")))],
                 [(0, tiles_of(flat_bias)), (6, spare)],
                 [(0, tiles_of(hT[:, :, :].rearrange("p k s -> p (k s)"))),
                  (4, tiles_of(mix[:, :, :].rearrange("p t n -> p (t n)")))]]
        softplus = lambda n: junk[:, n % 2 * HALF:n % 2 * HALF + 384]
        rows_of = lambda v: v.rearrange("p (k n) -> p k n", n=D)
        EXTRA_DOWN = [[(0, rows_of(kT[:, :, :].rearrange("p k s -> p (k s)"))),
                       (2, rows_of(vt[:, :, :].rearrange("p t n -> p (t n)")))],
                      [(0, rows_of(flat_bias)), (3, rows_of(scratch[:, 7168 - 2 * HALF:]))]]
        BESIDE = {1: {(0, 0): EXTRA[0], (0, 1): EXTRA[1], (1, 0): EXTRA[2]},
                  2: {(2, e): EXTRA_DOWN[e] for e in range(2)}}
        SB_ADD = bias[:, 8:10, :].rearrange("p a s -> p (a s)")[:, 0:384]
        SB_NEG = bias[:, 10:12, :].rearrange("p a s -> p (a s)")[:, 0:384]
        NL = NGRP + NEXP
        lgT = [mix[0:NL, 0, half * S:(half + 1) * S] for half in range(2)]
        stage = kT[:, 0:2, :].rearrange("p k s -> p (k s)")[:, 0:384].rearrange("p (a b) -> p a b", a=3)

        PS = [ctx.enter_context(nc.psum_tensor(f"bank{i}", [P, HALF], f32)) for i in range(8)]

        R_C, R_PRE, R_FPRE, R_MIX, R_FFN, R_SWA, R_DIL, R_SB, R_SUB = 0, 8, 16, 24, 32, 40, 44, 48, 52

        loaded = [sem(f"loaded{i}") for i in range(SLOT_N)]
        s_x = [sem(f"s_x{t}") for t in range(T)]
        s_stage = sem("s_stage")
        s_rows = sem("s_rows")
        s_sink = sem("s_sink")
        s_lamv = sem("s_lamv")
        s_const = sem("s_const")
        s_mask = sem("s_mask")
        s_qzero = sem("s_qzero")
        s_pool = sem("s_pool")
        s_vecT = sem("s_vecT")
        s_vec = sem("s_vec")
        s_lamx = sem("s_lamx")
        s_lame = sem("s_lame")
        s_c = sem("s_c")
        s_ms = sem("s_ms")
        s_rs = sem("s_rs")
        s_link = sem("s_link")
        s_alink = sem("s_alink")
        s_whi = sem("s_whi")
        s_wloP = sem("s_wloP")
        s_wloV = sem("s_wloV")
        s_hhiV = sem("s_hhiV")
        s_hhi = {t: sem("s_hhi_" + t) for t in ("attn1", "mix1", "ffn", "attn2", "mix2")}
        s_shift = sem("s_shift")
        s_prod = sem("s_prod")
        s_ahi = sem("s_ahi")
        TURNS = ["attn1", "mix1", "ffn", "attn2", "mix2", "moe"]
        s_src = {t: sem("s_src_" + t) for t in TURNS}
        s_turn = {t: sem("s_turn_" + t) for t in TURNS}
        s_hT = {t: sem("s_hT_" + t) for t in TURNS}
        s_gemm = [sem("s_gemm1"), sem("s_gemm2")]
        s_evA = [sem("s_evA1"), sem("s_evA2")]
        s_evV = [sem("s_evV1"), sem("s_evV2")]
        s_sc = [sem("s_sc1"), sem("s_sc2")]
        s_log = [sem("s_log1"), sem("s_log2")]
        s_max = [sem("s_max1"), sem("s_max2")]
        s_exp = [sem("s_exp1"), sem("s_exp2")]
        s_dif = sem("s_dif")
        s_tr = [sem("s_tr1"), sem("s_tr2")]
        s_pt = [sem("s_pt1"), sem("s_pt2")]
        s_pv = [sem("s_pv1"), sem("s_pv2")]
        s_hsq = sem("s_hsq")
        s_sk = sem("s_sk")
        s_ske = sem("s_ske")
        s_done = [sem("s_done1"), sem("s_done2")]
        s_mixed = sem("s_mixed")
        s_proj = [sem("s_proj1"), sem("s_proj2")]
        s_half = sem("s_half")
        s_xsum = sem("s_xsum")
        s_sq = [sem("s_sq1"), sem("s_sq2"), sem("s_sq3")]
        s_up = sem("s_up")
        s_tap = sem("s_tap")
        s_cv1 = sem("s_cv1")
        s_conv = sem("s_conv")
        s_sum = sem("s_sum")
        s_gelu = sem("s_gelu")
        s_act = sem("s_act")
        s_down = sem("s_down")
        s_bank = sem("s_bank")
        s_rfree = sem("s_rfree")
        s_adab = [sem("s_adab0"), sem("s_adab1")]
        s_ada0 = sem("s_ada0")
        s_adam = sem("s_adam")
        s_mod = sem("s_mod")
        s_modc = sem("s_modc")
        s_bias2 = sem("s_bias2")
        s_z = sem("s_z")
        s_zm = sem("s_zm")
        s_sb1 = sem("s_sb1")
        s_lk = sem("s_lk")
        s_R = sem("s_R")
        s_t = sem("s_t")
        s_w = sem("s_w")
        s_sbo = sem("s_sbo")
        s_wr = sem("s_wr")
        s_back = sem("s_back")
        s_h2 = sem("s_h2")
        s_lg = sem("s_lg")
        s_lgT = sem("s_lgT")
        s_hTA = sem("s_hTA")
        s_lg2 = sem("s_lg2")
        s_counts = sem("s_counts")
        s_r1 = sem("s_r1")
        s_r2 = sem("s_r2")
        s_A = sem("s_A")
        s_rank = sem("s_rank")
        s_np = sem("s_np")
        s_oneh = sem("s_oneh")
        s_onehw = sem("s_onehw")
        s_dispA = sem("s_dispA")
        s_disp = sem("s_disp")
        s_xeA = sem("s_xeA")
        s_xeV = sem("s_xeV")
        s_eg = sem("s_eg")
        s_eu = sem("s_eu")
        s_silu = sem("s_silu")
        s_eact = sem("s_eact")
        s_etr = sem("s_etr")
        s_eactT = sem("s_eactT")
        s_ctr = sem("s_ctr")
        s_combT = sem("s_combT")
        s_edn = sem("s_edn")
        s_yA = sem("s_yA")
        s_yV = sem("s_yV")
        s_comb = sem("s_comb")
        s_comb_last = sem("s_comb_last")
        s_fin = sem("s_fin")
        s_extra = [sem(f"s_extra{n}") for n in range(len(EXTRA))]
        s_out = [sem(f"s_out{t}") for t in range(T)]

        def chunk_view(slot):
            return ring[:, slot, :].rearrange("p (k n) -> p k n", n=HALF)

        def split_view(lane, n=HALF):
            return [ring_r[:, place, :].rearrange("p (k n) -> p k n", n=n) for place in (LANES + lane, lane)]

        def split_part(n, part):
            lane = n % LANES

            def view(tensor, place):
                if n == N_IN + IN_CHUNKS - 1:
                    tiles = tensor[:, place, :].rearrange("p (k n) -> p k n", n=HALF)
                    return tiles[:, part * KD // 2:(part + 1) * KD // 2, 0:S]
                cut = POOL_SHARE[n] if 0 < POOL_SHARE[n] < SLOT_W else SLOT_W // 2
                a0, a1 = ((0, cut), (cut, SLOT_W))[part]
                return tensor[:, place, a0:a1]

            return view(ring, lane), view(ring_r, LANES + lane), view(ring_r, lane)

        def parts_of(n):
            cut = 0 if POOL_SHARE[n] == 0 else 2 if POOL_SHARE[n] == SLOT_W else 1
            return (0, 1)[:cut], (0, 1)[cut:]

        def split_by(engine, n):
            return sum(len(parts_of(m)[engine]) > 0 for m in range(n + 1))

        QB0 = SWA_Q * HD + 2 * SWA_KV * HD
        KB0 = QB0 + DIFF_H * P
        items1 = [(0, "q", ("pair", j * P, 2 * j)) for j in range(4)]
        items1 += [(1, "ka", (0, 0)), (1, "v", (P, P, 0))]
        for pair_of in range(2):
            for h in (2 * pair_of, 2 * pair_of + 1):
                items1.append(((QB0 + h * P) // HALF, "q", ("pair", (QB0 + h * P) % HALF, 8 + 2 * h)))
                items1.append(((KB0 + h * P) // HALF, "k", ((KB0 + h * P) % HALF, 1 + h)))
            items1.append((3 + pair_of, "v", (S * (1 - pair_of), S, P + S * pair_of)))
        items2 = []
        for part in range(2):
            mine = 1 - part
            items2 += [(3 * part, "q", ("pair", j * P, 8 * mine + 2 * j)) for j in range(4)]
            items2 += [(3 * part + 1, "k", (j * P, 4 * mine + j)) for j in range(4)]
            items2 += [(3 * part + 2, "vt", (t, HALF * mine)) for t in range(T)]
        ITEMS = [items1, items2]
        AHEAD = [6, 10]

        def item_bank(blk, n):
            return PS[(4 + n) % 8] if n < AHEAD[blk] else PS[6 + n % 2]

        def item_waits(blk, n):
            return n - 8 if n < AHEAD[blk] else n - 2 if n >= AHEAD[blk] + 2 else None

        BETWEEN = [{0: [6], 1: [7], 2: [8], 3: [9], 4: [10], 5: [11], 6: [12], 7: [13, 14], 8: [15]},
                   {0: [10, 11], 1: [12], 2: [13], 3: [14], 4: [15, 16], 5: [17], 6: [18], 7: [19]}]

        SPLITS = [{1: (N_IN + 3, 0), 2: (N_IN + 3, 1), 4: (N_IN + 4, 0), 5: (N_IN + 4, 1), 8: (N_OUT, 0),
                   9: (N_OUT, 1)},
                  {0: (N_IN2 + 4, 0), 1: (N_IN2 + 4, 1), 2: (N_IN2 + 5, 0), 3: (N_IN2 + 5, 1), 5: (N_OUT2, 0),
                   6: (N_OUT2, 1), 7: (N_OUT2 + 1, 0), 8: (N_OUT2 + 1, 1)}]

        def consumed(n):
            if n < N_OUT:
                return s_gemm[0], 1 + max(m for m, it in enumerate(items1) if it[0] <= n - N_IN)
            if n < N_FFN:
                return s_proj[0], 2 * (T - 1) + n - N_OUT + 1
            if n < N_IN2:
                for i in range(CHUNKS):
                    if n in (seq_gate(i), seq_gate(i) + 1):
                        return s_up, 4 * i + 2 * (n - seq_gate(i) + 1)
                    if n == seq_down(i):
                        return (s_down, i + 1) if i < CHUNKS - 1 else (s_bank, 2 * T)
            if n < N_OUT2:
                return s_gemm[1], 1 + max(m for m, it in enumerate(items2) if it[0] <= n - N_IN2)
            return s_proj[1], 2 * (T - 1) + n - N_OUT2 + 1

        def expert_slot(c, e):
            return c + LANES * e

        def expert_loads(c, e):
            return 0 if e else N_MOE // LANES

        KA = (0, 5)

        def unit(kind, t, maps):
            return dict(kind=kind, t=t, maps=maps, w=P * (t + 1))
        swa_unit = lambda h: dict(q=h, k=KA[h // 4], b=h, v=(h // 4) * HD, vw=HD, o=h * HD, h=h)
        diff_unit = lambda h, m: dict(q=8 + 2 * h + m, k=1 + h, b=8 + h, v=128 + h * 128, vw=128, o=h * 128, h=h)
        dil_unit = lambda h: dict(q=h, k=h // 2, b=h, v=h * HD, vw=HD, o=h * HD, h=h)
        units1 = [unit("swa", 0, [swa_unit(h) for h in range(4 * u, 4 * u + 4)]) for u in range(2)]
        units1 += [unit("swa", 1, [swa_unit(2 * u), swa_unit(2 * u + 1)]) for u in range(4)]
        for u in range(2):
            units1.append(unit("diff", 0, [diff_unit(2 * u + i // 2, i % 2) for i in range(4)]))
            units1 += [unit("diff", 1, [diff_unit(h, 0), diff_unit(h, 1)]) for h in (2 * u, 2 * u + 1)]
        units2 = [unit("dil", 0, [dil_unit(h) for h in range(4 * u, 4 * u + 4)]) for u in range(2)]
        units2 += [unit("dil", 1, [dil_unit(2 * u), dil_unit(2 * u + 1)]) for u in range(4)]
        UNITS = [units1, units2]

        def row_of(u):
            return (2 if u["kind"] == "diff" else 0) + u["t"]

        def col_of(u):
            m = u["maps"][0]
            return (4 * (m["h"] // 2) if u["t"] == 0 else 2 * m["h"]) if u["kind"] == "diff" else m["h"]

        def out_bank(u):
            return PS[(6 if u["kind"] == "dil" else 4) + u["t"]]

        def needs(blk, i, values=False):
            if blk == 1:
                return len(items2)
            return AHEAD[0] + (5 * ((i - 3) // 3) - (0 if values else 1) if i >= 6 else 0)

        def turned(u):
            maps = u["maps"][0::2] if u["kind"] == "diff" else u["maps"]
            return [(i * u["w"] + kb * P, kb, m) for i, m in enumerate(maps) for kb in range(u["t"] + 1)]

        def finishes(blk):
            last = {}
            for n, u in enumerate(UNITS[blk]):
                last[(u["kind"], u["t"])] = n
            return last

        def taken(blk, kind, where, bank):
            if kind == "q":
                return [(qz[HD * g:HD * g + HD, where[2] + g, :], bank[HD * g:HD * g + HD, 0:S]) for g in range(2)]
            if kind == "ka":
                return [(kT[HD * half:HD * half + HD, KA[g], :], bank[HD * g:HD * g + HD, 0:S])
                        for g in range(2) for half in range(2)]
            if kind == "k":
                return [(kT[:, where[1], :], bank[:, 0:S])]
            if kind == "v":
                _, cw, c0 = where
                return [(vt[:, :, c0:c0 + cw], bank[:, 0:T * cw].rearrange("p (t n) -> p t n", t=T))]
            t, c0 = where
            return [(vt[:, t, c0:c0 + HALF], bank[:, :])]

        block = ctx.enter_context(nc.Block())

        @block.sync
        def _(sp):
            w_in = a["w_in"].rearrange("o (k p) n -> p (o k) n", p=P)
            w_ada = a["w_ada_2"].rearrange("o (k p) n -> p (o k) n", p=P)
            w_out = a["w_out"].rearrange("o (k p) n -> p (o k) n", p=P)
            w_up = a["w_up"].rearrange("o (k p) n -> p (o k) n", p=P)
            w_down = a["w_down"].rearrange("o (k p) n -> p (o k) n", p=P)
            w_in2 = a["w_in_2"].rearrange("o (k p) n -> p (o k) n", p=P)
            w_out2 = a["w_out_2"].rearrange("o (k p) n -> p (o k) n", p=P)
            w_gate = a["w_gate_2"].rearrange("o e (k p) n -> p (o e) k n", p=P)
            w_eup = a["w_up_2"].rearrange("o e (k p) n -> p (o e) k n", p=P)
            w_edown = a["w_down_2"].rearrange("o e (k p) n -> p (o e) k n", p=P)

            def load(slot, src, free):
                if free is not None:
                    sp.wait_ge(*free)
                dst = ring[:, slot, :].rearrange("p (k n) -> p k n", k=src.shape[1])
                if src.shape[2] < dst.shape[2]:
                    dst = dst[:, :, 0:src.shape[2]]
                sp.dma_start(dst, src).then_inc(loaded[slot], 16)

            def straight(n, src):
                load(n % LANES, src, consumed(n - LANES) if n >= LANES else None)

            xr = a["x"].rearrange("o (t p) d -> p (o t) d", p=P)
            for t in range(T):
                sp.dma_start(x[:, t, :], xr[:, t, :]).then_inc(s_x[t], 16)
            for c in range(IN_CHUNKS):
                if c == 1:
                    sp.wait_ge(s_stage, 16 * 12)
                    sp.wait_ge(s_lamv, 16 * 4)
                    sp.wait_ge(s_sink, 16)
                straight(N_IN + c, w_in[:, :, c * HALF:min((c + 1) * HALF, w_in.shape[2])])
            for c in range(2):
                straight(N_OUT + c, w_out[:, :, c * HALF:(c + 1) * HALF])
            for c in range(2):
                straight(N_FFN + c, w_up[:, :, c * FF:c * FF + HALF])

            def ffn_chunks(i):
                return (w_up[:, :, ds(i * HALF, HALF)], w_up[:, :, ds(FF + i * HALF, HALF)],
                        w_down[:, ds((i - 1) * KE, KE), :])

            def modulation(r, *units):
                for c in units:
                    sp.wait_ge(s_sum, 4 * (ADA_EACH * r + c) + 4)
                    sp.dma_start(ada_buf[:, c % 2, :, :],
                                 w_ada[:, 2 * (c % 4):2 * (c % 4) + 2, ds(1024 * r + 2 * ADA_W * (c // 4), 2 * ADA_W)])\
                        .then_inc(s_adab[c % 2], 16)

            for c, src in enumerate(ffn_chunks(1)):
                straight(seq_gate(1) + c, src)
            modulation(0, 0, 1, 2, 3)
            due = ((4, 5), (6, 7), (0, 1, 2, 3))
            with sp.Fori(2, CHUNKS - 1) as i:
                for c, (src, free) in enumerate(zip(ffn_chunks(i), ((s_up, 4 * (i - 1) + 2), (s_up, 4 * (i - 1) + 4),
                                                                    (s_down, i - 1)))):
                    load((seq_gate(1) + c) % LANES, src, free)
                    modulation(i - 2 if c < 2 else i - 1, *due[c])
            for c, src in enumerate(ffn_chunks(CHUNKS - 1)):
                straight(seq_gate(CHUNKS - 1) + c, src)
                if c < 2:
                    modulation(CHUNKS - 3, *due[c])
            straight(seq_down(CHUNKS - 1), w_down[:, (CHUNKS - 1) * KE:CHUNKS * KE, :])
            for c in range(IN2_CHUNKS):
                first = (c + IN2_CHUNKS // 2) % IN2_CHUNKS * HALF
                straight(N_IN2 + c, w_in2[:, :, first:first + HALF])
            for c in range(2):
                straight(N_OUT2 + c, w_out2[:, :, c * HALF:(c + 1) * HALF])

            def expert_load(p, q, c, free, experts=(0, 1)):
                w = (w_gate, w_eup, w_edown)[c]
                for e in experts:
                    load(expert_slot(c, e), w[:, ds(2 * q + e, 1), :, :].rearrange("p o k n -> p (o k) n"), free)

            def extra_load(m):
                src = (w_gate[:, 2, :, :], w_gate[:, 3, :, :], w_eup[:, 2, :, :])[m]
                for n, (k0, place) in enumerate(EXTRA[m]):
                    k1 = EXTRA[m][n + 1][0] if n + 1 < len(EXTRA[m]) else KD
                    sp.dma_start(place[:, 0:k1 - k0, :], src[:, k0:k1, :]).then_inc(s_extra[m], 16)

            def extra_down(e):
                for n, (k0, place) in enumerate(EXTRA_DOWN[e]):
                    k1 = EXTRA_DOWN[e][n + 1][0] if n + 1 < len(EXTRA_DOWN[e]) else KE
                    sp.dma_start(place[:, 0:k1 - k0, :], w_edown[:, 4 + e, k0:k1, :]).then_inc(s_extra[e], 16)

            expert_load(0, 0, 0, consumed(N_MOE - LANES))
            sp.wait_ge(s_src["mix2"], T)
            extra_load(0)
            for c in (1, 2):
                expert_load(0, 0, c, consumed(N_MOE - LANES + c))
            sp.wait_ge(s_proj[1], 2 * T)
            sp.wait_ge(s_mixed, 1)
            extra_load(1)
            sp.wait_ge(s_back, 4)
            extra_load(2)
            expert_load(2, 2, 0, (s_eg, 1))
            expert_load(1, 1, 1, (s_eu, 1), experts=(1,))
            expert_load(2, 2, 1, (s_eu, 1), experts=(0,))
            expert_load(1, 1, 2, (s_edn, 1))
            sp.wait_ge(s_eg, 2)
            for e in range(2):
                extra_down(e)
            expert_load(2, 2, 1, (s_eu, 2), experts=(1,))
            expert_load(3, 3, 2, (s_edn, 2))
            expert_load(3, 3, 0, (s_eg, 3))
            expert_load(3, 3, 1, (s_eu, 3))
            with sp.Fori(4, PAIRS - 1) as p:
                for c, used in enumerate((s_eg, s_eu, s_edn)):
                    expert_load(p, p, c, (used, p))
            expert_load(PAIRS - 1, PAIRS - 1, 0, (s_eg, PAIRS - 1))
            expert_load(PAIRS - 1, PAIRS - 1, 1, (s_eu, PAIRS - 1))
            expert_load(PAIRS - 1, PAIRS - 1, 2, (s_edn, PAIRS - 1), experts=(0,))
            dst = ring[:, expert_slot(2, 1), :].rearrange("p (k n) -> p k n", k=KE)
            for half, done in enumerate((s_half, loaded[expert_slot(2, 1)])):
                tiles = slice(half * KE // 2, (half + 1) * KE // 2)
                sp.dma_start(dst[:, tiles, :], w_edown[:, 2 * PAIRS - 1, tiles, :]).then_inc(done, 16)
            sp.wait_ge(s_np, 1)
            n_pairs = sp.value_load(n_pairs_i[0:1, 0:1], min_val=PAIRS, max_val=PAIRS * PASSES)
            with sp.If(n_pairs > PAIRS):
                with sp.Fori(1, PASSES) as r:
                    with sp.Fori(0, PAIRS) as q:
                        for c, done in enumerate((s_eg, s_eu, s_edn)):
                            expert_load(r * PAIRS + q, q, c, (done, r * PAIRS + q))
            rows = out.rearrange("o (t p) d -> p (o t) d", p=P)
            for t in range(T):
                sp.wait_ge(s_fin, t + 1)
                sp.dma_start(rows[:, t, :], hn[:, t, :]).then_inc(s_out[t], 16)
            for t in range(T):
                sp.wait_ge(s_out[t], 16)

        @block.gpsimd
        def _(pool):
            step = [0]
            norms = [0]

            def inverse_roots(count):
                for _ in range(count):
                    first, w = ROOTS[norms[0]]
                    norms[0] += 1
                    pool.wait_ge(s_ms, norms[0])
                    pool.tensor_tensor(rstd[:, first:first + w], ms[:, first:first + w], minus_half[:, 0:w],
                                       ALU.pow).then_inc(s_rs, 1)

            def then(ins):
                step[0] += 1
                ins.then_inc(s_pool, 1)
                pool.wait_ge(s_pool, step[0])

            def split(n, more=0):
                for part in parts_of(n)[0]:
                    pool.wait_ge(s_whi, 2 * n + 1 + part + 2 * more)
                    raw, hi, lo = split_part(n, part)
                    last = pool.tensor_tensor(lo, raw, hi, ALU.subtract)
                last.then_inc(s_wloP, 1)

            pool.memset(minus_half, -0.5)
            then(pool.memset(ident[:, :], 0.0))
            pool.affine_select(out=ident[:, :], in_=ident[:, :], compare_op=ALU.not_equal, fill=1.0, base=0,
                               pattern=[[-1, P]], channel_multiplier=1).then_inc(s_const, 1)
            pool.memset(ones[:, :], 1.0).then_inc(s_const, 1)
            pool.memset(zrow[:, :], 0.0).then_inc(s_const, 1)
            inverse_roots(T)
            pool.memset(qz[:, :, :], 0.0).then_inc(s_qzero, 1)
            split(N_IN)
            then(pool.memset(from_here[:, :], 1.0))
            pool.affine_select(out=from_here[:, :], in_=from_here[:, :], compare_op=ALU.is_ge, fill=0.0, base=0,
                               pattern=[[-1, P]], channel_multiplier=1).then_inc(s_const, 1)
            then(pool.memset(before[:, :], 1.0))
            pool.affine_select(out=before[:, :], in_=before[:, :], compare_op=ALU.is_gt, fill=0.0, base=0,
                               pattern=[[1, P]], channel_multiplier=-1).then_inc(s_const, 1)
            pool.iota(iota[:, :], [[1, SLOTS]], base=0, channel_multiplier=0,
                      allow_small_or_imprecise_dtypes=True).then_inc(s_const, 1)
            then(pool.iota(negdist[:, :], [[1, S]], base=-P, channel_multiplier=-1,
                           allow_small_or_imprecise_dtypes=True))
            for h in range(SWA_Q):
                pool.tensor_scalar(bias[:, h, :], negdist[:, :], float(np.float32(swa_slopes[h])), None, ALU.mult)
            for h in range(DIFF_H):
                last = pool.tensor_scalar(bias[:, SWA_Q + h, :], negdist[:, :], float(np.float32(diff_slopes[h])),
                                          None, ALU.mult)
            then(last)
            then(pool.affine_select(out=bias[:, :, :], in_=bias[:, :, :], compare_op=ALU.is_ge, fill=NEG, base=P,
                                    pattern=[[0, 12], [-1, S]], channel_multiplier=1))
            pool.affine_select(out=bias[:, 0:SWA_Q, :], in_=bias[:, 0:SWA_Q, :], compare_op=ALU.is_ge, fill=NEG,
                               base=WINDOW - 1 - P, pattern=[[0, SWA_Q], [1, S]],
                               channel_multiplier=-1).then_inc(s_mask, 1)
            pool.dma_start(post_attn[:, :], a["attn_post_g"][0].partition_broadcast(P)).then_inc(s_rows, 16)
            pool.dma_start(post_ffn[:, :], a["ffn_post_g"][0].partition_broadcast(P)).then_inc(s_rows, 16)
            for n in range(N_IN + 3, N_OUT + 1):
                split(n)
            inverse_roots(T)
            split(N_OUT + 1)
            split(N_FFN)
            inverse_roots(2 * T)
            split(seq_gate(0) + 1)
            pool.wait_ge(s_src["mix1"], T)
            then(pool.memset(ada, 0.0))
            pool.dma_start(ada[0:1, :], a["b_ada_2"]).then_inc(s_ada0, 16)
            then(pool.memset(SB_ADD, 0.0))
            then(pool.memset(SB_NEG, -1.0))
            for m, fill in ((SB_ADD, NEG), (SB_NEG, 0.0)):
                for c in (0, 256):
                    then(pool.affine_select(out=m[:, c:c + P], in_=m[:, c:c + P], compare_op=ALU.is_gt, fill=fill,
                                            base=0, pattern=[[1, P]], channel_multiplier=-1))
            pool.memset(tiny, 0.0).then_inc(s_bias2, 1)

            split(seq_gate(1))
            split(seq_gate(1) + 1)
            with pool.Fori(1, CHUNKS - 1) as i:
                split(seq_gate(1) + 2, 3 * (i - 1))
                split(seq_gate(2), 3 * (i - 1))
                split(seq_gate(2) + 1, 3 * (i - 1))
            for n in range(seq_gate(CHUNKS - 1) + 2, N_IN2 + 1):
                split(n)
            inverse_roots(2 * T)
            pool.wait_ge(s_adam, 6)
            pool.memset(qz[:, :, :], 0.0).then_inc(s_qzero, 1)
            for n in range(N_IN2 + 1, N_MOE):
                split(n)
            inverse_roots(T)
            pool.wait_ge(s_mixed, 1)
            pool.dma_start(wr[:, :, 0:NGRP], a["w_group_2"].rearrange("o (k p) n -> p (o k) n", p=P),
                           allow_slow_non_contiguous=True).then_inc(s_wr, 16)
            pool.dma_start(wr[:, :, NGRP:NGRP + NEXP], a["w_expert_2"].rearrange("o (k p) n -> p (o k) n", p=P),
                           allow_slow_non_contiguous=True).then_inc(s_wr, 16)
            pool.wait_ge(s_mixed, 1)
            pool.dma_start(final_g[:, :], a["g_final_2"].partition_broadcast(P)).then_inc(s_rows, 16)
            inverse_roots(2 * T)

        @block.tensor
        def _(pe):
            def turn(tag, src):
                for t in range(T):
                    pe.wait_ge(s_src[tag], t + 1)
                    for k in range(KD):
                        c = (k % 2) * S + t * P
                        last = pe.transpose(PS[k // 2][:, c:c + P], src[:, t, k * P:(k + 1) * P], ident[:, :])
                        if k % 2 and t == T - 1:
                            last.then_inc(s_turn[tag], 1)

            def split_ready(n, more=0):
                for engine, done in enumerate((s_wloP, s_wloV)):
                    if parts_of(n)[engine]:
                        pe.wait_ge(done, split_by(engine, n) + more)

            def product(dst, lhs, rhs, start, stop, **flags):
                pe.matmul(dst, lhs[0], rhs[0], start=start, stop=False, **flags)
                pe.matmul(dst, lhs[0], rhs[1], start=False, stop=False, **flags)
                return pe.matmul(dst, lhs[1], rhs[0], start=False, stop=stop, **flags)

            def tiles(tag, k, n0=0, n=S):
                return [hi_T[:, k, n0:n0 + n], lo_T[tag][:, k, n0:n0 + n]]

            def both(w, k, c0, n):
                return [v[:, k, c0:c0 + n] for v in w]

            def piece_taken(blk, n):
                pe.wait_ge(s_evA[blk], (n + 1) // 2)
                pe.wait_ge(s_evV[blk], n // 2)

            def project(blk, n_base, n):
                items = ITEMS[blk]
                c, kind, where = items[n]
                tag = ("attn1", "attn2")[blk]
                split_ready(n_base + c)
                bank = item_bank(blk, n)
                w = split_view((n_base + c) % LANES)
                m = item_waits(blk, n)
                if m is not None and m >= 0:
                    pe.wait_ge((s_evA, s_evV)[m % 2][blk], m // 2 + 1)
                for k in range(KD):
                    if n == 0:
                        pe.wait_ge(s_hT[tag], k + 1)
                    flags = dict(start=(k == 0), stop=(k == KD - 1))
                    if kind in ("q", "k", "ka"):
                        c0 = where[1] if kind == "q" else where[0]
                        last = product(bank[:, 0:S], both(w, k, c0, P), tiles(tag, k), **flags)
                    elif kind == "vt":
                        last = product(bank[:, :], tiles(tag, k, where[0] * P, P), both(w, k, 0, HALF), **flags)
                if kind == "v":
                    c0, cw, _ = where
                    for t in range(T):
                        for k in range(KD):
                            last = product(bank[:, t * cw:(t + 1) * cw], tiles(tag, k, t * P, P), both(w, k, c0, cw),
                                           start=(k == 0), stop=(k == KD - 1))
                last.then_inc(s_gemm[blk], 1)

            def attention(blk, n_base, fill):
                units = UNITS[blk]

                def scores(i):
                    u = units[i]
                    if i == 0 or needs(blk, i) > needs(blk, i - 1):
                        piece_taken(blk, needs(blk, i))
                    if i >= 2:
                        pe.wait_ge(s_log[blk], i - 1)
                    for j, m in enumerate(u["maps"]):
                        last = pe.matmul(PS[i % 2][:, j * u["w"]:(j + 1) * u["w"]],
                                         qz[:, m["q"], u["t"] * P:(u["t"] + 1) * P], kT[:, m["k"], 0:u["w"]],
                                         start=True, stop=True)
                    last.then_inc(s_sc[blk], 1)

                scores(0)
                for i in range(len(units) + 2):
                    if i + 1 < len(units):
                        scores(i + 1)
                    if 1 <= i <= len(units):
                        n = i - 1
                        u = units[n]
                        if u["kind"] == "diff":
                            pe.wait_ge(s_dif, n - len(units) // 2 + 1)
                        else:
                            pe.wait_ge(s_exp[blk], n + 1)
                        if n >= 2:
                            pe.wait_ge(s_pt[blk], n - 1)
                        for b, (c, kb, m) in enumerate(turned(u)):
                            last = pe.transpose(PS[2 + n % 2][:, b * P:(b + 1) * P], Eb[:, n % 2, c:c + P],
                                                ident[:, :])
                        last.then_inc(s_tr[blk], 1)
                    if i >= 2:
                        n = i - 2
                        u = units[n]
                        pe.wait_ge(s_pt[blk], n + 1)
                        if blk == 0 and n in (6, 9):
                            piece_taken(blk, needs(blk, n, values=True))
                        if u["kind"] == "diff":
                            pe.wait_ge(s_done[blk], u["t"] + 1)
                        for b, (c, kb, m) in enumerate(turned(u)):
                            last = pe.matmul(out_bank(u)[:, m["o"]:m["o"] + m["vw"]], PT[:, n % 2, b * P:(b + 1) * P],
                                             vt[:, kb, m["v"]:m["v"] + m["vw"]],
                                             start=(kb == 0), stop=(kb == u["t"]))
                        last.then_inc(s_pv[blk], 1)
                    for n in fill.get(i, []):
                        project(blk, n_base, n)

            def out_projection(blk, n_base):
                tag = ("mix1", "mix2")[blk]
                for t in range(T):
                    for c in range(2):
                        split_ready(n_base + c)
                        w = split_view((n_base + c) % LANES)
                        for k in range(KD):
                            if t == 0 and c == 0:
                                pe.wait_ge(s_hT[tag], k + 1)
                            last = product(PS[4 + 2 * t + c][:, :], tiles(tag, k, t * P, P), both(w, k, 0, HALF),
                                           start=(k == 0), stop=(k == KD - 1))
                        last.then_inc(s_proj[blk], 1)

            pe.wait_ge(s_const, 1)
            turn("attn1", hn)
            pe.wait_ge(s_stage, 16 * 12)
            pe.transpose(PS[7][:, 0:P], stage[:, 0, :], ident[:, :])
            pe.transpose(PS[7][:, P:2 * P], stage[:, 1, :], ident[:, :])
            pe.transpose(PS[7][:, 2 * P:2 * P + 53], stage[0:53, 2, :], ident[0:53, 0:53]).then_inc(s_vecT, 1)
            pe.wait_ge(s_vec, 1)
            for n in range(AHEAD[0]):
                project(0, N_IN, n)
            attention(0, N_IN, BETWEEN[0])
            turn("mix1", mix)
            out_projection(0, N_OUT)
            turn("ffn", hn)

            def zero_sums():
                for b in range(4, 8):
                    pe.matmul(PS[b][:, :], zrow[:, 0:P], zrow[:, :], start=True, stop=False, skip_group_check=True)

            def up(i, n, more=0):
                for part in range(2):
                    split_ready(n + part, more)
                    w = split_view((n + part) % LANES)
                    for b in range(2):
                        if not isinstance(i, int):
                            pe.wait_ge(s_conv, 4 * (i - 1) + 2 * part + b + 1)
                        for f in range(2):
                            c = (2 * b + f) * P
                            for k in range(KD):
                                if isinstance(i, int) and part == b == f == 0:
                                    pe.wait_ge(s_hT["ffn"], max(k + 1, 2))
                                last = product(PS[2 * part + b][:, f * S:(f + 1) * S], both(w, k, c, P),
                                               tiles("ffn", k), start=(k == 0), stop=(k == KD - 1))
                        last.then_inc(s_up, 1)

            def down(i, n, more=0, bank_done=None):
                split_ready(n, more)
                pe.wait_ge(s_act, i + 1)
                w = split_view(n % LANES, D)
                for t in range(T):
                    for c in range(2):
                        for k in range(KE):
                            rows = [act_r[:, h, k, t * P:(t + 1) * P] for h in range(2)]
                            last = product(PS[4 + 2 * t + c][:, :], rows, both(w, k, c * HALF, HALF),
                                           start=False, stop=False, skip_group_check=True)
                        if bank_done is not None:
                            last.then_inc(bank_done, 1)
                if bank_done is None:
                    last.then_inc(s_down, 1)

            pe.wait_ge(s_const, 6)
            up(0, seq_gate(0))
            zero_sums()
            with pe.Fori(1, CHUNKS) as i:
                up(i, seq_gate(1), 3 * (i - 1))
                down(i - 1, seq_down(0), 3 * (i - 1))

            pe.wait_ge(s_sum, 4 * ADA_UNITS + 8)
            pe.wait_ge(s_conv, 4 * CHUNKS)
            def columns(parts, bank):
                for n, part in enumerate(parts):
                    for k in range(KD):
                        c = part * D + k * P
                        last = pe.matmul(bank[:, n * KD + k:n * KD + k + 1], ada[:, c:c + P], ones[:, 0:1],
                                         start=True, stop=True)
                last.then_inc(s_adam, 1)

            def gate_rows(n):
                c = (2, 5)[n // 2] * D + (n % 2) * HALF
                pe.matmul(PS[(1, 2, 3, 0)[n]][:, :], ones[:, :], ada[:, c:c + HALF],
                          start=True, stop=True).then_inc(s_adam, 1)

            columns((0, 1), PS[0])
            down(CHUNKS - 1, seq_down(CHUNKS - 1), bank_done=s_bank)
            for n in range(4):
                if n == 3:
                    pe.wait_ge(s_mod, 1)
                gate_rows(n)
            pe.wait_ge(s_mod, 2)
            columns((3, 4), PS[1])

            pe.wait_ge(s_mod, 6)
            turn("attn2", rows2)
            for n in range(AHEAD[1]):
                project(1, N_IN2, n)

            piece_taken(1, AHEAD[1])
            def scores(n):
                if n >= 2:
                    pe.wait_ge(s_zm, n - 1)
                z = PS[n % 2]
                pe.matmul(z[:, 0:S], kT[:, 4 + n // 2, 0:P], qz[:, 8 + n, :], start=True, stop=True)
                pe.matmul(z[:, S:S + P], kT[:, 4 + n // 2, P:S], qz[:, 8 + n, P:S],
                          start=True, stop=True).then_inc(s_z, 1)

            scores(0)
            for i in range(SB_H + 2):
                if i + 1 < SB_H:
                    scores(i + 1)
                if 1 <= i <= SB_H:
                    n = i - 1
                    pe.wait_ge(s_lk, n + 1)
                    R = PS[2 + n % 2]
                    lk = Eb[:, n % 2, :]
                    pe.matmul(R[:, 0:S], from_here[:, :], lk[:, 0:S], start=True, stop=False)
                    pe.matmul(R[:, P:S], ones[:, :], lk[:, S:S + P], start=False, stop=True)
                    pe.matmul(R[:, S:S + P], from_here[:, :], lk[:, S:S + P], start=True, stop=True).then_inc(s_R, 1)
                if i >= 2:
                    n = i - 2
                    pe.wait_ge(s_w, n + 1)
                    w = PT[:, n % 2, :]
                    c = n * HD
                    v = lambda kb: vt[:, kb, HALF + c:HALF + c + HD]
                    pe.matmul(PS[4][:, c:c + HD], w[:, 0:P], v(0), start=True, stop=True)
                    pe.matmul(PS[5][:, c:c + HD], w[:, P:S], v(0), start=True, stop=False)
                    pe.matmul(PS[5][:, c:c + HD], w[:, S:S + P], v(1), start=False, stop=True).then_inc(s_sbo, 1)
                for n in BETWEEN[1].get(i, []):
                    project(1, N_IN2, n)

            attention(1, N_IN2, {})
            turn("mix2", mix)
            out_projection(1, N_OUT2)
            turn("moe", hn)

            pe.wait_ge(s_wr, 32)
            for n in range(KD // 2):
                for half, done in enumerate((s_hT["moe"], s_hTA)):
                    pe.wait_ge(done, n + 1)
                    k = 4 * (n // 2) + n % 2 + 2 * half
                    last = pe.matmul(PS[4][64 * half:64 * half + NL, 0:S], wr[:, k, :], hT[:, k, :], start=(n == 0),
                                     stop=(n == KD // 2 - 1))
            last.then_inc(s_lg, 1)

            def back(t, half):
                for k in range(4 * half, 4 * half + 4):
                    last = pe.transpose(PS[2 * t + half][:, (k % 4) * P:(k % 4 + 1) * P], hT[:, k, t * P:(t + 1) * P],
                                        ident[:, :])
                last.then_inc(s_back, 1)

            back(0, 0)
            pe.wait_ge(s_lgT, 1)
            for t in range(T):
                for half in range(2):
                    last = pe.matmul(PS[5][:, t * NL:(t + 1) * NL], lgT[half][:, t * P:(t + 1) * P], ident[0:NL, 0:NL],
                                     start=(half == 0), stop=(half == 1))
            last.then_inc(s_lg2, 1)
            back(0, 1)
            back(1, 0)
            back(1, 1)
            pe.wait_ge(s_h2, 4)
            for b in range(4):
                pe.matmul(PS[b][:, :], zrow[:, 0:P], zrow[:, :], start=True, stop=False, skip_group_check=True)
            pe.wait_ge(s_A, 1)
            rk = PS[7]
            pe.matmul(rk[:, 0:2 * NEXP], before[:, :], Aa.rearrange("p t n -> p (t n)"), start=True, stop=False)
            pe.matmul(rk[:, NEXP:2 * NEXP], ones[:, :], Aa[:, 0, :], start=False, stop=True).then_inc(s_rank, 1)
            for t in range(T):
                last = pe.matmul(PS[6][:, 0:NEXP], ones[:, :], Aa[:, t, :], start=(t == 0), stop=(t == T - 1))
            last.then_inc(s_rank, 1)

            ACC = [PS[0], PS[1], PS[2], PS[3]]
            XB = [PS[4], PS[5]]
            GB, UB = PS[6], PS[7]

            def dispatch(p):
                pe.wait_ge(s_oneh, p + 1)
                for k in range(KD):
                    for t in range(T):
                        last = pe.matmul(XB[k // 4][:, (k % 4) * P:(k % 4 + 1) * P], hn[:, t, k * P:(k + 1) * P],
                                         oneh[:, t, :], start=(t == 0), stop=(t == T - 1))
                    if k == KD // 2 - 1:
                        last.then_inc(s_dispA, 1)
                last.then_inc(s_disp, 1)

            def combine(p, bank_done=None):
                pe.wait_ge(s_combT, p + 2)
                pe.wait_ge(s_yA, p + 2)
                pe.wait_ge(s_yV, p + 2)
                for t in range(T):
                    for c in range(2):
                        last = pe.matmul(ACC[2 * t + c][:, :], combT[:, t, :], ye[:, c * HALF:(c + 1) * HALF],
                                         start=False, stop=False, skip_group_check=True)
                        if bank_done is not None:
                            last.then_inc(bank_done, 1)
                if bank_done is None:
                    last.then_inc(s_comb, 1)

            def pair(p, last_one=False):
                known = isinstance(p, int) and p < PAIRS - 1
                beside = BESIDE.get(p, {}) if known else {}

                def ready(c, experts=(0, 1)):
                    for e in experts:
                        if (c, e) in beside:
                            m = 2 if c == 1 else e
                            pe.wait_ge(s_extra[m], 16 * len(EXTRA[m]) + (16 * len(EXTRA_DOWN[e]) if c == 2 else 0))
                        else:
                            missed = sum((c, e) in BESIDE[q] for q in BESIDE if not known or q < p)
                            pe.wait_ge(loaded[expert_slot(c, e)], 16 * (expert_loads(c, e) + 1 - missed) + 16 * p)

                def weights(c, e, k):
                    if (c, e) in beside:
                        k0, place = [(k0, v) for k0, v in beside[(c, e)] if k0 <= k][-1]
                        return place[:, k - k0, :]
                    return ring[:, expert_slot(c, e), :].rearrange("p (k n) -> p k n", n=(HALF, HALF, D)[c])[:, k, :]

                pe.wait_ge(s_xeA, p + 1)
                pe.wait_ge(s_eactT, p + 1)
                ready(0)
                for k in range(KD):
                    if k == KD // 2:
                        pe.wait_ge(s_xeV, p + 1)
                    for e in range(2):
                        last = pe.matmul(GB[64 * e:64 * e + 64, :], xeT[:, k, 64 * e:64 * e + 64], weights(0, e, k),
                                         start=(k == 0), stop=(k == KD - 1))
                last.then_inc(s_eg, 1)
                if not (isinstance(p, int) and p < 2):
                    combine(p - 1)
                ready(1)
                pe.wait_ge(s_combT, p + 1)
                for k in range(KD):
                    for e in range(2):
                        last = pe.matmul(UB[64 * e:64 * e + 64, :], xeT[:, k, 64 * e:64 * e + 64], weights(1, e, k),
                                         start=(k == 0), stop=(k == KD - 1))
                last.then_inc(s_eu, 1)
                if not last_one:
                    pe.wait_ge(s_yA, p + 1)
                    pe.wait_ge(s_yV, p + 1)
                    dispatch(p + 1)
                pe.wait_ge(s_eact, p + 1)
                for f in range(KE):
                    last = pe.transpose(GB[:, f * P:(f + 1) * P], eact[:, f * P:(f + 1) * P], ident[:, :])
                last.then_inc(s_etr, 1)
                if isinstance(p, int) and p == 1:
                    combine(0)
                pe.wait_ge(s_onehw, p + 1)
                for t in range(T):
                    last = pe.transpose(UB[:, t * P:(t + 1) * P], onehw[:, t, :], ident[:, :])
                last.then_inc(s_ctr, 1)
                pe.wait_ge(s_eactT, p + 2)
                if not last_one:
                    pe.wait_ge(s_xeA, p + 2)
                    pe.wait_ge(s_xeV, p + 2)
                if last_one:
                    ready(2, experts=(0,))
                    pe.wait_ge(s_half, 16)
                else:
                    ready(2)
                for f in range(KE):
                    if last_one and f == KE // 2:
                        ready(2, experts=(1,))
                    for c in range(2):
                        for e in range(2):
                            last = pe.matmul(XB[c][64 * e:64 * e + 64, :], eactT[:, f, 64 * e:64 * e + 64],
                                             weights(2, e, f)[:, c * HALF:(c + 1) * HALF], start=(f == 0),
                                             stop=(f == KE - 1))
                last.then_inc(s_edn, 1)

            dispatch(0)
            pe.wait_ge(s_counts, 1)
            pair(0)
            pair(1)
            pair(2)
            with pe.Fori(3, PAIRS - 1) as p:
                pair(p)
            pair(PAIRS - 1, last_one=True)
            pe.wait_ge(s_np, 1)
            n_pairs = pe.value_load(n_pairs_i[0:1, 0:1], min_val=PAIRS, max_val=PAIRS * PASSES)
            with pe.If(n_pairs > PAIRS):
                pe.wait_ge(s_yA, PAIRS + 1)
                pe.wait_ge(s_yV, PAIRS + 1)
                dispatch(PAIRS)
                with pe.Fori(PAIRS, PAIRS * PASSES) as p:
                    pair(p)
            combine(n_pairs - 1, bank_done=s_comb_last)

        @block.scalar
        def _(sc):
            order = [0]

            def then(ins):
                order[0] += 1
                ins.then_inc(s_alink, 1)
                sc.wait_ge(s_alink, order[0])

            cw = a["conv_w"].rearrange("o j (f p) -> (o j f) p", p=P)
            cb = a["conv_b"].rearrange("o (f p) -> (o f) p", p=P)
            sc.dma_start(stage[:, 0, :], cw[0:P, :]).then_inc(s_stage, 16)
            sc.dma_start(stage[0:FT, 1, :], cw[P:P + FT, :]).then_inc(s_stage, 16)
            sc.dma_start(stage[FT:2 * FT, 1, :], cb).then_inc(s_stage, 16)
            for name, row in (("c_2", R_C), ("attn_pre_g", R_PRE), ("ffn_pre_g", R_FPRE), ("g_mix_2", R_MIX),
                              ("g_ffn_2", R_FFN), ("swa_out_g", R_SWA), ("g_dil_out_2", R_DIL),
                              ("g_sb_out_2", R_SB), ("diff_subln_g", R_SUB)):
                v = a[name].rearrange("o (f p) -> (o f) p", p=P)
                sc.dma_start(stage[row:row + v.shape[0], 2, :], v).then_inc(s_stage, 16)
            sc.dma_start(sinks, a["swa_sinks"][0].partition_broadcast(P)).then_inc(s_sink, 16)
            for n, name in enumerate(("diff_lq1", "diff_lk1", "diff_lq2", "diff_lk2")):
                sc.dma_start(lamv[:, n, :], a[name][0].partition_broadcast(P)).then_inc(s_lamv, 16)

            def scaled(tag, scale, shift=None):
                for k in (2, 3, 6, 7):
                    sc.wait_ge(s_turn[tag], k // 2 + 1)
                    sc.activation(hT[:, k, :], PS[k // 2][:, (k % 2) * S:(k % 2 + 1) * S], ACT.Identity,
                                  scale=scale(k), bias=0.0 if shift is None else shift(k)).then_inc(s_hTA, 1)

            def rounded(tag, scale, shift=None, first=0):
                for k in range(first, KD):
                    sc.wait_ge(s_turn[tag], k // 2 + 1)
                    sc.activation(hi_T[:, k, :], PS[k // 2][:, (k % 2) * S:(k % 2 + 1) * S], ACT.Identity,
                                  scale=scale(k), bias=0.0 if shift is None else shift(k)).then_inc(s_hhi[tag], 1)

            def split(n, more=0):
                for part in range(2):
                    split_one(n, part, more)

            def split_one(n, part, more=0):
                if part == 0:
                    sc.wait_ge(loaded[n % LANES], 16 * (n // LANES + 1) + 16 * more)
                raw, hi, _ = split_part(n, part)
                sc.activation(hi, raw, ACT.Copy).then_inc(s_whi, 1)

            def take(blk, pieces):
                for n in pieces:
                    if n % 2:
                        continue
                    c, kind, where = ITEMS[blk][n]
                    sc.wait_ge(s_gemm[blk], n + 1)
                    if n == 0:
                        sc.wait_ge(s_qzero, blk + 1)
                    for dst, src in taken(blk, kind, where, item_bank(blk, n)):
                        last = sc.activation(dst, src, ACT.Copy)
                    last.then_inc(s_evA[blk], 1)

            def softmaxes(blk, fill, splits):
                units = UNITS[blk]
                ends = finishes(blk)

                def exponentials(i):
                    u = units[i]
                    sc.wait_ge(s_max[blk], i + 1)
                    if i >= 2:
                        sc.wait_ge(s_tr[blk], i - 1)
                    r, c, w = row_of(u), col_of(u), u["w"]
                    for j in range(len(u["maps"])):
                        last = sc.activation(Eb[:, i % 2, j * w:(j + 1) * w], Lb[:, i % 2, j * w:(j + 1) * w],
                                             ACT.Exp, bias=nm[:, r, c + j:c + j + 1],
                                             accum_out=den[:, r, c + j:c + j + 1])
                    last.then_inc(s_exp[blk], 1)
                    if u["kind"] == "swa" and i == ends[("swa", u["t"])]:
                        sc.wait_ge(s_sk, u["t"] + 1)
                        sc.activation(esink[:, u["t"], :], esink[:, u["t"], :], ACT.Exp).then_inc(s_ske, 1)

                def head_squares(t):
                    n = ends[("diff", t)]
                    sc.wait_ge(s_pv[blk], n + 1)
                    if t > 0:
                        sc.wait_ge(s_hsq, t)
                    for h in range(DIFF_H):
                        last = sc.activation(junk[:, HALF + h * P:HALF + (h + 1) * P],
                                             out_bank(units[n])[:, h * P:(h + 1) * P], ACT.Square, scale=P ** -0.5,
                                             accum_out=hsq[:, t, h:h + 1])
                    last.then_inc(s_hsq, 1)

                exponentials(0)
                for i in range(len(units) + 1):
                    if i >= 1:
                        n = i - 1
                        w = P * len(turned(units[n]))
                        sc.wait_ge(s_tr[blk], n + 1)
                        if n >= 2:
                            sc.wait_ge(s_pv[blk], n - 1)
                        sc.activation(PT[:, n % 2, 0:w], PS[2 + n % 2][:, 0:w], ACT.Copy).then_inc(s_pt[blk], 1)
                    if i + 1 < len(units):
                        exponentials(i + 1)
                    take(blk, fill.get(i, []))
                    if i in splits:
                        split_one(*splits[i])
                    for t in range(T):
                        if blk == 0 and i == min(ends[("diff", t)] + 3, len(units)):
                            head_squares(t)

            def squares(m, t, bank_done):
                if t > 0:
                    sc.wait_ge(s_sq[m], 2 * t)
                for c in range(2):
                    sc.wait_ge(bank_done, 2 * t + c + 1)
                    sc.activation(junk[:, c * HALF:(c + 1) * HALF], PS[4 + 2 * t + c][:, :], ACT.Square,
                                  scale=D ** -0.5, accum_out=sq[:, 2 * t + c:2 * t + c + 1]).then_inc(s_sq[m], 1)

            split_one(N_IN, 0)
            sc.wait_ge(s_vec, 1)
            rounded("attn1", lambda k: vec[:, 2, R_PRE + k:R_PRE + k + 1], first=KD // 2)
            split_one(N_IN, 1)
            split(N_IN + 1)
            sc.wait_ge(s_lamx, 1)
            sc.activation(lam2, lam2, ACT.Exp).then_inc(s_lame, 1)
            take(0, range(3))
            split(N_IN + 2)
            take(0, range(3, AHEAD[0]))
            softmaxes(0, BETWEEN[0], SPLITS[0])
            split(N_OUT + 1)
            rounded("mix1", lambda k: vec[:, 2, R_SWA + k:R_SWA + k + 1] if k < 4 else subc)
            split(N_FFN)
            for t in range(T):
                squares(0, t, s_proj[0])
            rounded("ffn", lambda k: vec[:, 2, R_FPRE + k:R_FPRE + k + 1])
            split(seq_gate(0) + 1)
            sc.activation(siluc, vec[:, 2, R_C:R_C + KD], ACT.Silu).then_inc(s_c, 1)

            def taps(i, part, b):
                sc.wait_ge(s_up, 4 * i + 2 * part + b + 1)
                if (not isinstance(i, int) or i > 0) and b == 0:
                    sc.wait_ge(s_act, i)
                for f in range(2):
                    ft = KE * i + (FT // 2) * part + 2 * b + f
                    last = sc.activation(conv[:, part, 2 * b + f, :], PS[2 * part + b][:, f * S:(f + 1) * S],
                                         ACT.Identity, scale=vec[:, 1, ds(ft, 1)], bias=vec[:, 1, ds(ft + FT, 1)])
                last.then_inc(s_tap, 1)

            def ffn(i, more=None, last=False):
                later = more is not None
                taps(i, 0, 0)
                if later:
                    split(seq_down(0), more)
                taps(i, 0, 1)
                sc.wait_ge(s_conv, 4 * i + 2)
                sc.activation(conv[:, 0, :, :], conv[:, 0, :, :], ACT.Gelu_apprx_tanh).then_inc(s_gelu, 1)
                taps(i, 1, 0)
                split(*((seq_gate(2), more) if later else (seq_gate(1),)))
                taps(i, 1, 1)
                if not last:
                    split(*((seq_gate(2) + 1, more) if later else (seq_gate(1) + 1,)))
                sc.wait_ge(s_prod, i + 1)
                if later:
                    sc.wait_ge(s_down, i)
                sc.activation(act_r[:, 0, :, :], conv[:, 0, :, :], ACT.Copy).then_inc(s_ahi, 1)
                if last:
                    split(N_IN2)

            sc.preload_act_table(ACT.Gelu_apprx_tanh)
            ffn(0)
            with sc.Fori(1, CHUNKS - 1) as i:
                ffn(i, i - 1)
            ffn(CHUNKS - 1, CHUNKS - 2, last=True)
            def gate_rows(n):
                sc.wait_ge(s_adam, n + 2)
                dst = (post_attn, post_ffn)[n // 2][:, (n % 2) * HALF:(n % 2 + 1) * HALF]
                sc.activation(dst, PS[(1, 2, 3, 0)[n]][:, :], ACT.Copy).then_inc(s_mod, 1)

            sc.wait_ge(s_adam, 1)
            two = [PS[n][:, 0:2 * KD].rearrange("p (a b) -> p a b", a=2) for n in range(2)]
            sc.activation(modc[:, 0:2, :], two[0], ACT.Copy).then_inc(s_mod, 1)
            squares(1, 0, s_bank)
            split(N_IN2 + 1)
            squares(1, 1, s_bank)
            gate_rows(0)
            gate_rows(1)
            sc.wait_ge(s_rfree, 1)
            gate_rows(2)
            gate_rows(3)
            sc.wait_ge(s_adam, 6)
            sc.activation(modc[:, 2:4, :], two[1], ACT.Copy).then_inc(s_mod, 1)
            sc.wait_ge(s_modc, 1)
            rounded("attn2", lambda k: gmixc[:, k:k + 1], lambda k: modc[:, 0, k:k + 1])
            split(N_IN2 + 2)
            take(1, range(8))
            split(N_IN2 + 3)
            take(1, range(8, AHEAD[1]))
            sc.preload_act_table_set("natural_log_exp_and_others")
            def logarithms(n):
                sc.wait_ge(s_zm, n + 1)
                if n >= 2:
                    sc.wait_ge(s_lk, n - 1)
                dst = softplus(n)
                then(sc.activation(dst, Lb[:, n % 2, 0:384], ACT.Abs))
                then(sc.activation(dst, dst, ACT.Exp, scale=-1.0))
                sc.activation(dst, dst, ACT.Ln, bias=1.0).then_inc(s_sb1, 1)

            logarithms(0)
            for i in range(SB_H + 1):
                if i + 1 < SB_H:
                    logarithms(i + 1)
                if i >= 1:
                    n = i - 1
                    sc.wait_ge(s_t, n + 1)
                    sc.activation(PT[:, n % 2, 0:384], PT[:, n % 2, 0:384], ACT.Exp).then_inc(s_w, 1)
                take(1, BETWEEN[1].get(i, []))
                if i in SPLITS[1]:
                    split_one(*SPLITS[1][i])
            softmaxes(1, {}, {})
            rounded("mix2", lambda k: vec[:, 2, R_DIL + k:R_DIL + k + 1])
            sc.wait_ge(s_modc, 2)
            scaled("moe", lambda k: gffnc[:, k:k + 1], lambda k: modc[:, 2, k:k + 1])
            for n in range(4):
                sc.wait_ge(s_back, n + 1)
                sc.activation(hn[:, n // 2, n % 2 * HALF:(n % 2 + 1) * HALF], PS[n][:, :], ACT.Copy).then_inc(s_h2, 1)
            sc.wait_ge(s_r1, 1)
            for t in range(T):
                last = sc.activation(gexp[:, t, :], lg[:, t, 0:NGRP], ACT.Exp, bias=ngmax[:, t:t + 1],
                                     accum_out=gsum[:, t:t + 1])
            last.then_inc(s_r2, 1)
            sc.wait_ge(s_r1, 2)
            sc.activation(ed, ed, ACT.Exp).then_inc(s_r2, 1)
            sc.preload_act_table(ACT.Silu)

            def tokens(p):
                sc.wait_ge(s_dispA, p + 1)
                sc.activation(xeT[:, 0:4, :], PS[4][:, :].rearrange("p (a b) -> p a b", a=4), ACT.Copy)\
                    .then_inc(s_xeA, 1)

            def pair(p, last_one=False):
                sc.wait_ge(s_eg, p + 1)
                sc.wait_ge(s_etr, p + 1)
                sc.activation(eact, PS[6][:, :], ACT.Silu).then_inc(s_silu, 1)
                if not last_one:
                    tokens(p + 1)
                sc.wait_ge(s_etr, p + 2)
                sc.activation(eactT, PS[6][:, :].rearrange("p (a b) -> p a b", a=KE), ACT.Copy).then_inc(s_eactT, 1)
                sc.wait_ge(s_edn, p + 1)
                sc.activation(ye[:, 0:HALF], PS[4][:, :], ACT.Copy).then_inc(s_yA, 1)

            tokens(0)
            with sc.Fori(0, PAIRS - 1) as p:
                pair(p)
            pair(PAIRS - 1, last_one=True)
            sc.wait_ge(s_np, 1)
            n_pairs = sc.value_load(n_pairs_i[0:1, 0:1], min_val=PAIRS, max_val=PAIRS * PASSES)
            with sc.If(n_pairs > PAIRS):
                tokens(PAIRS)
                with sc.Fori(PAIRS, PAIRS * PASSES) as p:
                    pair(p)
            nobody_reads = (xeT[:, 0:4, :], xeT[:, 4:8, :], eactT, eact.rearrange("p (a b) -> p a b", a=KE))
            for n in range(2 * T):
                t, c = n // 2, n % 2
                sc.wait_ge(s_xsum, n + 1)
                sc.activation(nobody_reads[n], x[:, t, c * HALF:(c + 1) * HALF].rearrange("p (a b) -> p a b", a=KE),
                              ACT.Square, scale=D ** -0.5, accum_out=sq[:, n:n + 1]).then_inc(s_sq[2], 1)

        @block.vector
        def _(ve):
            order = [0]

            def then(ins):
                order[0] += 1
                ins.then_inc(s_link, 1)
                ve.wait_ge(s_link, order[0])

            asked, answered = [0], [0]

            def column():
                return ROOTS[asked[0]][0]

            def ask_root(ins):
                asked[0] += 1
                ins.then_inc(s_ms, 1)

            def root():
                answered[0] += 1
                ve.wait_ge(s_rs, answered[0])
                first = ROOTS[answered[0] - 1][0]
                return rstd[:, first:first + 1]

            def mean_squares(src, junk, at):
                return ve.tensor_tensor_reduce(junk, src, src, 1.0 / src.shape[1], EPS, ALU.mult, ALU.add,
                                               ms[:, at:at + 1])

            def norm(tag, t, dst):
                ask_root(mean_squares(x[:, t, :], mix[:, t, :], column()))
                ve.tensor_scalar(dst[:, t, :], x[:, t, :], root(), None, ALU.mult).then_inc(s_src[tag], 1)

            def scaled(tag, scale, shift=None):
                for k in (0, 1, 4, 5):
                    ve.wait_ge(s_turn[tag], k // 2 + 1)
                    src = PS[k // 2][:, (k % 2) * S:(k % 2 + 1) * S]
                    if shift is None:
                        ins = ve.tensor_scalar(hT[:, k, :], src, scale(k), None, ALU.mult)
                    else:
                        ins = ve.tensor_scalar(hT[:, k, :], src, scale(k), shift(k), ALU.mult, ALU.add)
                    ins.then_inc(s_hT[tag], 1)

            def low(tag, scale, shift=None, mine=0):
                dst = lo_T[tag]
                for k in range(mine):
                    ve.wait_ge(s_turn[tag], k // 2 + 1)
                    ve.tensor_scalar(hi_T[:, k, :], PS[k // 2][:, (k % 2) * S:(k % 2 + 1) * S], scale(k), None,
                                     ALU.mult).then_inc(s_hhiV, 1)
                for k in range(KD + 1):
                    if k < mine:
                        ve.wait_ge(s_hhiV, k + 1)
                    elif k < KD:
                        ve.wait_ge(s_hhi[tag], (k - mine) // 2 * 2 + 2)
                    if k < KD:
                        src = PS[k // 2][:, (k % 2) * S:(k % 2 + 1) * S]
                        if shift is None:
                            ve.scalar_tensor_tensor(dst[:, k, :], src, scale(k), hi_T[:, k, :],
                                                    ALU.mult, ALU.subtract).then_inc(s_hT[tag], 1)
                        else:
                            ve.tensor_scalar(shifted[:, k, :], src, scale(k), shift(k), ALU.mult, ALU.add)\
                                .then_inc(s_shift, 1)
                    if shift is not None and k > 0:
                        ve.wait_ge(s_shift, k)
                        ve.tensor_tensor(dst[:, k - 1, :], shifted[:, k - 1, :], hi_T[:, k - 1, :], ALU.subtract)\
                            .then_inc(s_hT[tag], 1)

            def split(n, more=0):
                for part in parts_of(n)[1]:
                    ve.wait_ge(s_whi, 2 * n + 1 + part + 2 * more)
                    raw, hi, lo = split_part(n, part)
                    last = ve.tensor_tensor(lo, raw, hi, ALU.subtract)
                if parts_of(n)[1]:
                    last.then_inc(s_wloV, 1)

            def take(blk, pieces):
                for n in pieces:
                    if n % 2 == 0:
                        continue
                    c, kind, where = ITEMS[blk][n]
                    ve.wait_ge(s_gemm[blk], n + 1)
                    if n == 1:
                        ve.wait_ge(s_qzero, blk + 1)
                    for dst, src in taken(blk, kind, where, item_bank(blk, n)):
                        last = ve.tensor_copy(dst, src)
                    last.then_inc(s_evV[blk], 1)

            def heads(v, t):
                return v[:, t, HALF:D].rearrange("p (h d) -> p h d", d=P)

            def softmaxes(blk, fill):
                units = UNITS[blk]
                ends = finishes(blk)

                def logits(i):
                    u = units[i]
                    w, n = u["w"], len(u["maps"])
                    ve.wait_ge(s_sc[blk], i + 1)
                    if i >= 2:
                        ve.wait_ge(s_exp[blk], i - 1)
                    b0 = u["maps"][0]["b"]
                    S3 = PS[i % 2][:, 0:n * w].rearrange("p (a b) -> p a b", a=n)
                    L3 = Lb[:, i % 2, 0:n * w].rearrange("p (a b) -> p a b", a=n)
                    if u["kind"] == "diff":
                        for h in range(n // 2):
                            bb = bias[:, b0 + h, S - w:S].unsqueeze(1).broadcast_to([P, 2, w])
                            last = ve.scalar_tensor_tensor(L3[:, 2 * h:2 * h + 2, :], S3[:, 2 * h:2 * h + 2, :], SCALE,
                                                           bb, ALU.mult, ALU.add)
                    else:
                        last = ve.scalar_tensor_tensor(L3, S3, SCALE, bias[:, b0:b0 + n, S - w:S], ALU.mult, ALU.add)
                    last.then_inc(s_log[blk], 1)
                    ve.wait_ge(s_log[blk], i + 1)
                    r, c = row_of(u), col_of(u)
                    red = ve.tensor_reduce(nm[:, r, c:c + n], L3, X, ALU.max, negate=True)
                    if u["kind"] == "swa":
                        then(red)
                        red = ve.tensor_tensor(nm[:, r, c:c + n], nm[:, r, c:c + n], negsink[:, c:c + n], ALU.min)
                    red.then_inc(s_max[blk], 1)
                    if u["kind"] == "swa" and i == ends[("swa", u["t"])]:
                        ve.wait_ge(s_max[blk], i + 1)
                        ve.tensor_tensor(esink[:, u["t"], :], nm[:, u["t"], :], sinks, ALU.add).then_inc(s_sk, 1)

                def difference(i):
                    u = units[i]
                    r, c, w, n = row_of(u), col_of(u), u["w"], len(u["maps"])
                    ve.wait_ge(s_exp[blk], i + 1)
                    then(ve.reciprocal(rden[:, r, c:c + n], den[:, r, c:c + n]))
                    for h in range(n // 2):
                        k = c + 2 * h
                        then(ve.tensor_scalar(rl[:, u["t"], h:h + 1], rden[:, r, k + 1:k + 2], lam, None, ALU.mult))
                        e0 = Eb[:, i % 2, 2 * h * w:(2 * h + 1) * w]
                        e1 = Eb[:, i % 2, (2 * h + 1) * w:(2 * h + 2) * w]
                        then(ve.tensor_scalar(e1, e1, rl[:, u["t"], h:h + 1], None, ALU.mult))
                        dst = Eb[:, i % 2, h * w:(h + 1) * w]
                        last = ve.scalar_tensor_tensor(dst, e0, rden[:, r, k:k + 1], e1, ALU.mult, ALU.subtract)
                    last.then_inc(s_dif, 1)

                def ask_heads(t):
                    ve.wait_ge(s_hsq, t + 1)
                    ask_root(ve.tensor_scalar(ms[:, 5 * t + 1:5 * t + 5], hsq[:, t, :], EPS, None, ALU.add))

                def finish(n):
                    u = units[n]
                    r, t = row_of(u), u["t"]
                    done = list(ends.values()).index(n) + 1
                    window = mix[:, t, 0:HALF]
                    ve.wait_ge(s_pv[blk], n + 1)
                    if u["kind"] == "diff":
                        ve.tensor_scalar(window, window, root(), None, ALU.mult)
                        ve.tensor_tensor(heads(mix, t), out_bank(u)[:, :].rearrange("p (h d) -> p h d", d=P),
                                         rstd[:, 5 * t + 1:5 * t + 5].unsqueeze(2).broadcast_to([P, DIFF_H, P]),
                                         ALU.mult).then_inc(s_src["mix1"], 1)
                        return
                    if u["kind"] == "swa":
                        ve.wait_ge(s_ske, t + 1)
                        then(ve.tensor_tensor(den[:, r, :], den[:, r, :], esink[:, t, :], ALU.add))
                    then(ve.reciprocal(rden[:, r, :], den[:, r, :]))
                    ve.tensor_tensor(window.rearrange("p (h d) -> p h d", d=HD),
                                     out_bank(u)[:, :].rearrange("p (h d) -> p h d", d=HD),
                                     rden[:, r, :].unsqueeze(2).broadcast_to([P, 8, HD]), ALU.mult)\
                        .then_inc(s_done[blk], 1)
                    ve.wait_ge(s_done[blk], done)
                    if u["kind"] == "swa":
                        mean_squares(window, junk[:, 0:HALF], 5 * t)
                        return
                    ask_root(mean_squares(window, junk[:, 0:HALF], 2 * t))
                    root()
                    for c in range(2):
                        last = ve.tensor_scalar(mix[:, t, c * HALF:(c + 1) * HALF], mix[:, t, c * HALF:(c + 1) * HALF],
                                                rstd[:, 2 * t + c:2 * t + c + 1], None, ALU.mult)
                    last.then_inc(s_src["mix2"], 1)

                logits(0)
                for i in range(len(units) + 2):
                    if 1 <= i <= len(units) and units[i - 1]["kind"] == "diff":
                        difference(i - 1)
                    if i + 1 < len(units):
                        logits(i + 1)
                    if blk == 1 and i in (0, 1):
                        stick_breaking_out(i)
                    if i - 3 in ends.values():
                        if units[i - 3]["kind"] == "diff":
                            ask_heads(units[i - 3]["t"])
                        else:
                            finish(i - 3)
                    if i == len(units) + 1:
                        if blk == 0:
                            ask_heads(T - 1)
                            for t in range(T - 1):
                                finish(ends[("diff", t)])
                        finish(len(units) - 1)
                    take(blk, fill.get(i, []))

            def post_norm(m, rows, t, read=None):
                at = column()
                for c in range(2):
                    half = slice(c * HALF, (c + 1) * HALF)
                    ve.wait_ge(s_sq[m], 2 * t + c + 1)
                    if c == 1:
                        ask_root(ve.scalar_tensor_tensor(ms[:, at:at + 1], sq[:, 2 * t:2 * t + 1], EPS,
                                                         sq[:, 2 * t + 1:2 * t + 2], ALU.add, ALU.add))
                    last = ve.tensor_tensor(mix[:, t, half], PS[4 + 2 * t + c][:, :], rows[:, half], ALU.mult)
                if read is None:
                    then(last)
                else:
                    last.then_inc(read, 1)
                    ve.wait_ge(read, 1)
                then(ve.scalar_tensor_tensor(x[:, t, :], mix[:, t, :], root(), x[:, t, :], ALU.mult, ALU.add))

            def gated(bank, rows, t, bank_done):
                for c in range(2):
                    half = slice(c * HALF, (c + 1) * HALF)
                    ve.wait_ge(bank_done, 2 * t + c + 1)
                    then(ve.tensor_tensor(mix[:, t, half], PS[bank + 2 * t + c][:, :], rows[:, half], ALU.mult))
                    then(ve.tensor_tensor(x[:, t, half], x[:, t, half], mix[:, t, half], ALU.add))
                    last = ve.tensor_tensor_reduce(mix[:, t, half], x[:, t, half], x[:, t, half], 1.0 / D, 0.0,
                                                   ALU.mult, ALU.add, sq[:, 2 * t + c:2 * t + c + 1])
                then(last)
                at = column()
                ask_root(ve.scalar_tensor_tensor(ms[:, at:at + 1], sq[:, 2 * t:2 * t + 1], EPS,
                                                 sq[:, 2 * t + 1:2 * t + 2], ALU.add, ALU.add))
                return root()

            for t in range(T):
                ve.wait_ge(s_x[t], 16)
                ask_root(mean_squares(x[:, t, :], mix[:, t, :], column()))
            for t in range(T):
                ve.tensor_scalar(hn[:, t, :], x[:, t, :], root(), None, ALU.mult).then_inc(s_src["attn1"], 1)
            ve.wait_ge(s_vecT, 1)
            ve.tensor_copy(vec[:, 0:2, :], PS[7][:, 0:2 * P].rearrange("p (a b) -> p a b", a=2))
            then(ve.tensor_copy(vec[:, 2, 0:53], PS[7][:, 2 * P:2 * P + 53]))
            ve.tensor_scalar(subc, vec[:, 2, R_SUB:R_SUB + 1], 1.0 - LAMBDA_INIT, None, ALU.mult).then_inc(s_vec, 1)
            low("attn1", lambda k: vec[:, 2, R_PRE + k:R_PRE + k + 1], mine=KD // 2)
            split(N_IN)
            split(N_IN + 1)
            ve.wait_ge(s_lamv, 64)
            for n in range(2):
                last = ve.tensor_tensor_reduce(mix[:, 1, n * HD:(n + 1) * HD], lamv[:, 2 * n, :], lamv[:, 2 * n + 1, :],
                                               1.0, 0.0, ALU.mult, ALU.add, lam2[:, n:n + 1])
            last.then_inc(s_lamx, 1)
            ve.wait_ge(s_sink, 16)
            ve.tensor_scalar(negsink, sinks, -1.0, None, ALU.mult)
            ve.wait_ge(s_lame, 1)
            then(ve.tensor_scalar(lam, lam2[:, 0:1], lam2[:, 1:2], LAMBDA_INIT, ALU.subtract, ALU.add))
            take(0, range(3))
            split(N_IN + 2)
            take(0, range(3, AHEAD[0]))
            ve.wait_ge(s_mask, 1)
            softmaxes(0, BETWEEN[0])
            split(N_OUT)
            low("mix1", lambda k: vec[:, 2, R_SWA + k:R_SWA + k + 1] if k < 4 else subc)
            split(N_OUT + 1)
            ve.tensor_scalar(frac, iota[:, 0:NEXP], 1.0 / 64, None, ALU.mult)
            dist = mix[:, 0, 0:S].bitcast(i32)
            masked = mix[:, 0, S:2 * S].bitcast(i32)
            four = mix[:, 0, 2 * S:3 * S]
            sixteen = mix[:, 0, 3 * S:4 * S]
            count = mix[:, 1, 0:S]
            term = mix[:, 1, S:2 * S]
            then(ve.tensor_scalar(dist, negdist[:, :], -1.0, None, ALU.mult))
            then(ve.tensor_scalar(masked, dist, 3, None, ALU.bitwise_and))
            then(ve.tensor_scalar(four, masked, 0.0, None, ALU.is_equal))
            then(ve.tensor_scalar(masked, dist, 15, None, ALU.bitwise_and))
            then(ve.tensor_scalar(sixteen, masked, 0.0, None, ALU.is_equal))
            then(ve.tensor_tensor(four, four, sixteen, ALU.add))
            then(ve.tensor_scalar(sixteen, negdist[:, :], -128.0, None, ALU.is_ge))
            then(ve.tensor_tensor(count, four, sixteen, ALU.add))
            then(ve.tensor_scalar(lncount[:, :], count, 2.0, math.log(2.0), ALU.is_ge, ALU.mult))
            then(ve.tensor_scalar(term, count, 3.0, math.log(3.0) - math.log(2.0), ALU.is_ge, ALU.mult))
            then(ve.tensor_tensor(lncount[:, :], lncount[:, :], term, ALU.add))
            then(ve.tensor_scalar(term, count, 1.0, NEG, ALU.is_lt, ALU.mult))
            then(ve.tensor_tensor(lncount[:, :], lncount[:, :], term, ALU.add))
            then(ve.tensor_scalar(term, negdist[:, :], 0.0, NEG, ALU.is_gt, ALU.mult))
            then(ve.tensor_tensor(lncount[:, :], lncount[:, :], term, ALU.add))
            for h in range(DIL_H):
                last = ve.scalar_tensor_tensor(bias[:, h, :], negdist[:, :], float(np.float32(dil_slopes[h])),
                                               lncount[:, :], ALU.mult, ALU.add)
            then(last)
            split(N_FFN)
            ve.wait_ge(s_rows, 32)
            for t in range(T):
                post_norm(0, post_attn, t)
                norm("ffn", t, hn)
            low("ffn", lambda k: vec[:, 2, R_FPRE + k:R_FPRE + k + 1])
            split(seq_gate(0) + 1)

            def convolve(i, part, b):
                ve.wait_ge(s_tap, 4 * i + 2 * part + b + 1)
                for back in (1, 2):
                    for f in range(2):
                        ft = KE * i + (FT // 2) * part + 2 * b + f
                        tap = vec[:, 0, ds(ft + FT * (2 - back), 1)]
                        c = conv[:, part, 2 * b + f, back:S]
                        n = 8 * i + 4 * part + 2 * b + f + 1
                        if back == 2:
                            ve.wait_ge(s_cv1, n)
                        last = ve.scalar_tensor_tensor(c, PS[2 * part + b][:, f * S:(f + 1) * S - back], tap, c,
                                                       ALU.mult, ALU.add)
                        if back == 1:
                            last.then_inc(s_cv1, 1)
                last.then_inc(s_conv, 1)

            def modulation(r, c):
                ve.wait_ge(s_adab[c % 2], 16 * (ADA_EACH // 2 * r + c // 2 + 1))
                for m in range(4):
                    h, k = m % 2, m // 2
                    dst = ada[:, ds(1024 * r + 2 * ADA_W * (c // 4) + ADA_W * h, ADA_W)]
                    ve.wait_ge(s_sum, 4 * (ADA_EACH * r + c) + m + 7)
                    tile = 2 * (c % 4) + k
                    ve.scalar_tensor_tensor(dst, ada_buf[:, c % 2, k, h * ADA_W:(h + 1) * ADA_W],
                                            siluc[:, tile:tile + 1], dst, ALU.mult, ALU.add).then_inc(s_sum, 1)

            def ffn(i, more=None, units=False, last=False):
                later = more is not None

                def modulate(*cs):
                    for c in cs:
                        if units:
                            modulation(i - 1, c)

                modulate(0, 1)
                convolve(i, 0, 0)
                if later:
                    split(seq_down(0), 3 * more)
                modulate(2, 3)
                convolve(i, 0, 1)
                modulate(4, 5)
                convolve(i, 1, 0)
                split(*((seq_gate(2), 3 * more) if later else (seq_gate(1),)))
                modulate(6)
                convolve(i, 1, 1)
                ve.wait_ge(s_conv, 4 * i + 4)
                ve.wait_ge(s_gelu, i + 1)
                ve.tensor_tensor(conv[:, 0, :, :], conv[:, 0, :, :], conv[:, 1, :, :], ALU.mult).then_inc(s_prod, 1)
                if not last:
                    split(*((seq_gate(2) + 1, 3 * more) if later else (seq_gate(1) + 1,)))
                modulate(7)
                ve.wait_ge(s_ahi, i + 1)
                ve.tensor_tensor(act_r[:, 1, :, :], conv[:, 0, :, :], act_r[:, 0, :, :], ALU.subtract)\
                    .then_inc(s_act, 1)
                if last:
                    split(N_IN2)

            ffn(0)
            ve.wait_ge(s_ada0, 16)
            ve.wait_ge(s_c, 1)
            ve.nop().then_inc(s_sum, 8)
            with ve.Fori(1, CHUNKS - 1) as i:
                ffn(i, i - 1, units=True)
            ffn(CHUNKS - 1, CHUNKS - 2, last=True)
            ve.wait_ge(s_mod, 1)
            ve.scalar_tensor_tensor(gmixc, modc[:, 1, :], 1.0, vec[:, 2, R_MIX:R_MIX + KD], ALU.add, ALU.mult)\
                .then_inc(s_modc, 1)
            for t in range(T):
                post_norm(1, post_ffn, t, read=s_rfree if t == T - 1 else None)
                norm("attn2", t, rows2)
            ve.wait_ge(s_modc, 1)
            ve.wait_ge(s_mod, 6)
            ve.scalar_tensor_tensor(gffnc, modc[:, 3, :], 1.0, vec[:, 2, R_FFN:R_FFN + KD], ALU.add, ALU.mult)\
                .then_inc(s_modc, 1)
            low("attn2", lambda k: gmixc[:, k:k + 1], lambda k: modc[:, 0, k:k + 1])
            split(N_IN2 + 1)
            split(N_IN2 + 2)
            take(1, range(AHEAD[1]))

            ve.wait_ge(s_bias2, 1)
            def scaled_scores(n):
                zs = Lb[:, n % 2, 0:384]
                ve.wait_ge(s_z, n + 1)
                ve.tensor_scalar(zs, PS[n % 2][:, 0:384], SCALE, None, ALU.mult).then_inc(s_zm, 1)
                ve.wait_ge(s_zm, n + 1)
                then(ve.tensor_scalar(mix[:, n % 2, HALF:HALF + 384], zs, 0.0, None, ALU.max))

            scaled_scores(0)
            for i in range(SB_H + 1):
                if i + 1 < SB_H:
                    scaled_scores(i + 1)
                if i < SB_H:
                    zs = Lb[:, i % 2, 0:384]
                    r = mix[:, i % 2, HALF:HALF + 384]
                    dst = PT[:, i % 2, 0:384]
                    if i >= 2:
                        ve.wait_ge(s_sbo, i - 1)
                    ve.tensor_tensor(dst, zs, SB_ADD, ALU.add)
                    ve.wait_ge(s_sb1, i + 1)
                    then(ve.tensor_tensor(r, r, softplus(i), ALU.add))
                    if i >= 2:
                        ve.wait_ge(s_R, i - 1)
                    ve.tensor_tensor(Eb[:, i % 2, 0:384], r, SB_NEG, ALU.mult).then_inc(s_lk, 1)
                if i >= 1:
                    n = i - 1
                    ve.wait_ge(s_R, n + 1)
                    dst = PT[:, n % 2, 0:384]
                    ve.tensor_tensor(dst, PS[2 + n % 2][:, 0:384], dst, ALU.add).then_inc(s_t, 1)
                take(1, BETWEEN[1].get(i, []))

            def stick_breaking_out(t):
                ve.wait_ge(s_sbo, SB_H)
                then(ve.tensor_copy(mix[:, t, HALF:D], PS[4 + t][:, :]))
                then(mean_squares(mix[:, t, HALF:D], junk[:, HALF:D], 2 * t + 1))

            softmaxes(1, {})
            ve.memset(ranks[:, :, PASSES * NEXP:], -1.0).then_inc(s_mixed, 1)
            low("mix2", lambda k: vec[:, 2, R_DIL + k:R_DIL + k + 1])
            ve.wait_ge(s_mod, 6)
            for t in range(T):
                r = gated(4, post_attn, t, s_proj[1])
                ve.tensor_scalar(hn[:, t, :], x[:, t, :], r, None, ALU.mult).then_inc(s_src["moe"], 1)
            scaled("moe", lambda k: gffnc[:, k:k + 1], lambda k: modc[:, 2, k:k + 1])

            def over_n(v, n):
                return v.unsqueeze(2).broadcast_to([P, T, n])

            experts = lambda v, t: v[:, t, :].rearrange("p (g j) -> p g j", j=EPG)

            def first_largest(v, largest, dst):
                for t in range(T):
                    last = ve.scalar_tensor_tensor(dst[:, t, :], v[:, t, :], largest[:, t:t + 1], frac[:, 0:v.shape[2]],
                                                   ALU.is_lt, ALU.add)
                then(last)

            def one_hot(dst, at):
                for t in range(T):
                    last = ve.tensor_scalar(dst[:, t, :], frac, at[:, t:t + 1], None, ALU.is_equal)
                return last

            ve.wait_ge(s_lg, 1)
            for half in range(2):
                last = ve.tensor_copy(lgT[half], PS[4][64 * half:64 * half + NL, 0:S])
            last.then_inc(s_lgT, 1)
            ve.wait_ge(s_lg2, 1)
            then(ve.tensor_copy(lg, PS[5][:, 0:T * NL].rearrange("p (t n) -> p t n", t=T)))
            groups = lg[:, :, 0:NGRP]
            then(ve.tensor_reduce(gmax, groups, X, ALU.max))
            ve.tensor_scalar(ngmax, gmax, -1.0, None, ALU.mult).then_inc(s_r1, 1)
            first_largest(groups, gmax, gfirst)
            then(ve.tensor_reduce(gidx, gfirst, X, ALU.min))
            for t in range(T):
                last = ve.tensor_scalar(outside[:, t, :], frac[:, 0:NGRP], gidx[:, t:t + 1], NEG, ALU.not_equal, ALU.mult)
            then(last)
            for t in range(T):
                last = ve.tensor_tensor(experts(el, t), lg[:, t, NGRP:].rearrange("p (g j) -> p g j", j=EPG),
                                        outside[:, t, :].unsqueeze(2).broadcast_to([P, NGRP, EPG]), ALU.add)
            then(last)
            then(ve.tensor_reduce(m1, el, X, ALU.max))
            first_largest(el, m1, first)
            then(ve.tensor_reduce(i1, first, X, ALU.min))
            then(one_hot(A1, i1))
            then(ve.scalar_tensor_tensor(el2, A1, 2 * NEG, el, ALU.mult, ALU.add))
            then(ve.tensor_reduce(m2, el2, X, ALU.max))
            ve.tensor_tensor(ed, m2, m1, ALU.subtract).then_inc(s_r1, 1)
            first_largest(el2, m2, first)
            then(ve.tensor_reduce(i2, first, X, ALU.min))
            then(one_hot(A2, i2))
            ve.tensor_tensor(Aa, A1, A2, ALU.add).then_inc(s_A, 1)
            for place_free in (s_eactT, s_combT, s_yA, s_yV, s_ctr, s_etr, s_comb):
                ve.nop().then_inc(place_free, 1)
            ve.wait_ge(s_rank, 1)
            then(ve.scalar_tensor_tensor(rank1, PS[7][:, 0:2 * NEXP].rearrange("p (t n) -> p t n", t=T), 1.0, Aa,
                                         ALU.add, ALU.mult))

            def slots(q):
                return ve.tensor_scalar(ranks[:, :, q * NEXP:(q + 1) * NEXP], rank1, -1.0 - SLOTS * q, None, ALU.add)

            def pick(p):
                for e in range(2):
                    for t in range(T):
                        last = ve.tensor_scalar(oneh[:, t, e * SLOTS:(e + 1) * SLOTS], iota[:, :],
                                                ranks[:, t, ds(2 * p + e, 1)], None, ALU.is_equal)
                last.then_inc(s_oneh, 1)

            def tokens(p):
                ve.wait_ge(s_disp, p + 1)
                ve.tensor_copy(xeT[:, 4:8, :], PS[5][:, :].rearrange("p (a b) -> p a b", a=4)).then_inc(s_xeV, 1)

            def pair(p, last_one=False):
                ve.wait_ge(s_disp, p + 1)
                pick(p + 1)
                ve.wait_ge(s_ctr, p + 1)
                for e in range(2):
                    for t in range(T):
                        last = ve.tensor_scalar(onehw[:, t, e * SLOTS:(e + 1) * SLOTS], iota[:, :],
                                                ranks[:, t, ds(2 * p + e, 1)], wsel[:, t, ds(2 * p + e, 1)],
                                                ALU.is_equal, ALU.mult)
                last.then_inc(s_onehw, 1)
                ve.wait_ge(s_eu, p + 1)
                ve.wait_ge(s_silu, p + 1)
                ve.tensor_tensor(eact, eact, PS[7][:, :], ALU.mult).then_inc(s_eact, 1)
                if not last_one:
                    tokens(p + 1)
                ve.wait_ge(s_ctr, p + 2)
                ve.wait_ge(s_comb, p + 1)
                ve.tensor_copy(combT, PS[7][:, 0:S].rearrange("p (t n) -> p t n", t=T)).then_inc(s_combT, 1)
                ve.wait_ge(s_edn, p + 1)
                ve.tensor_copy(ye[:, HALF:D], PS[5][:, :]).then_inc(s_yV, 1)

            then(slots(0))
            pick(0)
            for q in range(1, PASSES):
                last = slots(q)
            then(last)
            ve.wait_ge(s_rank, 2)
            then(ve.tensor_reduce(cmax, PS[6][:, 0:NEXP], X, ALU.max))
            ve.nop().then_inc(s_counts, 1)
            then(ve.tensor_scalar(over, cmax, float(SLOTS), float(PAIRS * (PASSES - 1)), ALU.is_gt, ALU.mult))
            ve.tensor_scalar(n_pairs_i[:, :], over, float(PAIRS), None, ALU.add).then_inc(s_np, 1)
            ve.wait_ge(s_r2, 2)
            ve.reciprocal(ggate, gsum)
            then(ve.tensor_scalar(p1, ed, 1.0, None, ALU.add))
            then(ve.reciprocal(p1, p1))
            then(ve.tensor_tensor(p1, p1, ggate, ALU.mult))
            then(ve.tensor_tensor(p2, p1, ed, ALU.mult))
            then(ve.tensor_tensor(Wt, A1, over_n(p1, NEXP), ALU.mult))
            then(ve.tensor_tensor(Wt2, A2, over_n(p2, NEXP), ALU.mult))
            then(ve.tensor_tensor(Wt, Wt, Wt2, ALU.add))
            for q in range(PASSES):
                last = ve.tensor_copy(wsel[:, :, q * NEXP:(q + 1) * NEXP], Wt)
            then(last)
            ve.wait_ge(s_np, 1)
            tokens(0)
            with ve.Fori(0, PAIRS - 1) as p:
                pair(p)
            pair(PAIRS - 1, last_one=True)
            n_pairs = ve.value_load(n_pairs_i[0:1, 0:1], min_val=PAIRS, max_val=PAIRS * PASSES)
            with ve.If(n_pairs > PAIRS):
                tokens(PAIRS)
                with ve.Fori(PAIRS, PAIRS * PASSES) as p:
                    pair(p)

            ve.wait_ge(s_rows, 48)
            def ask_tile_root(t):
                ve.wait_ge(s_sq[2], 2 * t + 2)
                at = column()
                ask_root(ve.scalar_tensor_tensor(ms[:, at:at + 1], sq[:, 2 * t:2 * t + 1], EPS,
                                                 sq[:, 2 * t + 1:2 * t + 2], ALU.add, ALU.add))

            for t in range(T):
                for c in range(2):
                    half = slice(c * HALF, (c + 1) * HALF)
                    ve.wait_ge(s_comb_last, 2 * t + c + 1)
                    then(ve.tensor_tensor(mix[:, t, half], PS[2 * t + c][:, :], post_ffn[:, half], ALU.mult))
                    ve.tensor_tensor(x[:, t, half], x[:, t, half], mix[:, t, half], ALU.add).then_inc(s_xsum, 1)
                    if t == 1 and c == 0:
                        ask_tile_root(0)
            for t in range(T):
                if t > 0:
                    ask_tile_root(t)
                ve.wait_ge(s_xsum, 2 * t + 2)
                ve.scalar_tensor_tensor(hn[:, t, :], x[:, t, :], root(), final_g[:, :], ALU.mult, ALU.mult)\
                    .then_inc(s_fin, 1)


_INS = ["x", "attn_pre_g", "w_in", "swa_sinks", "swa_out_g", "diff_lq1", "diff_lk1", "diff_lq2", "diff_lk2",
        "diff_subln_g", "w_out", "attn_post_g", "ffn_pre_g", "w_up", "conv_w", "conv_b", "w_down", "ffn_post_g",
        "c_2", "w_ada_2", "b_ada_2", "g_mix_2", "w_in_2", "g_dil_out_2", "g_sb_out_2", "w_out_2", "g_ffn_2",
        "w_group_2", "w_expert_2", "w_gate_2", "w_up_2", "w_down_2", "g_final_2"]


def kernel(**inputs):
    import concourse.bacc as bacc
    from concourse.bass_utils import run_bass_kernel_spmd

    nc = bacc.Bacc("TRN2", target_bir_lowering=False, num_devices=1)
    arrays, args = {}, {}
    for name in _INS:
        array = np.ascontiguousarray(inputs[name])
        arrays["in_" + name] = array
        args[name] = nc.dram_tensor("in_" + name, array.shape, mybir.dt.from_np(array.dtype),
                                    kind="ExternalInput").ap()
    out = nc.dram_tensor("out_0", inputs["x"].shape, mybir.dt.float32, kind="ExternalOutput").ap()
    two_block_kernel(nc, args, out)
    result = run_bass_kernel_spmd(nc, [arrays], core_ids=[0])
    return result.results[0]["out_0"]
```
